# Optimizing a Trainium2 kernel written in Bass

```python
import jax
import jax.numpy as jnp
from jax import lax
import numpy as np

D_MODEL = 1024
BATCH = 1
SEQ = 256
DEPTH = 2

HEAD_DIM = 64
BRANCH_W = 384
N_BRANCHES = 3
RWKV_HEADS = BRANCH_W // HEAD_DIM
RWKV_W = RWKV_HEADS * HEAD_DIM
DECAY_LORA = 64
AAA_LORA = 64
GATE_LORA = 160
RWKV_GN_EPS = 64e-5
SB_HEADS = BRANCH_W // HEAD_DIM
SB_W = SB_HEADS * HEAD_DIM
MLA_HEADS = 6
MLA_Q_LORA = 256
MLA_KV_LORA = 128
MLA_NOPE_DIM = 64
MLA_ROPE_DIM = 32
MLA_V_DIM = 64
MLA_W = MLA_HEADS * MLA_V_DIM
ROPE_THETA = 10000.0
MAX_POS_OFFSET = 1024
D_FF = 2816
MACARON_WEIGHT = 0.5
Q_BLOCK = 128
NORM_EPS = 1e-6
N_ADA = 9
RWKV_COLS = 3 * RWKV_W + DECAY_LORA + AAA_LORA + GATE_LORA
REST_SPLITS = (SB_W, SB_W, SB_W, MLA_Q_LORA, MLA_KV_LORA, MLA_ROPE_DIM, N_BRANCHES * D_MODEL)
D_IN = RWKV_COLS + 3 * SB_W + MLA_Q_LORA + MLA_KV_LORA + MLA_ROPE_DIM + N_BRANCHES * D_MODEL

kernel_name = 'hybrid_rwkv7_stickbreak_mla_macaron_adaln'

def _rms_norm(x, g):
    xf = x.astype(jnp.float32)
    y = xf * lax.rsqrt(jnp.mean(xf * xf, axis=-1, keepdims=True) + NORM_EPS)
    return (y * g.astype(jnp.float32)).astype(x.dtype)

def _modulated_norm(x, g, shift, scale):
    return _rms_norm(x, g) * (1.0 + scale[:, None, :]) + shift[:, None, :]

def _swiglu(h, w_in, w_out):
    gate, up = jnp.split(h @ w_in, 2, axis=-1)
    return (jax.nn.silu(gate) * up) @ w_out

def _split(p, sizes):
    out, off = [], 0
    for s in sizes:
        out.append(p[..., off:off + s])
        off += s
    return out

def _heads(t, n_heads):
    b, s, _ = t.shape
    return t.reshape(b, s, n_heads, -1)

def _token_shift(p, mu):
    prev = jnp.pad(p, ((0, 0), (1, 0), (0, 0)))[:, :-1]
    return p + (prev - p) * mu

def _wkv7_scan(r, w, k, v, a, b):
    bsz, _, n_heads, n = r.shape

    def step(state, inp):
        r_t, w_t, k_t, v_t, a_t, b_t = inp
        sa = jnp.einsum('bhvk,bhk->bhv', state, a_t)
        state = (state * w_t[:, :, None, :] + sa[..., None] * b_t[:, :, None, :]
                 + v_t[..., None] * k_t[:, :, None, :])
        return state, jnp.einsum('bhvk,bhk->bhv', state, r_t)

    xs = tuple(jnp.swapaxes(t, 0, 1) for t in (r, w, k, v, a, b))
    state0 = jnp.zeros((bsz, n_heads, n, n), jnp.float32)
    _, ys = lax.scan(step, state0, xs)
    return jnp.swapaxes(ys, 0, 1)

def _rwkv7_branch(r, k, v, dw, da, dg, w0, w2, a0, a2, g2, k_k, k_a, r_k, lnx_g, lnx_b):
    out_dtype = r.dtype
    f32 = jnp.float32
    r, k, v, dw, da, dg = (t.astype(f32) for t in (r, k, v, dw, da, dg))
    bsz, seq, _ = r.shape
    w_log = -jax.nn.softplus(-(w0 + jnp.tanh(dw) @ w2)) - 0.5
    decay = jnp.exp(-jnp.exp(w_log))
    a = jax.nn.sigmoid(a0 + da @ a2)
    g = jax.nn.sigmoid(dg) @ g2
    kk = _heads(k * k_k, RWKV_HEADS)
    kk = kk * lax.rsqrt(jnp.maximum(jnp.sum(kk * kk, axis=-1, keepdims=True), 1e-24))
    k = k * (1.0 + (a - 1.0) * k_a)
    rh, kh, vh, ah, wh = (_heads(t, RWKV_HEADS) for t in (r, k, v, a, decay))
    y = _wkv7_scan(rh, wh, kh, vh, -kk, kk * ah)
    mean = jnp.mean(y, axis=-1, keepdims=True)
    var = jnp.mean(jnp.square(y - mean), axis=-1, keepdims=True)
    y = ((y - mean) * lax.rsqrt(var + RWKV_GN_EPS)).reshape(bsz, seq, RWKV_W) * lnx_g + lnx_b
    bonus = jnp.sum(rh * kh * r_k, axis=-1, keepdims=True) * vh
    y = (y + bonus.reshape(bsz, seq, RWKV_W)) * g
    return y.astype(out_dtype)

def _stick_breaking_branch(q, k, v):
    bsz, seq, _ = q.shape
    q, k, v = (_heads(t, SB_HEADS) for t in (q, k, v))
    scale = HEAD_DIM ** -0.5
    outs = []
    for start in range(0, seq, Q_BLOCK):
        end = min(start + Q_BLOCK, seq)
        kp, vp = k[:, :end], v[:, :end]
        z = jnp.einsum('bqhd,bkhd->bhqk', q[:, start:end], kp).astype(jnp.float32) * scale
        t_idx = jnp.arange(start, end)
        s_idx = jnp.arange(end)
        mask = s_idx[None, :] < t_idx[:, None]
        log_1m = jnp.where(mask, jax.nn.log_sigmoid(-z), 0.0)
        rev = lax.cumsum(log_1m, axis=3, reverse=True)
        after = jnp.concatenate([rev[..., 1:], jnp.zeros_like(rev[..., :1])], axis=-1)
        weights = jnp.where(mask, jnp.exp(jax.nn.log_sigmoid(z) + after), 0.0)
        outs.append(jnp.einsum('bhqk,bkhd->bqhd', weights.astype(vp.dtype), vp))
    return jnp.concatenate(outs, axis=1).reshape(bsz, seq, SB_W)

def _rope_cos_sin(positions):
    inv_freq = 1.0 / (ROPE_THETA ** (jnp.arange(0, MLA_ROPE_DIM, 2, dtype=jnp.float32) / MLA_ROPE_DIM))
    ang = positions.astype(jnp.float32)[..., None] * inv_freq
    return jnp.cos(ang)[:, :, None, :], jnp.sin(ang)[:, :, None, :]

def _apply_rope(x, cos, sin):
    xf = x.astype(jnp.float32)
    half = MLA_ROPE_DIM // 2
    x1, x2 = xf[..., :half], xf[..., half:]
    return jnp.concatenate([x1 * cos - x2 * sin, x2 * cos + x1 * sin], axis=-1).astype(x.dtype)

def _mla_branch(cq, ckv, krope, positions, q_norm_g, w_uq, kv_norm_g, w_ukv):
    bsz, seq, _ = cq.shape
    q = (_rms_norm(cq, q_norm_g) @ w_uq).reshape(bsz, seq, MLA_HEADS, MLA_NOPE_DIM + MLA_ROPE_DIM)
    kv = (_rms_norm(ckv, kv_norm_g) @ w_ukv).reshape(bsz, seq, MLA_HEADS, MLA_NOPE_DIM + MLA_V_DIM)
    cos, sin = _rope_cos_sin(positions)
    q_nope = q[..., :MLA_NOPE_DIM]
    q_rope = _apply_rope(q[..., MLA_NOPE_DIM:], cos, sin)
    k_nope, v = kv[..., :MLA_NOPE_DIM], kv[..., MLA_NOPE_DIM:]
    k_rope = _apply_rope(krope[:, :, None, :], cos, sin)[:, :, 0]
    scale = (MLA_NOPE_DIM + MLA_ROPE_DIM) ** -0.5
    outs = []
    for start in range(0, seq, Q_BLOCK):
        end = min(start + Q_BLOCK, seq)
        s = (jnp.einsum('bqhd,bkhd->bhqk', q_nope[:, start:end], k_nope[:, :end])
             + jnp.einsum('bqhr,bkr->bhqk', q_rope[:, start:end], k_rope[:, :end])).astype(jnp.float32) * scale
        mask = jnp.arange(end)[None, :] <= jnp.arange(start, end)[:, None]
        probs = jax.nn.softmax(jnp.where(mask, s, -jnp.inf), axis=-1)
        outs.append(jnp.einsum('bhqk,bkhd->bqhd', probs.astype(v.dtype), v[:, :end]))
    return jnp.concatenate(outs, axis=1).reshape(bsz, seq, MLA_W)

def _token_mixer(h, positions, w_in, mu, w0, w2, a0, a2, g2, k_k, k_a, r_k, lnx_g, lnx_b,
                 q_norm_g, w_uq, kv_norm_g, w_ukv, branch_w, w_out):
    bsz, seq, _ = h.shape
    p = h @ w_in
    p_rwkv = _token_shift(p[..., :RWKV_COLS], mu)
    r, k, v, dw, da, dg = _split(p_rwkv, (RWKV_W, RWKV_W, RWKV_W, DECAY_LORA, AAA_LORA, GATE_LORA))
    sb_q, sb_k, sb_v, cq, ckv, krope, gate_logits = _split(p[..., RWKV_COLS:], REST_SPLITS)
    y_a = _rwkv7_branch(r, k, v, dw, da, dg, w0, w2, a0, a2, g2, k_k, k_a, r_k, lnx_g, lnx_b)
    y_b = _stick_breaking_branch(sb_q, sb_k, sb_v)
    y_c = _mla_branch(cq, ckv, krope, positions, q_norm_g, w_uq, kv_norm_g, w_ukv)
    ys = jnp.stack([y_a, y_b, y_c], axis=2)
    proj = jnp.einsum('bsnw,nwd->bsnd', ys, branch_w)
    gates = jax.nn.sigmoid(gate_logits.reshape(bsz, seq, N_BRANCHES, D_MODEL))
    merged = jnp.sum(gates * proj, axis=2)
    return merged @ w_out

def setup_inputs(seed: int = 0) -> dict:
    key = jax.random.key(seed)
    ks = jax.random.split(key, 32)
    f32 = jnp.float32

    def nrm(k, shape, fan_in, gain=1.0):
        return jax.random.normal(k, shape, f32) * (gain * fan_in ** -0.5)

    def noisy(k, shape, center, std):
        return center + std * jax.random.normal(k, shape, f32)

    x = jax.random.normal(ks[0], (BATCH, SEQ, D_MODEL), f32)
    c = jax.random.normal(ks[1], (BATCH, D_MODEL), f32)
    positions = (jnp.arange(SEQ, dtype=jnp.int32)[None, :]
                 + jax.random.randint(ks[2], (BATCH, 1), 0, MAX_POS_OFFSET, dtype=jnp.int32))
    return {
        'x': x,
        'c': c,
        'positions': positions,
        'ada_w': nrm(ks[3], (DEPTH, D_MODEL, N_ADA * D_MODEL), D_MODEL, 0.5),
        'ada_b': noisy(ks[4], (DEPTH, N_ADA * D_MODEL), 0.0, 0.01),
        'norm_g': noisy(ks[5], (DEPTH, 3, D_MODEL), 1.0, 0.05),
        'ffn1_w_in': nrm(ks[6], (DEPTH, D_MODEL, 2 * D_FF), D_MODEL),
        'ffn1_w_out': nrm(ks[7], (DEPTH, D_FF, D_MODEL), D_FF),
        'mix_w_in': nrm(ks[8], (DEPTH, D_MODEL, D_IN), D_MODEL),
        'rwkv_mu': jax.random.uniform(ks[9], (DEPTH, RWKV_COLS), f32),
        'rwkv_w0': jax.random.uniform(ks[10], (DEPTH, RWKV_W), f32, -6.0, 1.0),
        'rwkv_w2': nrm(ks[11], (DEPTH, DECAY_LORA, RWKV_W), DECAY_LORA),
        'rwkv_a0': noisy(ks[12], (DEPTH, RWKV_W), 0.0, 0.5),
        'rwkv_a2': nrm(ks[13], (DEPTH, AAA_LORA, RWKV_W), AAA_LORA),
        'rwkv_g2': nrm(ks[14], (DEPTH, GATE_LORA, RWKV_W), GATE_LORA),
        'rwkv_k_k': noisy(ks[15], (DEPTH, RWKV_W), 0.85, 0.05),
        'rwkv_k_a': noisy(ks[16], (DEPTH, RWKV_W), 1.0, 0.05),
        'rwkv_r_k': noisy(ks[17], (DEPTH, RWKV_HEADS, HEAD_DIM), 0.0, 0.1),
        'rwkv_lnx_g': noisy(ks[18], (DEPTH, RWKV_W), 1.0, 0.05),
        'rwkv_lnx_b': noisy(ks[19], (DEPTH, RWKV_W), 0.0, 0.01),
        'mla_q_norm_g': noisy(ks[20], (DEPTH, MLA_Q_LORA), 1.0, 0.05),
        'mla_w_uq': nrm(ks[21], (DEPTH, MLA_Q_LORA, MLA_HEADS * (MLA_NOPE_DIM + MLA_ROPE_DIM)), MLA_Q_LORA),
        'mla_kv_norm_g': noisy(ks[22], (DEPTH, MLA_KV_LORA), 1.0, 0.05),
        'mla_w_ukv': nrm(ks[23], (DEPTH, MLA_KV_LORA, MLA_HEADS * (MLA_NOPE_DIM + MLA_V_DIM)), MLA_KV_LORA),
        'branch_w': nrm(ks[24], (DEPTH, N_BRANCHES, BRANCH_W, D_MODEL), BRANCH_W),
        'mix_w_out': nrm(ks[25], (DEPTH, D_MODEL, D_MODEL), D_MODEL),
        'ffn2_w_in': nrm(ks[26], (DEPTH, D_MODEL, 2 * D_FF), D_MODEL),
        'ffn2_w_out': nrm(ks[27], (DEPTH, D_FF, D_MODEL), D_FF),
        'final_norm_g': noisy(ks[28], (D_MODEL,), 1.0, 0.05),
    }

def reference(x, c, positions, ada_w, ada_b, norm_g, ffn1_w_in, ffn1_w_out, mix_w_in,
              rwkv_mu, rwkv_w0, rwkv_w2, rwkv_a0, rwkv_a2, rwkv_g2, rwkv_k_k, rwkv_k_a,
              rwkv_r_k, rwkv_lnx_g, rwkv_lnx_b, mla_q_norm_g, mla_w_uq, mla_kv_norm_g,
              mla_w_ukv, branch_w, mix_w_out, ffn2_w_in, ffn2_w_out, final_norm_g):
    bsz = x.shape[0]
    c_act = jax.nn.silu(c)
    for l in range(DEPTH):
        mod = (c_act @ ada_w[l] + ada_b[l]).reshape(bsz, 3, 3, D_MODEL)
        h = _modulated_norm(x, norm_g[l, 0], mod[:, 0, 0], mod[:, 0, 1])
        x = x + MACARON_WEIGHT * mod[:, 0, 2][:, None, :] * _swiglu(h, ffn1_w_in[l], ffn1_w_out[l])
        h = _modulated_norm(x, norm_g[l, 1], mod[:, 1, 0], mod[:, 1, 1])
        mix = _token_mixer(h, positions, mix_w_in[l], rwkv_mu[l], rwkv_w0[l], rwkv_w2[l],
                           rwkv_a0[l], rwkv_a2[l], rwkv_g2[l], rwkv_k_k[l], rwkv_k_a[l],
                           rwkv_r_k[l], rwkv_lnx_g[l], rwkv_lnx_b[l], mla_q_norm_g[l],
                           mla_w_uq[l], mla_kv_norm_g[l], mla_w_ukv[l], branch_w[l], mix_w_out[l])
        x = x + mod[:, 1, 2][:, None, :] * mix
        h = _modulated_norm(x, norm_g[l, 2], mod[:, 2, 0], mod[:, 2, 1])
        x = x + MACARON_WEIGHT * mod[:, 2, 2][:, None, :] * _swiglu(h, ffn2_w_in[l], ffn2_w_out[l])
    return _rms_norm(x, final_norm_g)


_drawn_inputs = setup_inputs


def setup_inputs(seed=0):
    import zlib

    import numpy as np

    out = dict(_drawn_inputs(seed))
    spreads = {}
    factors = {'ada_b': 4.389,
     'rwkv_w2': 5.007,
     'rwkv_k_k': 7.68,
     'rwkv_k_a': 6.287,
     'rwkv_lnx_g': 8.0,
     'rwkv_lnx_b': 27.863,
     'mla_q_norm_g': 8.0,
     'mla_kv_norm_g': 8.0}
    for name, (base, spread) in spreads.items():
        noise = np.random.default_rng([zlib.crc32(name.encode()), seed]).standard_normal(out[name].shape)
        drawn = base * np.exp(spread * noise) if base else spread * noise
        out[name] = jnp.asarray(drawn.astype(out[name].dtype))
    for name, factor in factors.items():
        out[name] = (out[name] * factor).astype(out[name].dtype)
    return out
```

```python
from contextlib import ExitStack

import numpy as np

import concourse.bass as bass
from concourse import mybir

F32 = mybir.dt.float32
F32R = mybir.dt.float32r
I32 = mybir.dt.int32
ALU = mybir.AluOpType
ACT = mybir.ActivationFunctionType
AX_X = mybir.AxisListType.X

P = 128
DEPTH, D, T, F = 2, 1024, 256, 2816
KD, KF, TT = D // P, F // P, T // P
HEADS, HD, BW, NB = 6, 64, 384, 3
PAIRS = HEADS // 2
LORA_W, LORA_A, LORA_G = 64, 64, 160
Q_LORA, KV_LORA, ROPE, NOPE = 256, 128, 32, 64
RW_COLS = 3 * BW + LORA_W + LORA_A + LORA_G
SBQ, SBV = RW_COLS, RW_COLS + 2 * BW
CQ = RW_COLS + 3 * BW
CKV = CQ + Q_LORA
KR = CKV + KV_LORA
GATE0 = KR + ROPE
D_IN = GATE0 + NB * D
N_ADA = 9
CHUNK = 64
EPS, GN_EPS = 1e-6, 64e-5
SB_SCALE = HD ** -0.5
MLA_SCALE = (NOPE + ROPE) ** -0.5
NEG = -1e30

SLOT = 2048
FFN1_IN, FFN1_OUT = 0, 22
ATT_IN, RW_IN, GATE_IN = 33, 40, 46
BRANCH, MIX_OUT = 58, 63
FFN2_IN, FFN2_OUT = 67, 89
SLOTS = 100
IN_COLS = {
    33: (SBQ, SBQ + 128), 34: (SBQ + 256, SBQ + 384), 35: (SBQ + 512, SBQ + 640),
    37: (SBV + 256, CKV), 38: (CQ, CQ + 128),
    40: (0, 128), 41: (256, 384), 42: (512, 640), 43: (768, 896), 44: (1024, 1152),
    45: (1280, RW_COLS - 128),
}
SLOT_V, SLOT_KR = 36, 39


def slot_size(s):
    if s == SLOT_KR:
        return 2 * KD * 96
    return D if s == MIX_OUT - 1 else SLOT


def slot_dmas(s):
    s %= SLOTS
    if s == SLOT_KR:
        return 3
    if s == SLOT_V or FFN1_OUT <= s < ATT_IN or BRANCH <= s < FFN2_IN or s >= FFN2_OUT:
        return 1
    return 2


def dmas_before(s):
    return sum(slot_dmas(x) for x in range(s % 4, s + 1, 4))


V_ADA, V_NORM, V_MU, V_W0, V_A0, V_KK, V_KA, V_RK, V_LG, V_LB, V_QN, V_KVN = (
    0, 72, 96, 108, 111, 114, 117, 120, 123, 126, 129, 131)
N_VEC = 132

(C_ID, C_ONE, C_BLK, C_TRI, C_SBM, C_MIN, C_CAUS, C_LO1, C_UP, C_UPI, C_UP1, C_UP2, C_UP4, C_UP8,
 C_UP16, C_UP32, C_RST0, C_RST1, C_ROPE) = range(19)
LEVELS = (C_UP2, C_UP4, C_UP8, C_UP16, C_UP32)


def shape_constants():
    r, c = np.arange(P)[:, None], np.arange(P)[None, :]
    same = (r // CHUNK) == (c // CHUNK)
    out = [np.eye(P), np.ones((P, P)), same, r >= c, r < c, np.where(r < c, 0.0, NEG),
           np.where(c <= r, 0.0, NEG), (r // 2 == c // 2) & (r > c), same & (r < c), same & (r <= c)]
    for b in (1, 2, 4, 8, 16, 32):
        out.append((r // (2 * b) == c // (2 * b)) & (r % (2 * b) < b) & (c % (2 * b) >= b))
    reset = np.ones((P, T))
    reset[:, ::CHUNK] = 0.0
    out += [reset[:, :P], reset[:, P:]]
    rope = np.zeros((P, P))
    half = ROPE // 2
    freq = (1.0 / (np.float32(10000.0) ** (np.arange(0, ROPE, 2, dtype=np.float32) / np.float32(ROPE))))
    rope[NOPE:NOPE + half, 0] = freq
    rope[NOPE + half:NOPE + ROPE, 0] = freq
    rope[NOPE:NOPE + half, 1] = -1.0
    rope[NOPE + half:NOPE + ROPE, 1] = 1.0
    out.append(rope)
    return np.concatenate([x.astype(np.float32) for x in out], axis=1)


PER_LAYER = {
    "vec_ready": 1, "w_hi": 200, "sq_ready": 24, "rt_ready": 3, "hh_ready": 24, "sil_ready": 44,
    "att_in": 7, "sb_z": 3, "sb_ln": 3, "sb_w": 3, "sb_yh": 3, "mla_sq": 1, "mla_rt": 1,
    "mla_kv_ready": 2, "mla_qn": 3, "mla_sc": 2, "mla_exp": 2, "mla_p": 6, "mla_yh": 6, "pb_ready":
    6, "lora_in": 1, "wa_ready": 3, "g_ready": 1, "kk_sq": 1, "kk_rt": 1, "e_neg": 1, "e_cum": 1,
    "e_prev": 1, "tok_act": 4, "z_ready": 10, "wt_ready": 2, "ya_ready": 2, "gn_sq": 1, "gn_rt": 1,
    "ya_hi": 1, "gate_ready": 12, "mg_hi": 4, "ada_used": 36, "w_split": 200, "rinv_ready": 3,
    "t_ready": 24, "h_ready": 24, "hf_ready": 44, "x_ready": 24, "sb_sp": 3, "sb_lw": 3, "sb_yl": 3,
    "mla_rinv": 1, "mla_lat": 3, "mla_qr": 3, "mla_sub": 2, "mla_pr": 2, "mla_yl": 6, "shifted": 12,
    "cum_ready": 1, "kk_max": 1, "bon_in": 1, "kk_rinv": 1, "tilde": 1, "S_ready": 5, "tok_dve": 2,
    "at_ready": 2, "T_ready": 12, "ak_ready": 6, "G_ready": 2, "u0_ready": 2, "u_ready": 4,
    "gn_sub": 1, "gn_rinv": 1, "ya_final": 1, "ya_lo": 1, "mod_done": 1, "br_used": 12, "merged": 4,
    "mg_lo": 4, "hid_ready": 44, "sb_min": 3, "pb_zero": 1, "shift_d": 12, "kk0": 1, "X_ready": 10,
    "pcm_ready": 4, "vec_rows": 1, "acc_used": 18, "sq_used": 24, "rb_ready": 3, "w_used": 100,
    "out_done": 9, "sb_scored": 3, "sb_summed": 3, "sb_y": 3, "mla_sum": 1, "mla_rb": 1, "mla_k": 3,
    "mla_v": 1, "mla_q": 3, "mla_scored": 2, "mla_tr": 6, "mla_y": 6, "lora_done": 1, "kk_stat": 1,
    "bon_done": 1, "kk_rb": 1, "tok_done": 2, "ab_done": 4, "ak_done": 6, "z_done": 10, "tz_done":
    10, "g_done": 2, "wt_done": 2, "u0_done": 2, "u_done": 4, "s_done": 4, "y_done": 2, "gn_mean":
    1, "gn_stat": 1, "gn_rb": 1, "br_done": 10,
}
BEFORE = {"w_split": 6, "w_used": 1, "hf_ready": 3, "hid_ready": 1, "gate_ready": 3}
OUT_BANKS = ((4, 5, 6, 2), (0, 1, 2, 3), (4, 5, 6, 2))
BR_BANKS = (4, 0, 4)
NORM_BANK = (3, 3, 4)


def hybrid_trunk(nc, a, per_layer, tally):
    out_dram = a["out"]
    ctx = ExitStack()
    with ctx:
        ctx.enter_context(nc.allow_non_contiguous_dma(reason="vectors and column blocks"))

        def sb(name, shape, dt=F32):
            return ctx.enter_context(nc.sbuf_tensor(name, shape, dt))

        raw = sb("raw", [P, 4, SLOT])
        wh = sb("wh", [P, 2, SLOT], F32R)
        wl = sb("wl", [P, 2, SLOT], F32R)
        ada_w = sb("ada_w_ring", [P, 2, SLOT])
        acc = sb("ada_acc", [P, 512])
        x = sb("x", [P, KD, T])
        hh = sb("h_hi", [P, KD, T], F32R)
        hl = sb("h_lo", [P, KD, T], F32R)
        scr = sb("scr", [P, KD, T])
        cst = sb("cst", [P, 19 * P])
        vrows = sb("vrows", [P, 2, P])
        vec = sb("vec", [P, N_VEC])
        mod = sb("mod", [P, N_ADA * KD])
        gsc = sb("gsc", [P, 3, KD])
        hgate = sb("hgate", [P, 3, KD])
        omka = sb("omka", [P, 3])
        cact = sb("cact", [P, 2 * KD])
        rt = sb("rt", [P, 2])
        rinv = sb("rinv", [P, 2])
        hstat = sb("hstat", [P, 2, 12])
        epsb = sb("eps_col", [P, 1])
        gneps = sb("gn_eps_col", [P, 1])
        one_b = sb("one_col", [P, 1])
        lora = sb("lora", [P, BW])
        lora_g = sb("lora_g", [P, 2, BW])
        w_uq = sb("w_uq", [P, 2, HEADS * 96])
        w_sw = sb("w_sw", [P, 2, HEADS, ROPE])
        w_ukv = sb("w_ukv", [P, HEADS * P])
        cosT = sb("cosT", [P, T])
        sinT = sb("sinT", [P, T])

        def const(n):
            return cst[:, n * P:(n + 1) * P]

        ident, ones, blk = const(C_ID), const(C_ONE), const(C_BLK)
        onecol = cst[:, C_ONE * P:C_ONE * P + 1]
        blk2 = cst[:, C_BLK * P:C_BLK * P + P:CHUNK]
        reset = cst[:, C_RST0 * P:C_RST0 * P + T]

        base = nc.sbuf_base
        base = (base + 63) // 64 * 64
        room = nc.sbuf_usable_end - base
        cur = [0]
        names = {}

        def at_(name, cols, dt=F32, off=None):
            if off is not None:
                cur[0] = off
            o = cur[0]
            cur[0] += cols * 4
            assert cur[0] <= room, (name, cur[0], room)
            names[name] = o
            return nc.alloc_sbuf_tensor_at(name, [P, cols], dt, offset=base + o)

        def v3(t, n):
            return t[:, :].rearrange("p (a b) -> p a b", a=n)

        hidh = v3(at_("hid_hi", KF * T, F32R, 0), KF)
        hidl = v3(at_("hid_lo", KF * T, F32R), KF)
        sil = v3(at_("sil", 2 * T), 2)
        hf = v3(at_("hf", 2 * T), 2)
        yh = v3(at_("y_hi", 9 * T, F32R, 0), 9)
        yl = v3(at_("y_lo", 9 * T, F32R), 9)
        mix0 = cur[0]
        qk = v3(at_("sb_qk", 6 * T, off=mix0), 6)
        vs = v3(at_("sb_v", 2 * BW), 2)
        cqkv = v3(at_("cqkv", 3 * T), 3)
        qT = v3(at_("mla_qT", HEADS * T), HEADS)
        kT = v3(at_("mla_kT", HEADS * T), HEADS)
        vm = v3(at_("mla_v", 2 * BW), 2)
        krA = v3(at_("krope", 2 * T), 2)
        sbz = at_("sb_z", 2 * 768)[:, :].rearrange("p (r h n) -> p r h n", r=2, h=2)
        sbe = at_("sb_e", 2 * 768)[:, :].rearrange("p (r h n) -> p r h n", r=2, h=2)
        sbs = at_("sb_s", 2 * 768)[:, :].rearrange("p (r h n) -> p r h n", r=2, h=2)
        rA = at_("ropeA", 2 * T)
        rB = at_("ropeB", 2 * T)
        mls = at_("mla_s", 3 * 384, off=names["sb_z"])[:, :].rearrange("p (h n) -> p h n", h=3)
        mlp = at_("mla_p", 3 * 384)[:, :].rearrange("p (h n) -> p h n", h=3)
        mlx = at_("mla_x", 16)
        m = v3(at_("rw_m", 12 * T, off=mix0), 12)
        lw = v3(at_("rw_lw", 3 * T), 3)
        av = v3(at_("rw_a", 3 * T), 3)
        kk = v3(at_("rw_kk", 3 * T), 3)
        cum = v3(at_("rw_cum", 3 * T), 3)
        ex = v3(at_("rw_e", 3 * T), 3)
        g = v3(at_("rw_g", 3 * T), 3)
        bon = v3(at_("rw_bon", 3 * T), 3)
        rr, kp, vv = m[:, 0:3], m[:, 3:6], m[:, 6:9]
        ya = lw
        tokr = at_("rw_tok", 4 * BW)
        tok = v3(tokr, 4)
        scr_all = scr[:, :, :].rearrange("p a b -> p (a b)")
        u_, u0 = scr_all[:, 0:BW], scr_all[:, BW:2 * BW]
        S, wT, pcm = (scr_all[:, i * BW:(i + 1) * BW].rearrange("p (a b) -> p a b", a=3) for i in (2, 3, 4))
        amat = cur[0]

        def six(name, off=None):
            return at_(name, 6 * P, off=off)[:, :].rearrange("p (a c n) -> p a c n", a=2, c=3)

        AT, X, Tm, TTm, Z, Aak = (six(n) for n in ("A_T", "A_X", "A_inv", "A_invT", "A_Z", "A_ak"))
        Arb, Ark = six("A_rb"), six("A_rk")
        pb = at_("rw_pb", 12 * (T + 1), off=amat)[:, :].rearrange("p (a b) -> p a b", a=12)
        Gm = Z[:, :, :, :].rearrange("p a c n -> p (a c n)")[:, 0:BW]
        gates = v3(at_("gates", 24 * T, off=mix0), 24)
        mg = v3(at_("merged", KD * T), KD)
        mt = v3(at_("merge_t", 4 * T), 4)
        xin = v3(at_("x_rows", 2 * D, off=0), 2)
        xo = v3(at_("out_rows", 2 * D), 2)
        posi = at_("pos_i", T, I32)
        ang = at_("ang", 4 * T)[:, :].rearrange("p (a b) -> p a b", a=4)

        PS = ctx.enter_context(nc.psum_tensor("PS", [P, 8, 512], F32))

        def bank(b):
            return PS[:, b, :]

        sems = {}
        tally.clear()
        times = [1]

        def sem(name):
            if name not in sems:
                sems[name] = ctx.enter_context(nc.semaphore(name))
            return sems[name]

        def one(name, n=1):
            tally[name] = tally.get(name, 0) + n * times[0]
            return sem(name), n

        def once(name, n=1):
            return sem(name), n

        def at(name, k, l=0):
            return sem(name), l * per_layer.get(name, 0) + (k + BEFORE.get(name, 0))

        def still(n):
            return 0

        def steps(eng, first, count, peel=0, tail=0):
            for s in range(first, first + peel):
                yield s, still
            rounds = (count - peel - tail) // 4
            at0 = first + peel
            times[0] = rounds
            with eng.Fori(0, rounds) as i:
                for u in range(4):
                    yield at0 + u, lambda n: i * n
            times[0] = 1
            for s in range(at0 + 4 * rounds, first + count):
                yield s, still

        def ada_place(n, l):
            if n < 32:
                return l, n // 2
            return ((l + 1) % DEPTH, n // 2 - 16) if n < 40 else (l, n // 2 - 4)

        def loaded(s, o, l):
            q = s % 4
            per = sum(slot_dmas(v) for v in range(q, SLOTS, 4))
            per_round = slot_dmas(s)
            return sem(f"raw_loaded{q}"), l * (16 * per) + 16 * dmas_before(s) + o(16 * per_round)

        block = ctx.enter_context(nc.Block())

        @block.sync
        def _(sp):
            win = [a[n].rearrange("l (k p) n -> p (l k) n", p=P) for n in ("ffn1_w_in", "ffn2_w_in")]
            wout = [a[n].rearrange("l (k p) n -> p (l k) n", p=P) for n in ("ffn1_w_out", "ffn2_w_out")]
            wmix = a["mix_w_in"].rearrange("l (k p) n -> p (l k) n", p=P)
            wbr = a["branch_w"].rearrange("l n (k p) d -> p (l n k) d", p=P)
            wmo = a["mix_w_out"].rearrange("l (k p) n -> p (l k) n", p=P)
            wada = a["ada_w"].rearrange("l (k p) n -> p (l k) n", p=P)

            def free(s, o, l):
                sp.wait_ge(*at("w_split", 2 * (s - 4) + 2 + o(8), l))

            def halves(s, n=P):
                return raw[:, s % 4, 0:2 * KD * n].rearrange("p (g k n) -> p g k n", g=2, k=KD)

            def rows(s, k):
                return raw[:, s % 4, 0:k * D].rearrange("p (k n) -> p k n", k=k)

            def ada(n, o, r, l):
                if n >= 2:
                    sp.wait_ge(*at("ada_used", n - 1 + o(r), l))
                layer, group = ada_place(n, l)
                sp.dma_start(ada_w[:, n % 2, :].rearrange("p (k n) -> p k n", k=4),
                             wada[:, bass.ds(layer * KD + (n % 2) * 4, 4), bass.ds(o(256 * r) + group * 512, 512)])\
                    .then_inc(sem(f"ada_loaded{n % 2}"), 16)

            def ffn_loads(l, f):
                s0, s1 = (FFN1_IN, FFN1_OUT) if f == 0 else (FFN2_IN, FFN2_OUT)
                for s, o in steps(sp, s0, KF, *((0, 0), (4, 2))[f]):
                    j = s - s0
                    free(s, o, l)
                    for half in (1, 0):
                        c0 = half * F + j * P
                        cols = bass.ds(o(4 * P) + c0, P)
                        sp.dma_start(halves(s)[:, half], win[f][:, bass.ds(l * KD, KD), cols])\
                            .then_inc(sem(f"raw_loaded{s % 4}"), 16)
                    if f == 0 and j % 2:
                        ada(8 + j // 2, o, 2, l)
                    if f == 1 and j % 2 and 4 <= j < 20:
                        ada(32 + (j - 4) // 2, o, 2, l)
                for s, o in steps(sp, s1, 11, peel=1, tail=2):
                    j = s - s1
                    free(s, o, l)
                    sp.dma_start(rows(s, 2), wout[f][:, bass.ds(l * KF + 2 * j + o(8), 2), :])\
                        .then_inc(sem(f"raw_loaded{s % 4}"), 16)
                    if j and j % 2 == 0 and j <= (10, 8)[f]:
                        ada((19, 40)[f] + j // 2 - 1, o, 2, l)

            sp.dma_start(cst[:, :], a["consts"]).then_inc(sem("cst_loaded"), 16)
            sp.wait_ge(sem("zeroed"), 1)
            sp.dma_start(vrows[0:KD, 0, :], a["c"].rearrange("b (k p) -> (b k) p", p=P))\
                .then_inc(sem("c_loaded"), 16)
            sp.dma_start(vrows[KD:2 * KD, 0, :], a["final_norm_g"].rearrange("(k p) -> k p", p=P))\
                .then_inc(sem("c_loaded"), 16)
            sp.dma_start(posi[NOPE:NOPE + ROPE, :], a["positions"].broadcast_to([ROPE, T]))\
                .then_inc(sem("pos_loaded"), 16)
            ada(0, still, 0, 0)
            ada(1, still, 0, 0)
            sp.dma_start(xin[:, :, :], a["x"][0].rearrange("(t p) d -> p t d", p=P)).then_inc(sem("x_loaded"), 16)
            for n in range(2, 8):
                ada(n, still, 0, 0)
            with sp.Fori(0, DEPTH) as l:
                sp.wait_ge(sem("cT_ready"), 1)
                sp.wait_ge(*at("vec_rows", 0, l))
                ab = a["ada_b"].rearrange("l (k p) -> (l k) p", p=P)
                ng = a["norm_g"].rearrange("l i (k p) -> (l i k) p", p=P)
                todo = [(V_ADA, 0, ab, 72), (V_NORM, 0, ng, 24)]
                for c0, n, w in ((V_W0, "rwkv_w0", 3), (V_A0, "rwkv_a0", 3), (V_KK, "rwkv_k_k", 3),
                                 (V_KA, "rwkv_k_a", 3), (V_LG, "rwkv_lnx_g", 3), (V_LB, "rwkv_lnx_b", 3),
                                 (V_QN, "mla_q_norm_g", 2), (V_KVN, "mla_kv_norm_g", 1)):
                    todo.append((c0 % 126, c0 // 126, a[n].rearrange("l (k p) -> (l k) p", p=P), w))
                rk = a["rwkv_r_k"].rearrange("l (k h) d -> (l k) (h d)", h=2)
                todo.append((V_RK, 0, rk, 3))
                for r0, half, src, w in todo:
                    sp.dma_start(vrows[r0:r0 + w, half, :], src[bass.ds(l * w, w), :])\
                        .then_inc(sem("rows_loaded"), 16)
                mu = a["rwkv_mu"]
                sp.dma_start(vrows[V_MU:V_MU + 11, 0, :],
                             mu[bass.ds(l, 1), 0:11 * P].rearrange("l (k p) -> (l k) p", p=P))\
                    .then_inc(sem("rows_loaded"), 16)
                sp.dma_start(vrows[V_MU + 11:V_MU + 12, 0, :], mu[bass.ds(l, 1), RW_COLS - P:RW_COLS])\
                    .then_inc(sem("rows_loaded"), 16)
                ffn_loads(l, 0)
                sp.wait_ge(*at("lora_done", 0, l))
                sp.dma_start(lora[0:64, :], a["rwkv_w2"].rearrange("l p n -> p l n")[:, bass.ds(l, 1), :])\
                    .then_inc(sem("small_loaded"), 16)
                sp.dma_start(lora[64:128, :], a["rwkv_a2"].rearrange("l p n -> p l n")[:, bass.ds(l, 1), :])\
                    .then_inc(sem("small_loaded"), 16)
                g2 = a["rwkv_g2"].rearrange("l p n -> p l n")
                sp.dma_start(lora_g[:, 0, :], g2[0:P, bass.ds(l, 1), :]).then_inc(sem("small_loaded"), 16)
                sp.dma_start(lora_g[96:128, 1, :], g2[P:LORA_G, bass.ds(l, 1), :])\
                    .then_inc(sem("small_loaded"), 16)
                uq = a["mla_w_uq"].rearrange("l (k p) n -> p (l k) n", p=P)
                sp.dma_start(w_uq[:, :, :], uq[:, bass.ds(l * 2, 2), :]).then_inc(sem("small_loaded"), 16)
                uqh = a["mla_w_uq"].rearrange("l (k p) (h n) -> p (l k) h n", p=P, h=HEADS)
                for k in range(2):
                    for half in range(2):
                        src = NOPE + 16 * (1 - half)
                        sp.dma_start(w_sw[:, k, :, 16 * half:16 * half + 16],
                                     uqh[:, bass.ds(l * 2 + k, 1), :, src:src + 16].rearrange("p k h n -> p (k h) n"))\
                            .then_inc(sem("small_loaded"), 16)
                sp.dma_start(w_ukv[:, :], a["mla_w_ukv"].rearrange("l p n -> p l n")[:, bass.ds(l, 1), :])\
                    .then_inc(sem("small_loaded"), 16)
                for s in range(ATT_IN, GATE_IN):
                    free(s, still, l)
                    kd = bass.ds(l * KD, KD)
                    inc = sem(f"raw_loaded{s % 4}")
                    if s == SLOT_V:
                        sp.dma_start(raw[:, s % 4, :].rearrange("p (k n) -> p k n", k=KD),
                                     wmix[:, kd, SBV:SBV + 256]).then_inc(inc, 16)
                    elif s == SLOT_KR:
                        sp.dma_start(halves(s, 96)[:, 0], wmix[:, kd, KR - 64:KR + 32]).then_inc(inc, 16)
                        sp.dma_start(halves(s, 96)[:, 1, :, 0:80], wmix[:, kd, KR - 48:KR + 32]).then_inc(inc, 16)
                        sp.dma_start(halves(s, 96)[:, 1, :, 80:96], wmix[:, kd, KR:KR + 16]).then_inc(inc, 16)
                    else:
                        for half in (1, 0):
                            c0 = IN_COLS[s][half]
                            sp.dma_start(halves(s)[:, half], wmix[:, kd, c0:c0 + P]).then_inc(inc, 16)
                    if s - ATT_IN in (1, 3):
                        ada(24 + (s - ATT_IN) // 2, still, 0, l)
                for s, o in steps(sp, GATE_IN, 12, tail=4):
                    j = s - GATE_IN
                    free(s, o, l)
                    for half in range(2):
                        c0 = GATE0 + j * 256 + half * P
                        cols = bass.ds(o(4 * 256) + c0, P)
                        sp.dma_start(halves(s)[:, half], wmix[:, bass.ds(l * KD, KD), cols])\
                            .then_inc(sem(f"raw_loaded{s % 4}"), 16)
                    if j % 2:
                        ada(26 + j // 2, o, 2, l)
                for s in range(BRANCH, FFN2_IN):
                    free(s, still, l)
                    w, k0, per = (wbr, 2 * (s - BRANCH), 9) if s < MIX_OUT else (wmo, 2 * (s - MIX_OUT), KD)
                    n = slot_size(s) // D
                    sp.dma_start(rows(s, n), w[:, bass.ds(l * per + k0, n), :])\
                        .then_inc(sem(f"raw_loaded{s % 4}"), 16)
                ffn_loads(l, 1)
            for t in range(TT):
                sp.wait_ge(sem("out_ready"), t + 1)
                sp.dma_start(out_dram[0, t * P:(t + 1) * P, :], xo[:, t, :]).then_inc(sem("stored"), 16)
            sp.wait_ge(sem("stored"), 16 * TT)

        @block.scalar
        def _(act):
            def round_w(s, o, l):
                act.wait_ge(*loaded(s, o, l))
                act.wait_ge(*at("w_used", s - 1 + o(4), l))
                n = slot_size(s) // 2
                for h in range(2):
                    nc.scalar.activation(wh[:, s % 2, h * n:(h + 1) * n], raw[:, s % 4, h * n:(h + 1) * n],
                                         ACT.Copy).then_inc(*one("w_hi"))

            def norm(l, n, final=False):
                for c in range(KD):
                    act.wait_ge(*at("x_ready", n * KD + c + 1, l))
                    nc.scalar.activation(scr[:, c, :], x[:, c, :], ACT.Square)\
                        .then_inc(*(once if final else one)("sq_ready"))
                act.wait_ge(*at("sq_used", (n + 1) * KD, l))
                nc.scalar.activation(rt[:, :], PS[:, NORM_BANK[n], 0:2], ACT.Sqrt, scale=1.0 / D, bias=epsb[:, 0:1])\
                    .then_inc(*(once if final else one)("rt_ready"))
                if final:
                    return
                for c in range(KD):
                    act.wait_ge(*at("t_ready", n * KD + c + 1, l))
                    sh = [0, 3, 6][n] * KD + c
                    nc.scalar.activation(hh[:, c, :], scr[:, c, :], ACT.Identity,
                                         bias=mod[:, sh:sh + 1]).then_inc(*one("hh_ready"))

            def ffn(l, f):
                s0, s1 = (FFN1_IN, FFN1_OUT) if f == 0 else (FFN2_IN, FFN2_OUT)
                for s, o in steps(act, s0, KF):
                    j = s - s0
                    round_w(s + 2, o, l)
                    act.wait_ge(*at("w_used", s + 1 + o(4), l))
                    act.wait_ge(*at("hf_ready", f * KF + j - 1 + o(4), l))
                    nc.scalar.activation(sil[:, j % 2, :], PS[:, j % 4, 0:T], ACT.Silu)\
                        .then_inc(*one("sil_ready"))
                for s, o in steps(act, s1, 11, peel=1, tail=2):
                    if s + 2 < SLOTS:
                        round_w(s + 2, o, l)

            act.sem_inc(sem("gate_ready"), BEFORE["gate_ready"])
            act.wait_ge(sem("zeroed"), 1)
            act.wait_ge(sem("cT_ready"), 1)
            nc.scalar.activation(cact[:, 0:KD], bank(6)[:, 0:KD], ACT.Silu)
            nc.scalar.activation(cact[:, KD:2 * KD], bank(6)[:, KD:2 * KD], ACT.Copy)\
                .then_inc(sem("cact_ready"), 1)
            act.wait_ge(sem("ang_ready"), 1)
            r6 = slice(NOPE, NOPE + ROPE)
            nc.scalar.activation(ang[r6, 2, :], ang[r6, 0, :], ACT.Sin)
            nc.scalar.activation(ang[r6, 3, :], ang[r6, 0, :], ACT.Sin, scale=0.5).then_inc(sem("sin_ready"), 1)

            with act.Fori(0, DEPTH) as l:
                act.wait_ge(*at("vec_rows", 1, l))
                nc.scalar.activation(vec[:, 0:126], bank(0)[:, 0:126], ACT.Copy)
                nc.scalar.activation(vec[:, 126:N_VEC], bank(0)[:, P:P + 6], ACT.Copy)\
                    .then_inc(*one("vec_ready"))
                round_w(0, still, l)
                round_w(1, still, l)
                norm(l, 0)
                ffn(l, 0)
                norm(l, 1)
                for s in range(ATT_IN, RW_IN):
                    round_w(s + 2, still, l)
                    i = s - ATT_IN
                    act.wait_ge(*at("w_used", s + 1, l))
                    b = bank(i)
                    if i < 3:
                        ins = nc.scalar.activation(qk[:, 2 * i:2 * i + 2, :].rearrange("p a b -> p (a b)"), b,
                                                   ACT.Copy)
                    elif s == SLOT_V:
                        ins = nc.scalar.activation(vs[:, :, 0:256], b.rearrange("p (t n) -> p t n", t=2), ACT.Copy)
                    elif i == 4:
                        nc.scalar.activation(vs[:, :, 256:384], b[:, 0:256].rearrange("p (t n) -> p t n", t=2),
                                             ACT.Copy)
                        ins = nc.scalar.activation(cqkv[:, 2, :], b[:, 256:512], ACT.Copy)
                    elif i == 5:
                        ins = nc.scalar.activation(cqkv[:, 0:2, :].rearrange("p a b -> p (a b)"), b, ACT.Copy)
                    else:
                        ins = nc.scalar.activation(krA[NOPE:96, :, :].rearrange("p a b -> p (a b)"),
                                                   b[NOPE:96, :], ACT.Copy)
                    ins.then_inc(*one("att_in"))

                def sb_scores(c):
                    act.wait_ge(*at("sb_scored", c + 1, l))
                    ps = PS[:, 2 * (c % 2):2 * (c % 2) + 2, 0:384]
                    if c >= 2:
                        act.wait_ge(*at("sb_summed", c - 1, l))
                    nc.scalar.activation(sbz[:, c % 2], ps, ACT.Copy, scale=SB_SCALE).then_inc(*one("sb_z"))
                    act.drain()
                    nc.scalar.activation(sbe[:, c % 2], sbz[:, c % 2], ACT.Abs)
                    act.drain()
                    nc.scalar.activation(sbe[:, c % 2], sbe[:, c % 2], ACT.Exp, scale=-1.0)
                    act.drain()
                    nc.scalar.activation(sbe[:, c % 2], sbe[:, c % 2], ACT.Ln, bias=one_b[:, 0:1])\
                        .then_inc(*one("sb_ln"))

                def sb_weights(c):
                    act.wait_ge(*at("sb_lw", c + 1, l))
                    nc.scalar.activation(sbe[:, c % 2], sbz[:, c % 2], ACT.Exp).then_inc(*one("sb_w"))

                def sb_out(c):
                    act.wait_ge(*at("sb_y", c + 1, l))
                    nc.scalar.activation(yh[:, 3 + c, :], PS[:, 4 + c, 0:T], ACT.Copy)\
                        .then_inc(*one("sb_yh"))

                sb_scores(0)
                sb_scores(1)
                sb_weights(0)
                sb_out(0)
                sb_weights(1)
                sb_scores(2)
                sb_out(1)
                sb_weights(2)
                sb_out(2)
                nc.scalar.activation(scr[:, 0:3, :], cqkv[:, :, :], ACT.Square).then_inc(*one("mla_sq"))
                act.wait_ge(*at("mla_sum", 1, l))
                nc.scalar.activation(hstat[:, 0, 0:2], PS[:, 3, 0:2], ACT.Sqrt, scale=1.0 / Q_LORA, bias=epsb[:, 0:1])
                nc.scalar.activation(hstat[:, 0, 2:4], PS[:, 3, 2:4], ACT.Sqrt, scale=1.0 / KV_LORA,
                                     bias=epsb[:, 0:1]).then_inc(*one("mla_rt"))
                for i in range(PAIRS):
                    act.wait_ge(*at("mla_k", i + 1, l))
                    nc.scalar.activation(kT[0:NOPE, 2 * i:2 * i + 2, :].rearrange("p a b -> p (a b)"),
                                         PS[0:NOPE, i, :], ACT.Copy)
                act.wait_ge(*at("mla_v", 1, l))
                for t in range(TT):
                    nc.scalar.activation(vm[:, t, :], PS[:, 6 + t, 0:BW], ACT.Copy).then_inc(*one("mla_kv_ready"))
                for i in range(PAIRS):
                    act.wait_ge(*at("mla_q", i + 1, l))
                    nc.scalar.activation(qT[0:NOPE, 2 * i:2 * i + 2, :].rearrange("p a b -> p (a b)"),
                                         PS[0:NOPE, 3 + (i % 2), :], ACT.Copy).then_inc(*one("mla_qn"))
                for r in range(2):
                    act.wait_ge(*at("mla_scored", r + 1, l))
                    if r:
                        act.wait_ge(*at("mla_tr", 3, l))
                    nc.scalar.activation(mls[:, :, :], PS[:, 3 * r:3 * r + 3, 0:384], ACT.Copy, scale=MLA_SCALE)\
                        .then_inc(*one("mla_sc"))
                    act.wait_ge(*at("mla_sub", r + 1, l))
                    nc.scalar.activation(mls[:, :, :], mls[:, :, :], ACT.Exp).then_inc(*one("mla_exp"))
                    for i in range(3):
                        h = 3 * r + i
                        act.wait_ge(*at("mla_tr", h + 1, l))
                        if r:
                            act.wait_ge(*at("mla_y", i + 1, l))
                        nc.scalar.activation(mlp[:, i, :], PS[:, 6, 0:384], ACT.Copy).then_inc(*one("mla_p"))
                        act.wait_ge(*at("mla_y", h + 1, l))
                        o = NOPE * (h % 2)
                        nc.scalar.activation(yh[o:o + 64, 6 + h // 2, :], PS[o:o + 64, 7, 0:T], ACT.Copy)\
                            .then_inc(*one("mla_yh"))
                for i in range(6):
                    round_w(RW_IN + i + 2, still, l)
                    act.wait_ge(*at("w_used", RW_IN + i + 1, l))
                    if i == 0:
                        act.wait_ge(*at("pb_zero", 1, l))
                    nc.scalar.activation(pb[:, 2 * i:2 * i + 2, 1:T + 1],
                                         PS[:, i % 4, :].rearrange("p (a b) -> p a b", a=2), ACT.Copy)\
                        .then_inc(*one("pb_ready"))
                act.wait_ge(*at("shifted", 12, l))
                nc.scalar.activation(ex[0:64, 0, :], m[0:64, 9, :], ACT.Tanh)
                nc.scalar.activation(m[:, 10, :], m[:, 10, :], ACT.Sigmoid)
                nc.scalar.activation(m[96:128, 11, :], m[96:128, 11, :], ACT.Sigmoid).then_inc(*one("lora_in"))
                act.wait_ge(*at("lora_done", 1, l))
                for c in range(3):
                    nc.scalar.activation(lw[:, c, :], PS[:, 2 + c // 2, (c % 2) * T:(c % 2 + 1) * T], ACT.Sigmoid,
                                         bias=vec[:, V_W0 + c:V_W0 + c + 1])
                    nc.scalar.activation(av[:, c, :], PS[:, 4 + c // 2, (c % 2) * T:(c % 2 + 1) * T], ACT.Sigmoid,
                                         bias=vec[:, V_A0 + c:V_A0 + c + 1]).then_inc(*one("wa_ready"))
                nc.scalar.activation(g[:, 0:2, :].rearrange("p a b -> p (a b)"), PS[:, 6, :], ACT.Copy)
                nc.scalar.activation(g[:, 2, :], PS[:, 7, 0:T], ACT.Copy).then_inc(*one("g_ready"))
                act.wait_ge(*at("kk0", 1, l))
                nc.scalar.activation(ex[:, :, :], kk[:, :, :], ACT.Square).then_inc(*one("kk_sq"))
                act.wait_ge(*at("kk_max", 1, l))
                nc.scalar.activation(hstat[:, 0, :], hstat[:, 1, :], ACT.Sqrt).then_inc(*one("kk_rt"))
                act.wait_ge(*at("cum_ready", 1, l))
                act.wait_ge(*at("kk_stat", 1, l))
                nc.scalar.activation(ex[:, :, :], cum[:, :, :], ACT.Exp, scale=-1.0).then_inc(*one("e_neg"))
                act.drain()
                nc.scalar.activation(cum[:, :, :], cum[:, :, :], ACT.Exp).then_inc(*one("e_cum"))
                nc.scalar.activation(lw[:, :, :], lw[:, :, :], ACT.Exp).then_inc(*one("e_prev"))
                for tt in range(TT):
                    act.wait_ge(*at("tok_done", tt + 1, l))
                    for i in (0, 1):
                        nc.scalar.activation(tok[:, i, :], PS[:, i, 0:BW], ACT.Copy).then_inc(*one("tok_act"))
                    for b in range(5):
                        act.wait_ge(*at("z_done", tt * 5 + b + 1, l))
                        nc.scalar.activation(Z[:, :, :, :], PS[:, 0:2, 0:384].rearrange("p a (c n) -> p a c n", c=3),
                                             ACT.Copy).then_inc(*one("z_ready"))
                    act.wait_ge(*at("wt_done", tt + 1, l))
                    nc.scalar.activation(wT[:, :, :].rearrange("p a b -> p (a b)"), PS[:, 4, 0:BW], ACT.Copy)\
                        .then_inc(*one("wt_ready"))
                    act.wait_ge(*at("y_done", tt + 1, l))
                    nc.scalar.activation(ya[:, :, tt * P:(tt + 1) * P],
                                         PS[:, 6, 0:BW].rearrange("p (a b) -> p a b", a=3), ACT.Copy)\
                        .then_inc(*one("ya_ready"))
                act.wait_ge(*at("gn_sub", 1, l))
                nc.scalar.activation(ex[:, :, :], ya[:, :, :], ACT.Square).then_inc(*one("gn_sq"))
                act.wait_ge(*at("gn_stat", 1, l))
                nc.scalar.activation(hstat[:, 0, :], PS[:, 3, 0:12], ACT.Sqrt, scale=1.0 / HD, bias=gneps[:, 0:1])\
                    .then_inc(*one("gn_rt"))
                act.wait_ge(*at("ya_final", 1, l))
                nc.scalar.activation(yh[:, 0:3, :], ya[:, :, :], ACT.Copy).then_inc(*one("ya_hi"))
                for s, o in steps(act, GATE_IN, 12, tail=4):
                    j = s - GATE_IN
                    round_w(s + 2, o, l)
                    act.wait_ge(*at("w_used", s + 1 + o(4), l))
                    if j < 4:
                        act.wait_ge(*at("ya_lo", 1, l))
                    nc.scalar.activation(gates[:, bass.ds(o(8) + 2 * j, 2), :], PS[:, j % 4, :].rearrange("p (a b) -> p a b", a=2), ACT.Sigmoid)\
                        .then_inc(*one("gate_ready"))
                for s in range(BRANCH, FFN2_IN):
                    round_w(s + 2, still, l)
                    if s == MIX_OUT - 1:
                        for i in range(4):
                            act.wait_ge(*at("merged", i + 1, l))
                            nc.scalar.activation(hh[:, 2 * i:2 * i + 2, :], mg[:, 2 * i:2 * i + 2, :], ACT.Copy)\
                                .then_inc(*one("mg_hi"))
                norm(l, 2)
                ffn(l, 1)
            norm(DEPTH, 0, final=True)
            for t in range(TT):
                act.wait_ge(sem("out_tr"), t + 1)
                nc.scalar.activation(xo[:, t, :].rearrange("p (a b) -> p a b", a=2), PS[:, 2 * t + 4:2 * t + 6, :],
                                     ACT.Copy).then_inc(sem("out_ready"), 1)

        @block.vector
        def _(dve):
            V = nc.vector

            def split(s, o, l):
                n = slot_size(s) // 2
                for h in range(2):
                    dve.wait_ge(*at("w_hi", 2 * s + h + 1 + o(8), l))
                    V.tensor_tensor(wl[:, s % 2, h * n:(h + 1) * n], raw[:, s % 4, h * n:(h + 1) * n],
                                    wh[:, s % 2, h * n:(h + 1) * n].bitcast(F32), ALU.subtract)\
                        .then_inc(*one("w_split"))

            def norm(l, n):
                dve.wait_ge(*at("rt_ready", n + 1, l))
                V.reciprocal(rinv[:, :], rt[:, :]).then_inc(*one("rinv_ready"))
                dve.wait_ge(*at("rb_ready", n + 1, l))
                rb = PS[:, NORM_BANK[n], T:2 * T]

                def lo(c):
                    dve.wait_ge(*at("hh_ready", n * KD + c + 1, l))
                    sh = [0, 3, 6][n] * KD + c
                    V.scalar_tensor_tensor(hl[:, c, :], scr[:, c, :], mod[:, sh:sh + 1],
                                           hh[:, c, :].bitcast(F32), ALU.add, ALU.subtract)\
                        .then_inc(*one("h_ready"))

                for c in range(KD + 2):
                    if c < KD:
                        V.scalar_tensor_tensor(scr[:, c, :], x[:, c, :], gsc[:, n, c:c + 1], rb,
                                               ALU.mult, ALU.mult).then_inc(*one("t_ready"))
                    if c >= 2:
                        lo(c - 2)

            def evac_out(l, n, gate):
                for c in range(KD):
                    if c % 2 == 0:
                        dve.wait_ge(*(at("out_done", 3 * n + c // 2 + 1, l) if c < KD - 2 else
                                      at("w_used", (FFN1_OUT + 11, MIX_OUT + 4, FFN2_OUT + 11)[n], l)))
                    b = OUT_BANKS[n][c // 2]
                    V.scalar_tensor_tensor(x[:, c, :], PS[:, b, (c % 2) * T:(c % 2 + 1) * T], gate[:, c:c + 1],
                                           x[:, c, :], ALU.mult, ALU.add).then_inc(*one("x_ready"))

            def ffn(l, f):
                s0, s1 = (FFN1_IN, FFN1_OUT) if f == 0 else (FFN2_IN, FFN2_OUT)
                for s, o in steps(dve, s0, KF, *((0, 0), (4, 2))[f]):
                    j = s - s0
                    split(s + 2, o, l)
                    dve.wait_ge(*at("sil_ready", f * KF + j + 1 + o(4), l))
                    dve.wait_ge(*at("hid_ready", f * KF + j - 1 + o(4), l))
                    V.tensor_tensor(hf[:, j % 2, :], PS[:, j % 4, T:2 * T], sil[:, j % 2, :], ALU.mult)\
                        .then_inc(*one("hf_ready"))
                    if f == 0 and j % 2 == 0:
                        ada(8 + j // 2, o, 2, l)
                    if f == 1 and j % 2 == 0 and 4 <= j < 20:
                        ada(32 + (j - 4) // 2, o, 2, l)
                for s, o in steps(dve, s1, 11, peel=1, tail=2):
                    j = s - s1
                    if s + 2 < SLOTS:
                        split(s + 2, o, l)
                    if j % 2 and j <= (9, 7)[f]:
                        ada((19, 40)[f] + j // 2, o, 2, l)

            def ada(n, o, r, l, inc=one):
                q = n % 2
                dve.drain()
                dve.wait_ge(sem(f"ada_loaded{q}"), l * (18 * 16) + 16 * (n // 2 + 1) + o(8 * r))
                w4 = ada_w[:, q, :].rearrange("p (k n) -> p k n", k=4)
                if q == 0 and n:
                    dve.wait_ge(*at("acc_used", n // 2 + o(r // 2), l))
                for k in range(4):
                    cc = cact[:, 4 * q + k:4 * q + k + 1]
                    if q == 0 and k == 0:
                        V.tensor_scalar(acc[:, :], w4[:, 0, :], cc, None, ALU.mult)
                    else:
                        if k:
                            dve.drain()
                        last = V.scalar_tensor_tensor(acc[:, :], w4[:, k, :], cc, acc[:, :], ALU.mult, ALU.add)
                last.then_inc(*inc("ada_used"))

            def mod_part(l, lo, hi, groups):
                dve.wait_ge(*at("acc_used", groups, l))
                V.tensor_tensor(mod[:, lo:hi], PS[:, 7, lo:hi], vec[:, V_ADA + lo:V_ADA + hi], ALU.add)
                dve.drain()

            def scales(n):
                sc = mod[:, (3 * n + 1) * KD:(3 * n + 2) * KD]
                return V.scalar_tensor_tensor(gsc[:, n, :], sc, 1.0, vec[:, V_NORM + n * KD:V_NORM + (n + 1) * KD],
                                       ALU.add, ALU.mult)

            def half_gate(n, w):
                return V.tensor_scalar(hgate[:, n, :], mod[:, (3 * n + 2) * KD:(3 * n + 3) * KD], w, None, ALU.mult)

            for name in ("w_split", "hf_ready"):
                dve.sem_inc(sem(name), BEFORE[name])
            V.memset(epsb[:, :], EPS)
            V.memset(gneps[:, :], GN_EPS)
            V.memset(one_b[:, :], 1.0)
            V.memset(vrows[:, :, :], 0.0).then_inc(sem("zeroed"), 1)
            dve.wait_ge(sem("cact_ready"), 1)
            ada(0, still, 0, 0, once)
            ada(1, still, 0, 0, once)
            for i in range(4):
                dve.wait_ge(sem("x_tr"), i + 1)
                for t in range(2):
                    for c in (2 * i, 2 * i + 1):
                        ins = V.tensor_copy(x[:, c, t * P:(t + 1) * P],
                                            PS[:, i, ((c % 2) * 2 + t) * P:((c % 2) * 2 + t + 1) * P])
            ins.then_inc(sem("x_ready"), KD)
            for n in range(2, 6):
                ada(n, still, 0, 0, once)
            r6 = slice(NOPE, NOPE + ROPE)
            rc = C_ROPE * P
            dve.wait_ge(sem("pos_loaded"), 16)
            dve.wait_ge(sem("cst_loaded"), 16)
            V.tensor_copy(ang[r6, 1, :], posi[r6, :])
            dve.drain()
            V.tensor_scalar(ang[r6, 0, :], ang[r6, 1, :], cst[r6, rc:rc + 1], None, ALU.mult)
            dve.drain()
            magic = 1.5 * 2.0 ** 23
            V.tensor_scalar(ang[r6, 1, :], ang[r6, 0, :], 1.0 / (2 * np.pi), magic, ALU.mult, ALU.add)
            dve.drain()
            V.tensor_scalar(ang[r6, 1, :], ang[r6, 1, :], magic, None, ALU.subtract)
            c1 = 6.28125
            c2 = 0.0019350051879882812
            c3 = 2 * np.pi - c1 - c2
            for cc in (c1, c2, c3):
                dve.drain()
                V.scalar_tensor_tensor(ang[r6, 0, :], ang[r6, 1, :], -cc, ang[r6, 0, :], ALU.mult, ALU.add)
            dve.drain()
            V.tensor_scalar(ang[r6, 0, :], ang[r6, 0, :], 3.1415925, -3.1415925, ALU.min, ALU.max)\
                .then_inc(sem("ang_ready"), 1)
            dve.wait_ge(sem("sin_ready"), 1)
            V.tensor_scalar(sinT[r6, :], ang[r6, 2, :], cst[r6, rc + 1:rc + 2], None, ALU.mult)
            V.tensor_tensor(ang[r6, 1, :], ang[r6, 3, :], ang[r6, 3, :], ALU.mult)
            dve.drain()
            V.tensor_scalar(cosT[r6, :], ang[r6, 1, :], -2.0, 1.0, ALU.mult, ALU.add)
            for n in range(6, 8):
                ada(n, still, 0, 0, once)

            with dve.Fori(0, DEPTH) as l:
                dve.wait_ge(*at("vec_ready", 1, l))
                mod_part(l, 0, 16, 4)
                scales(0)
                V.tensor_scalar(omka[:, :], vec[:, V_KA:V_KA + 3], -1.0, 1.0, ALU.mult, ALU.add)
                split(0, still, l)
                split(1, still, l)
                norm(l, 0)
                ffn(l, 0)
                mod_part(l, 16, 48, 12)
                scales(1)
                half_gate(0, 0.5)
                half_gate(1, 1.0)
                dve.drain()
                evac_out(l, 0, hgate[:, 0, :])
                norm(l, 1)
                for s in range(ATT_IN, RW_IN):
                    split(s + 2, still, l)
                    if s - ATT_IN in (0, 2):
                        ada(24 + (s - ATT_IN) // 2, still, 0, l)
                mod_part(l, 48, 52, 13)
                mask2 = const(C_SBM).unsqueeze(1).unsqueeze(1).broadcast_to([P, 2, 2, P])

                def diag(t):
                    return t.rearrange("p h (b n) -> p h b n", b=3)[:, :, 0:3:2, :]

                def sb_soft(c):
                    dve.wait_ge(*at("sb_z", c + 1, l))
                    if c >= 2:
                        dve.wait_ge(*at("sb_summed", c - 1, l))
                    V.tensor_scalar(sbs[:, c % 2], sbz[:, c % 2], 0.0, None, ALU.max)
                    dve.drain()
                    dve.wait_ge(*at("sb_ln", c + 1, l))
                    V.tensor_tensor(sbs[:, c % 2], sbs[:, c % 2], sbe[:, c % 2], ALU.add)
                    dve.drain()
                    V.tensor_tensor(diag(sbs[:, c % 2]), diag(sbs[:, c % 2]), mask2, ALU.mult)\
                        .then_inc(*one("sb_sp"))

                def sb_lw(c):
                    dve.wait_ge(*at("sb_summed", c + 1, l))
                    dve.wait_ge(*at("sb_min", c + 1, l))
                    V.tensor_tensor(sbz[:, c % 2], sbz[:, c % 2], PS[:, 2 * (c % 2):2 * (c % 2) + 2, 0:384],
                                    ALU.subtract).then_inc(*one("sb_lw"))

                def sb_lo(c):
                    dve.wait_ge(*at("sb_yh", c + 1, l))
                    V.tensor_tensor(yl[:, 3 + c, :], PS[:, 4 + c, 0:T], yh[:, 3 + c, :].bitcast(F32), ALU.subtract)\
                        .then_inc(*one("sb_yl"))

                sb_soft(0)
                sb_soft(1)
                sb_lw(0)
                sb_lw(1)
                sb_lo(0)
                sb_soft(2)
                sb_lo(1)
                sb_lw(2)
                sb_lo(2)
                dve.wait_ge(*at("mla_rt", 1, l))
                V.reciprocal(hstat[:, 1, 0:4], hstat[:, 0, 0:4]).then_inc(*one("mla_rinv"))
                dve.wait_ge(*at("mla_rb", 1, l))
                for c in range(3):
                    rb = PS[:, 4 if c < 2 else 5, 0:T]
                    gcol = V_QN + c if c < 2 else V_KVN
                    V.scalar_tensor_tensor(cqkv[:, c, :], cqkv[:, c, :], vec[:, gcol:gcol + 1], rb,
                                           ALU.mult, ALU.mult).then_inc(*one("mla_lat"))
                R = slice(NOPE, 96)
                V.tensor_tensor(rA[R, 0:T], krA[R, 0, :], cosT[R, :], ALU.mult)
                V.tensor_tensor(rB[R, 0:T], krA[R, 1, :], sinT[R, :], ALU.mult)
                dve.drain()
                V.tensor_tensor(kT[R, :, :], rA[R, 0:T].unsqueeze(1).broadcast_to([32, HEADS, T]),
                                rB[R, 0:T].unsqueeze(1).broadcast_to([32, HEADS, T]), ALU.add)
                cos2 = cosT[R, :].unsqueeze(1).broadcast_to([32, 2, T])
                sin2 = sinT[R, :].unsqueeze(1).broadcast_to([32, 2, T])
                for i in range(PAIRS):
                    dve.drain()
                    dve.wait_ge(*at("mla_q", i + 1, l))
                    V.tensor_tensor(rA[R, :].rearrange("p (a b) -> p a b", a=2),
                                    PS[R, 3 + (i % 2), :].rearrange("p (a b) -> p a b", a=2), cos2, ALU.mult)
                    V.tensor_tensor(rB[R, :].rearrange("p (a b) -> p a b", a=2),
                                    PS[R, 5, :].rearrange("p (a b) -> p a b", a=2),
                                    sin2, ALU.mult)
                    dve.drain()
                    V.tensor_tensor(qT[R, 2 * i:2 * i + 2, :].rearrange("p a b -> p (a b)"), rA[R, :], rB[R, :],
                                    ALU.add).then_inc(*one("mla_qr"))
                caus6 = const(C_CAUS).unsqueeze(1).unsqueeze(1).broadcast_to([P, 3, 2, P])
                for r in range(2):
                    dve.wait_ge(*at("mla_sc", r + 1, l))
                    V.tensor_tensor(diag(mls), diag(mls), caus6, ALU.add)
                    dve.drain()
                    V.tensor_reduce(mlx[:, 0:3], mls[:, :, 0:P], AX_X, ALU.max)
                    V.tensor_reduce(mlx[:, 3:6], mls[:, :, P:384], AX_X, ALU.max)
                    dve.drain()
                    for k, (lo_, n_) in enumerate(((0, P), (P, 256))):
                        last = V.tensor_tensor(mls[:, :, lo_:lo_ + n_], mls[:, :, lo_:lo_ + n_],
                                               mlx[:, 3 * k:3 * k + 3].unsqueeze(2).broadcast_to([P, 3, n_]), ALU.subtract)
                    last.then_inc(*one("mla_sub"))
                    dve.wait_ge(*at("mla_exp", r + 1, l))
                    V.tensor_reduce(mlx[:, 6:9], mls[:, :, 0:P], AX_X, ALU.add)
                    V.tensor_reduce(mlx[:, 9:12], mls[:, :, P:384], AX_X, ALU.add)
                    dve.drain()
                    V.reciprocal(mlx[:, 0:6], mlx[:, 6:12])
                    dve.drain()
                    for k, (lo_, n_) in enumerate(((0, P), (P, 256))):
                        last = V.tensor_tensor(mls[:, :, lo_:lo_ + n_], mls[:, :, lo_:lo_ + n_],
                                               mlx[:, 3 * k:3 * k + 3].unsqueeze(2).broadcast_to([P, 3, n_]), ALU.mult)
                    last.then_inc(*one("mla_pr"))
                    for i in range(3):
                        h = 3 * r + i
                        o = NOPE * (h % 2)
                        dve.wait_ge(*at("mla_yh", h + 1, l))
                        V.tensor_tensor(yl[o:o + 64, 6 + h // 2, :], PS[o:o + 64, 7, 0:T],
                                        yh[o:o + 64, 6 + h // 2, :].bitcast(F32), ALU.subtract)\
                            .then_inc(*one("mla_yl"))
                for i in range(6):
                    split(RW_IN + i + 2, still, l)
                    for c in (2 * i, 2 * i + 1):
                        dve.wait_ge(*at("shift_d", c + 1, l))
                        V.scalar_tensor_tensor(m[:, c, :], m[:, c, :], vec[:, V_MU + c:V_MU + c + 1],
                                               pb[:, c, 1:T + 1], ALU.mult, ALU.add).then_inc(*one("shifted"))
                dve.wait_ge(*at("wa_ready", 3, l))
                V.tensor_scalar(lw[:, :, :], lw[:, :, :], -float(np.exp(-0.5)), None, ALU.mult)
                dve.drain()
                for c in range(3):
                    V.tensor_tensor_scan(cum[:, c, :], reset, lw[:, c, :], 0.0, ALU.mult, ALU.add)
                dve.drain()
                V.tensor_tensor(lw[:, :, :], cum[:, :, :], lw[:, :, :], ALU.subtract).then_inc(*one("cum_ready"))
                dve.wait_ge(*at("kk_stat", 1, l))
                V.tensor_scalar(hstat[:, 1, :], PS[:, 3, 0:12], 1e-24, None, ALU.max).then_inc(*one("kk_max"))
                for c in range(3):
                    V.tensor_scalar(bon[:, c, :], av[:, c, :], vec[:, V_KA + c:V_KA + c + 1], omka[:, c:c + 1],
                                    ALU.mult, ALU.add)
                dve.drain()
                V.tensor_tensor(kp, kp, bon[:, :, :], ALU.mult)
                dve.drain()
                for c in range(3):
                    last = V.scalar_tensor_tensor(bon[:, c, :], rr[:, c, :], vec[:, V_RK + c:V_RK + c + 1], kp[:, c, :],
                                                  ALU.mult, ALU.mult)
                last.then_inc(*one("bon_in"))
                dve.wait_ge(*at("kk_rt", 1, l))
                V.reciprocal(hstat[:, 1, :], hstat[:, 0, :]).then_inc(*one("kk_rinv"))
                dve.wait_ge(*at("kk_rb", 1, l))
                V.tensor_tensor(kk[:, 0:2, :], kk[:, 0:2, :], PS[:, 4, :].rearrange("p (a b) -> p a b", a=2), ALU.mult)
                V.tensor_tensor(kk[:, 2, :], kk[:, 2, :], PS[:, 5, 0:T], ALU.mult)
                dve.drain()
                V.tensor_tensor(av[:, :, :], kk[:, :, :], av[:, :, :], ALU.mult)
                dve.wait_ge(*at("bon_done", 1, l))
                V.tensor_tensor(bon[:, 0:2, :], PS[:, 6, :].rearrange("p (a b) -> p a b", a=2), vv[:, 0:2, :], ALU.mult)
                V.tensor_tensor(bon[:, 2, :], PS[:, 7, 0:T], vv[:, 2, :], ALU.mult)
                dve.drain()
                dve.wait_ge(*at("e_neg", 1, l))
                V.tensor_tensor(av[:, :, :], av[:, :, :], ex[:, :, :], ALU.mult)
                V.tensor_tensor(kp, kp, ex[:, :, :], ALU.mult)
                dve.wait_ge(*at("e_cum", 1, l))
                V.tensor_tensor(rr, rr, cum[:, :, :], ALU.mult)
                dve.wait_ge(*at("e_prev", 1, l))
                V.scalar_tensor_tensor(kk[:, :, :], kk[:, :, :], -1.0, lw[:, :, :], ALU.mult, ALU.mult)\
                    .then_inc(*one("tilde"))
                V.memset(S[:, :, :], 0.0).then_inc(*one("S_ready"))

                def six_mask(n):
                    return const(n).unsqueeze(1).unsqueeze(1).broadcast_to([P, 2, 3, P])

                def two(b):
                    return PS[:, b:b + 2, 0:384].rearrange("p a (c n) -> p a c n", c=3)

                for tt in range(TT):
                    dve.wait_ge(*at("tok_done", tt + 1, l))
                    for i in (2, 3):
                        last = V.tensor_copy(tok[:, i, :], PS[:, i, 0:BW])
                    last.then_inc(*one("tok_dve"))
                    dve.wait_ge(*at("ab_done", 2 * tt + 1, l))
                    V.tensor_tensor(AT[:, :, :, :], two(4), six_mask(C_UP), ALU.mult).then_inc(*one("at_ready"))
                    dve.wait_ge(*at("ab_done", 2 * tt + 2, l))
                    V.tensor_tensor(Tm[:, :, :, :], two(6), six_mask(C_LO1), ALU.mult)
                    dve.drain()
                    V.tensor_tensor(Tm[:, :, :, :], Tm[:, :, :, :], six_mask(C_ID), ALU.add)
                    V.tensor_tensor(TTm[:, :, :, :], AT[:, :, :, :], six_mask(C_UP1), ALU.mult)
                    dve.drain()
                    V.tensor_tensor(TTm[:, :, :, :], TTm[:, :, :, :], six_mask(C_ID), ALU.add).then_inc(*one("T_ready"))
                    for i, (dst, msk) in enumerate(((Aak, C_UP), (Arb, C_UPI), (Ark, C_UPI))):
                        dve.wait_ge(*at("ak_done", 3 * tt + i + 1, l))
                        V.tensor_tensor(dst[:, :, :, :], two((4, 6, 4)[i]), six_mask(msk), ALU.mult)\
                            .then_inc(*one("ak_ready"))
                    for b in range(5):
                        dve.wait_ge(*at("tz_done", 5 * tt + b + 1, l))
                        if b < 4:
                            V.tensor_tensor(Tm[:, :, :, :], Tm[:, :, :, :], two(2), ALU.add)
                        V.tensor_tensor(TTm[:, :, :, :], TTm[:, :, :, :], two(4), ALU.add).then_inc(*one("T_ready"))
                    dve.wait_ge(*at("g_done", tt + 1, l))
                    V.tensor_copy(Gm, PS[:, 0, 0:BW]).then_inc(*one("G_ready"))
                    dve.wait_ge(*at("u0_done", tt + 1, l))
                    V.tensor_copy(u0[:, :], PS[:, 1, 0:BW]).then_inc(*one("u0_ready"))
                    for q in (2 * tt, 2 * tt + 1):
                        rows = slice((q % 2) * 64, (q % 2) * 64 + 64)
                        dve.drain()
                        dve.wait_ge(*at("u_done", q + 1, l))
                        V.tensor_tensor(u_[rows, :], PS[rows, 5, 0:BW], u0[rows, :], ALU.add).then_inc(*one("u_ready"))
                        dve.wait_ge(*at("s_done", q + 1, l))
                        V.tensor_tensor(S[:, :, :].rearrange("p a b -> p (a b)"),
                                        S[:, :, :].rearrange("p a b -> p (a b)"), PS[:, 3, 0:BW], ALU.add)
                        dve.drain()
                        dve.wait_ge(*at("pcm_ready", q + 1, l))
                        V.tensor_tensor(S[:, :, :], S[:, :, :], pcm[:, :, :], ALU.mult).then_inc(*one("S_ready"))
                dve.wait_ge(*at("gn_mean", 1, l))
                V.scalar_tensor_tensor(ya[:, 0:2, :], PS[:, 0, :].rearrange("p (a b) -> p a b", a=2), -1.0 / HD,
                                       ya[:, 0:2, :], ALU.mult, ALU.add)
                V.scalar_tensor_tensor(ya[:, 2, :], PS[:, 1, 0:T], -1.0 / HD, ya[:, 2, :], ALU.mult, ALU.add)\
                    .then_inc(*one("gn_sub"))
                dve.wait_ge(*at("gn_rt", 1, l))
                V.reciprocal(hstat[:, 1, :], hstat[:, 0, :]).then_inc(*one("gn_rinv"))
                dve.wait_ge(*at("gn_rb", 1, l))
                for c in range(3):
                    V.scalar_tensor_tensor(ya[:, c, :], ya[:, c, :], vec[:, V_LG + c:V_LG + c + 1],
                                           PS[:, 4 + c // 2, (c % 2) * T:(c % 2 + 1) * T], ALU.mult, ALU.mult)
                dve.drain()
                for c in range(3):
                    V.scalar_tensor_tensor(ya[:, c, :], ya[:, c, :], vec[:, V_LB + c:V_LB + c + 1], bon[:, c, :],
                                           ALU.add, ALU.add)
                dve.drain()
                V.tensor_tensor(ya[:, :, :], ya[:, :, :], g[:, :, :], ALU.mult).then_inc(*one("ya_final"))
                dve.wait_ge(*at("ya_hi", 1, l))
                V.tensor_tensor(yl[:, 0:3, :], ya[:, :, :], yh[:, 0:3, :].bitcast(F32), ALU.subtract)\
                    .then_inc(*one("ya_lo"))
                for s, o in steps(dve, GATE_IN, 12, tail=4):
                    j = s - GATE_IN
                    split(s + 2, o, l)
                    if j % 2 == 0:
                        ada(26 + j // 2, o, 2, l)
                mod_part(l, 52, 64, 16)
                scales(2).then_inc(*one("mod_done"))
                dve.wait_ge(*at("gate_ready", 12, l))
                for s in range(BRANCH + 2, MIX_OUT):
                    split(s, still, l)
                for n in range(NB):
                    for i in range(4):
                        dve.wait_ge(*(at("br_done", (0, 4, 7)[n] + i + 1, l) if n == 0 or i < 3 else
                                      at("w_used", BRANCH + (3, 5)[n - 1], l)))
                        ps = PS[:, BR_BANKS[n] + i, :].rearrange("p (a b) -> p a b", a=2)
                        gt = gates[:, n * KD + 2 * i:n * KD + 2 * i + 2, :]
                        if n == 0:
                            V.tensor_tensor(mg[:, 2 * i:2 * i + 2, :], ps, gt, ALU.mult).then_inc(*one("br_used"))
                        else:
                            t = mt[:, 2 * (i % 2):2 * (i % 2) + 2, :]
                            V.tensor_tensor(t, ps, gt, ALU.mult).then_inc(*one("br_used"))
                            dve.drain()
                            ins = V.tensor_tensor(mg[:, 2 * i:2 * i + 2, :], mg[:, 2 * i:2 * i + 2, :], t, ALU.add)
                            if n == 2:
                                ins.then_inc(*one("merged"))
                    if n < 2:
                        split(MIX_OUT + n, still, l)
                for i in range(4):
                    dve.wait_ge(*at("mg_hi", i + 1, l))
                    V.tensor_tensor(hl[:, 2 * i:2 * i + 2, :], mg[:, 2 * i:2 * i + 2, :],
                                    hh[:, 2 * i:2 * i + 2, :].bitcast(F32), ALU.subtract).then_inc(*one("mg_lo"))
                for s in range(MIX_OUT + 2, FFN2_IN + 2):
                    split(s, still, l)
                evac_out(l, 1, hgate[:, 1, :])
                norm(l, 2)
                ffn(l, 1)
                mod_part(l, 64, 72, 22)
                half_gate(2, 0.5)
                dve.drain()
                evac_out(l, 2, hgate[:, 2, :])
            dve.wait_ge(*at("rt_ready", 1, DEPTH))
            V.reciprocal(rinv[:, :], rt[:, :]).then_inc(sem("rinv_ready"), 1)
            dve.wait_ge(*at("rb_ready", 1, DEPTH))
            for c in range(KD):
                V.scalar_tensor_tensor(x[:, c, :], x[:, c, :], cact[:, KD + c:KD + c + 1], PS[:, 3, T:2 * T],
                                       ALU.mult, ALU.mult).then_inc(sem("y_ready"), 1)

        @block.gpsimd
        def _(pool):
            G = nc.gpsimd

            def ffn(l, f):
                s0 = FFN1_IN if f == 0 else FFN2_IN
                for s, o in steps(pool, s0, KF):
                    j = s - s0
                    pool.wait_ge(*at("hf_ready", f * KF + j + 1 + o(4), l))
                    dh = hidh[:, bass.ds(o(4) + j, 1), :].rearrange("p a b -> p (a b)")
                    dl = hidl[:, bass.ds(o(4) + j, 1), :].rearrange("p a b -> p (a b)")
                    pool.sem_inc(sem("pool_on"), 1)
                    G.tensor_copy(dh, hf[:, j % 2, :])
                    pool.drain()
                    G.tensor_tensor(dl, hf[:, j % 2, :], dh.bitcast(F32), ALU.subtract).then_inc(*one("hid_ready"))

            pool.sem_inc(sem("hid_ready"), BEFORE["hid_ready"])
            with pool.Fori(0, DEPTH) as l:
                ffn(l, 0)
                pool.wait_ge(*at("att_in", 7, l))
                mn = const(C_MIN).unsqueeze(1).unsqueeze(1).broadcast_to([P, 2, 2, P])
                for c in range(PAIRS):
                    pool.wait_ge(*at("sb_sp", c + 1, l))
                    z = sbz[:, c % 2].rearrange("p h (b n) -> p h b n", b=3)[:, :, 0:3:2, :]
                    G.tensor_tensor(z, z, mn, ALU.add).then_inc(*one("sb_min"))
                pool.wait_ge(*at("mla_yl", 6, l))
                pool.sem_inc(sem("pool_on"), 1)
                G.memset(pb[:, :, 0:1], 0.0).then_inc(*one("pb_zero"))
                for i in range(6):
                    pool.wait_ge(*at("pb_ready", i + 1, l))
                    for c in (2 * i, 2 * i + 1):
                        G.tensor_tensor(m[:, c, :], pb[:, c, 0:T], pb[:, c, 1:T + 1], ALU.subtract)\
                            .then_inc(*one("shift_d"))
                pool.wait_ge(*at("shifted", 12, l))
                pool.sem_inc(sem("pool_on"), 1)
                for c in range(3):
                    ins = G.tensor_scalar(kk[:, c, :], kp[:, c, :], vec[:, V_KK + c:V_KK + c + 1], None, ALU.mult)
                ins.then_inc(*one("kk0"))
                pool.wait_ge(*at("e_cum", 1, l))
                for tt in range(TT):
                    pool.wait_ge(*at("at_ready", tt + 1, l))
                    for b in range(5):
                        if b:
                            pool.wait_ge(*at("z_done", 5 * tt + b, l))
                        G.tensor_tensor(X[:, :, :, :], AT[:, :, :, :],
                                        const(LEVELS[b]).unsqueeze(1).unsqueeze(1).broadcast_to([P, 2, 3, P]),
                                        ALU.mult).then_inc(*one("X_ready"))
                    for q in (2 * tt, 2 * tt + 1):
                        if q:
                            pool.wait_ge(*at("S_ready", q + 1, l))
                        G.tensor_tensor(pcm[:, :, :],
                                        const(C_BLK).unsqueeze(1).broadcast_to([P, 3, P]),
                                        cum[:, :, 64 * q + 63:64 * q + 64].broadcast_to([P, 3, P]), ALU.mult)\
                            .then_inc(*one("pcm_ready"))
                ffn(l, 1)

        @block.tensor
        def _(pe):
            M = nc.tensor.matmul

            def mm3(out, wsl, rhs_h, rhs_l, start, stop):
                M(out, wh[(slice(None),) + wsl], rhs_h, start=start, stop=False, skip_group_check=True)
                M(out, wh[(slice(None),) + wsl], rhs_l, start=False, stop=False, skip_group_check=True)
                return M(out, wl[(slice(None),) + wsl], rhs_h, start=False, stop=stop, skip_group_check=True)

            def in_tile(s, half, b, col, n=P, ready=None):
                for k in range(KD):
                    if ready:
                        ready(k)
                    w0 = (half * KD + k) * n
                    last = mm3(PS[0:n, b, col:col + T], (s % 2, slice(w0, w0 + n)), hh[:, k, :], hl[:, k, :],
                               k == 0, k == KD - 1)
                return last

            def split_ready(s, half, o, l):
                pe.wait_ge(*at("w_split", 2 * s + half + 1 + o(8), l))

            def row_slot(s, banks, first, last_, moving, l, o):
                for k in range(2):
                    split_ready(s, k, o, l)
                    for c in range(KD):
                        w0 = k * D + c * P
                        rh, rl = moving(k)
                        ins = mm3(PS[:, banks[c // 2], (c % 2) * T:(c % 2 + 1) * T], (s % 2, slice(w0, w0 + P)),
                                  rh, rl, first and k == 0 and c % 2 == 0, last_ and k == 1)
                        if last_ and k == 1 and c % 2 and c < KD - 1:
                            ins.then_inc(*one("out_done"))
                ins.then_inc(*one("w_used"))

            def tok_mm(out, k, t, wsl):
                ts = slice(t * P, (t + 1) * P)
                w = (slice(None),) + wsl
                M(out, hh[:, k, ts], wh[w], start=(k == 0), stop=False)
                M(out, hl[:, k, ts], wh[w], start=False, stop=False)
                return M(out, hh[:, k, ts], wl[w], start=False, stop=(k == KD - 1))

            def norm(l, n, inc=one):
                b = NORM_BANK[n]
                for c in range(KD):
                    pe.wait_ge(*at("sq_ready", n * KD + c + 1, l))
                    for t in range(TT):
                        ins = M(PS[:, b, t:t + 1], scr[:, c, t * P:(t + 1) * P], onecol,
                                start=(c == 0 and t == 0), stop=(c == KD - 1), skip_group_check=True)
                    ins.then_inc(*inc("sq_used"))
                pe.wait_ge(*at("rinv_ready", n + 1, l))
                for t in range(TT):
                    ins = M(PS[:, b, T + t * P:T + (t + 1) * P], rinv[:, t:t + 1].broadcast_to([P, P]), ident,
                            start=(t == 0), stop=True, skip_group_check=True)
                ins.then_inc(*inc("rb_ready"))

            def ada_sum(gr, l, o=still, r=0, inc=one):
                col = 4 * ada_place(2 * gr, 0)[1]
                pe.wait_ge(*at("ada_used", 2 * gr + 2 + o(2 * r), l))
                for i in range(4):
                    ins = M(PS[:, 7, bass.ds(o(4 * r) + col + i, 1)], acc[:, i * P:(i + 1) * P], onecol,
                            start=True, stop=True)
                ins.then_inc(*inc("acc_used"))

            def ffn(l, f):
                s0, s1 = (FFN1_IN, FFN1_OUT) if f == 0 else (FFN2_IN, FFN2_OUT)
                for s, o in steps(pe, s0, KF, peel=(2, 6)[f]):
                    j = s - s0
                    pe.wait_ge(*at("hf_ready", f * KF + j - 3 + o(4), l))
                    for half in range(2):
                        split_ready(s, half, o, l)
                        ready = (lambda k: pe.wait_ge(*at("h_ready", f * 2 * KD + k + 1, l))) if j + half == 0 else None
                        ins = in_tile(s, half, j % 4, half * T, ready=ready)
                    ins.then_inc(*one("w_used"))
                    if f == 0 and j % 4 == 3:
                        ada_sum(4 + j // 4, l, o, 1)
                    if f == 1 and j % 4 == 3 and j >= 7:
                        ada_sum(16 + (j - 7) // 4, l, o, 1)
                for s, o in steps(pe, s1, 11, peel=1, tail=2):
                    j = s - s1
                    pe.wait_ge(*at("hid_ready", f * KF + 2 * j + 2 + o(8), l))
                    if s == s1:
                        pe.wait_ge(*at("hid_ready", f * KF + 19, l))

                    def moving(k):
                        r = bass.ds(o(8) + 2 * j + k, 1)
                        return (hidh[:, r, :].rearrange("p a b -> p (a b)"),
                                hidl[:, r, :].rearrange("p a b -> p (a b)"))

                    row_slot(s, OUT_BANKS[2 * f], s == s1, s == s1 + 10, moving, l, o)
                    if f == 0 and j in (2, 10):
                        ada_sum(9 if j == 2 else 11, l, o, 1)
                    if f == 1 and j == 4:
                        ada_sum(20, l, o, 1)

            pe.wait_ge(sem("cst_loaded"), 16)
            pe.wait_ge(sem("c_loaded"), 32)
            pe.wait_ge(sem("zeroed"), 1)
            nc.tensor.transpose(PS[:, 6, 0:P], vrows[:, 0, :], ident).then_inc(sem("cT_ready"), 1)
            pe.wait_ge(sem("x_loaded"), 16)
            pe.sem_inc(sem("w_used"), BEFORE["w_used"])
            for i in range(4):
                for c in (2 * i, 2 * i + 1):
                    for t in range(TT):
                        col = ((c % 2) * 2 + t) * P
                        ins = nc.tensor.transpose(PS[:, i, col:col + P], xin[:, t, c * P:(c + 1) * P], ident)
                ins.then_inc(sem("x_tr"), 1)
            pe.wait_ge(sem("cact_ready"), 1)
            for gr in range(4):
                ada_sum(gr, 0, inc=once)

            with pe.Fori(0, DEPTH) as l:
                pe.wait_ge(sem("rows_loaded"), (l + 1) * (16 * 13))
                pe.wait_ge(*at("x_ready", KD, l))
                nc.tensor.transpose(PS[:, 0, 0:P], vrows[:, 0, :], ident)
                nc.tensor.transpose(PS[:, 0, P:2 * P], vrows[:, 1, :], ident).then_inc(*one("vec_rows"))
                norm(l, 0)
                ffn(l, 0)
                norm(l, 1)
                pe.wait_ge(*at("h_ready", 2 * KD, l))
                for s in range(ATT_IN, RW_IN):
                    i = s - ATT_IN
                    split_ready(s, 1, still, l)
                    if s == SLOT_V:
                        for t in range(TT):
                            for k in range(KD):
                                ins = tok_mm(PS[:, i, t * 256:(t + 1) * 256], k, t, (s % 2, slice(k * 256, (k + 1) * 256)))
                    elif i == 4:
                        for t in range(TT):
                            for k in range(KD):
                                tok_mm(PS[:, i, t * P:(t + 1) * P], k, t, (s % 2, slice(k * P, (k + 1) * P)))
                        ins = in_tile(s, 1, i, T)
                    else:
                        n = 96 if s == SLOT_KR else P
                        in_tile(s, 0, i, 0, n)
                        ins = in_tile(s, 1, i, T, n)
                    ins.then_inc(*one("w_used"))
                    if i == 3:
                        ada_sum(12, l)
                pe.wait_ge(*at("att_in", 7, l))

                def sb_scores(c):
                    if c == 2:
                        pe.wait_ge(*at("sb_lw", 1, l))
                    for h in range(2):
                        r = slice(64 * h, 64 * h + 64)
                        b = 2 * (c % 2) + h
                        q, k = qk[:, c, :], qk[:, 3 + c, :]
                        M(PS[:, b, 0:T], k[r, 0:P], q[r, :], start=True, stop=True)
                        ins = M(PS[:, b, T:384], k[r, P:T], q[r, P:T], start=True, stop=True)
                    ins.then_inc(*one("sb_scored"))

                def sb_sum(c):
                    pe.wait_ge(*at("sb_sp", c + 1, l))
                    pe.wait_ge(*at("sb_ln", c + 1, l))
                    for h in range(2):
                        b = 2 * (c % 2) + h
                        s0, s1 = sbs[:, c % 2, h, 0:T], sbs[:, c % 2, h, T:384]
                        M(PS[:, b, 0:T], const(C_TRI), s0, start=True, stop=False, skip_group_check=True)
                        M(PS[:, b, P:T], ones, s1, start=False, stop=True, skip_group_check=True)
                        ins = M(PS[:, b, T:384], const(C_TRI), s1, start=False, stop=True, skip_group_check=True)
                    ins.then_inc(*one("sb_summed"))

                def sb_y(c):
                    pe.wait_ge(*at("sb_w", c + 1, l))
                    for h in range(2):
                        r = slice(64 * h, 64 * h + 64)
                        hc = slice((2 * c + h) * 64, (2 * c + h) * 64 + 64)
                        M(PS[r, 4 + c, 0:T], vs[:, 0, hc], sbe[:, c % 2, h, 0:T], start=True, stop=False,
                          skip_group_check=True)
                        ins = M(PS[r, 4 + c, P:T], vs[:, 1, hc], sbe[:, c % 2, h, T:384], start=False, stop=True,
                                skip_group_check=True)
                    ins.then_inc(*one("sb_y"))

                sb_scores(0)
                sb_scores(1)
                sb_sum(0)
                sb_sum(1)
                sb_y(0)
                sb_scores(2)
                sb_y(1)
                sb_sum(2)
                sb_y(2)
                pe.wait_ge(*at("mla_sq", 1, l))
                pe.wait_ge(*at("sb_lw", 3, l))
                for i, (c, st, sp_) in enumerate(((0, True, False), (1, False, True), (2, True, True))):
                    for t in range(TT):
                        col = t if c < 2 else 2 + t
                        ins = M(PS[:, 3, col:col + 1], scr[:, c, t * P:(t + 1) * P], onecol, start=(i == 0 and t == 0),
                                stop=sp_, skip_group_check=True)
                ins.then_inc(*one("mla_sum"))
                pe.wait_ge(*at("mla_rinv", 1, l))
                pe.wait_ge(*at("sb_yl", 2, l))
                for i in range(2):
                    for t in range(TT):
                        ins = M(PS[:, 4 + i, t * P:(t + 1) * P],
                                hstat[:, 1, 2 * i + t:2 * i + t + 1].broadcast_to([P, P]), ident, start=True, stop=True)
                ins.then_inc(*one("mla_rb"))
                pe.wait_ge(*at("mla_lat", 3, l))
                pe.wait_ge(sem("small_loaded"), (l + 1) * (16 * 10))
                for i in range(PAIRS):
                    for h in range(2):
                        c0 = (2 * i + h) * P
                        ins = M(PS[0:NOPE, i, h * T:(h + 1) * T], w_ukv[:, c0:c0 + NOPE], cqkv[:, 2, :],
                                start=True, stop=True)
                    ins.then_inc(*one("mla_k"))
                pe.wait_ge(*at("sb_yl", 3, l))
                vcols = w_ukv[:, :].rearrange("p (h n) -> p h n", h=HEADS)[:, :, NOPE:P]
                for t in range(TT):
                    ins = M(PS[:, 6 + t, 0:BW], cqkv[:, 2, t * P:(t + 1) * P], vcols, start=True, stop=True)
                ins.then_inc(*one("mla_v"))
                for i in range(PAIRS):
                    if i:
                        pe.wait_ge(*at("mla_qr", i, l))
                    if i == 2:
                        pe.wait_ge(*at("mla_qn", 1, l))
                    for h in range(2):
                        hd = 2 * i + h
                        for k in range(2):
                            M(PS[0:96, 3 + (i % 2), h * T:(h + 1) * T], w_uq[:, k, hd * 96:(hd + 1) * 96], cqkv[:, k, :],
                              start=(k == 0), stop=(k == 1))
                        for k in range(2):
                            ins = M(PS[NOPE:96, 5, h * T:(h + 1) * T], w_sw[:, k, hd, :], cqkv[:, k, :],
                                    start=(k == 0), stop=(k == 1))
                    ins.then_inc(*one("mla_q"))
                pe.wait_ge(*at("mla_kv_ready", 2, l))
                pe.wait_ge(*at("mla_qr", 3, l))
                pe.wait_ge(*at("mla_qn", 3, l))
                for r in range(2):
                    for i in range(3):
                        h = 3 * r + i
                        M(PS[:, h, 0:P], qT[0:96, h, 0:P], kT[0:96, h, 0:P], start=True, stop=True)
                        ins = M(PS[:, h, P:384], qT[0:96, h, P:T], kT[0:96, h, :], start=True, stop=True)
                    ins.then_inc(*one("mla_scored"))
                for r in range(2):
                    pe.wait_ge(*at("mla_pr", r + 1, l))
                    for i in range(3):
                        h = 3 * r + i
                        if h:
                            pe.wait_ge(*at("mla_p", h, l))
                        for j in range(3):
                            ins = nc.tensor.transpose(PS[:, 6, j * P:(j + 1) * P], mls[:, i, j * P:(j + 1) * P], ident)
                        ins.then_inc(*one("mla_tr"))
                        pe.wait_ge(*at("mla_p", h + 1, l))
                        if h:
                            pe.wait_ge(*at("mla_yl", h, l))
                        o = 64 * (h % 2)
                        M(PS[o:o + 64, 7, 0:T], vm[:, 0, h * 64:(h + 1) * 64], mlp[:, i, 0:T], start=True, stop=False,
                          skip_group_check=True)
                        M(PS[o:o + 64, 7, P:T], vm[:, 1, h * 64:(h + 1) * 64], mlp[:, i, T:384], start=False,
                          stop=True, skip_group_check=True).then_inc(*one("mla_y"))
                for i in range(6):
                    s = RW_IN + i
                    if i == 0:
                        pe.wait_ge(*at("mla_yl", 6, l))
                    if i >= 4:
                        pe.wait_ge(*at("pb_ready", i - 3, l))
                    split_ready(s, 1, still, l)
                    in_tile(s, 0, i % 4, 0)
                    in_tile(s, 1, i % 4, T).then_inc(*one("w_used"))
                pe.wait_ge(*at("lora_in", 1, l))
                for c in range(3):
                    cs, col = slice(c * P, (c + 1) * P), slice((c % 2) * T, (c % 2 + 1) * T)
                    M(PS[:, 2 + c // 2, col], lora[0:64, cs], ex[0:64, 0, :], start=True, stop=True)
                    M(PS[:, 4 + c // 2, col], lora[64:128, cs], m[64:128, 9, :], start=True, stop=True)
                for c in range(3):
                    cs, col = slice(c * P, (c + 1) * P), slice((c % 2) * T, (c % 2 + 1) * T)
                    M(PS[:, 6 + c // 2, col], lora_g[:, 0, cs], m[:, 10, :], start=True, stop=False)
                    ins = M(PS[:, 6 + c // 2, col], lora_g[96:128, 1, cs], m[96:128, 11, :], start=False, stop=True)
                ins.then_inc(*one("lora_done"))

                def head_stats(src, name):
                    for c in range(3):
                        for t in range(TT):
                            col = (t * 3 + c) * 2
                            ins = M(PS[:, 3, col:col + 2], src[:, c, t * P:(t + 1) * P], blk2, start=True, stop=True)
                    ins.then_inc(*one(name))

                def head_spread(name):
                    for c in range(3):
                        for t in range(TT):
                            col = (t * 3 + c) * 2
                            o = (c % 2) * T + t * P
                            for h in range(2):
                                w = hstat[:, 1, col + h:col + h + 1].broadcast_to([P, 64])
                                ins = M(PS[64 * h:64 * h + 64, 4 + c // 2, o:o + P], w, ident, start=True, stop=True)
                    ins.then_inc(*one(name))

                pe.wait_ge(*at("kk_sq", 1, l))
                pe.wait_ge(*at("wa_ready", 3, l))
                head_stats(ex, "kk_stat")
                pe.wait_ge(*at("bon_in", 1, l))
                pe.wait_ge(*at("g_ready", 1, l))
                for c in range(3):
                    ins = M(PS[:, 6 + c // 2, (c % 2) * T:(c % 2 + 1) * T], blk, bon[:, c, :], start=True, stop=True)
                ins.then_inc(*one("bon_done"))
                pe.wait_ge(*at("kk_rinv", 1, l))
                head_spread("kk_rb")
                pe.wait_ge(*at("tilde", 1, l))

                def A(dst, lhs, rhs, tt, name):
                    ts = slice(tt * P, (tt + 1) * P)
                    for par in range(2):
                        r = slice(64 * par, 64 * par + 64)
                        for c in range(3):
                            ins = M(PS[:, dst + par, c * P:(c + 1) * P], lhs[:, c, ts][r], rhs[:, c, ts][r],
                                    start=True, stop=True)
                    ins.then_inc(*one(name))

                for tt in range(TT):
                    ts = slice(tt * P, (tt + 1) * P)
                    pe.wait_ge(*at("S_ready", 2 * tt + 1, l))
                    for i, src in enumerate((kk, av, kp, vv)):
                        for c in range(3):
                            ins = nc.tensor.transpose(PS[:, i, c * P:(c + 1) * P], src[:, c, ts], ident)
                    ins.then_inc(*one("tok_done"))
                    A(4, av, kk, tt, "ab_done")
                    if tt:
                        pe.wait_ge(*at("ya_ready", tt, l))
                    A(6, kk, av, tt, "ab_done")
                    pe.wait_ge(*at("at_ready", tt + 1, l))
                    A(4, kp, kk, tt, "ak_done")
                    pe.wait_ge(*at("T_ready", 6 * tt + 1, l))
                    A(6, av, rr, tt, "ak_done")
                    pe.wait_ge(*at("ak_ready", 3 * tt + 1, l))
                    A(4, kp, rr, tt, "ak_done")
                    pe.wait_ge(*at("tok_act", 2 * tt + 2, l))
                    pe.wait_ge(*at("tok_dve", tt + 1, l))
                    for b in range(5):
                        pe.wait_ge(*at("X_ready", 5 * tt + b + 1, l))
                        pe.wait_ge(*at("T_ready", 6 * tt + b + 1, l))
                        for p_ in range(2):
                            for c in range(3):
                                ins = M(PS[:, p_, c * P:(c + 1) * P], X[:, p_, c, :], Tm[:, p_, c, :], start=True,
                                        stop=True)
                        ins.then_inc(*one("z_done"))
                        pe.wait_ge(*at("z_ready", 5 * tt + b + 1, l))
                        if b == 0:
                            pe.wait_ge(*at("ak_ready", 3 * tt + 3, l))
                        for p_ in range(2):
                            for c in range(3):
                                if b < 4:
                                    M(PS[:, 2 + p_, c * P:(c + 1) * P], TTm[:, p_, c, :], Z[:, p_, c, :], start=True,
                                      stop=True)
                                ins = M(PS[:, 4 + p_, c * P:(c + 1) * P], Z[:, p_, c, :], TTm[:, p_, c, :],
                                        start=True, stop=True)
                        ins.then_inc(*one("tz_done"))
                    for h in range(HEADS):
                        hc = slice(h * 64, h * 64 + 64)
                        ins = M(PS[:, 0, hc], Aak[:, h % 2, h // 2, :], tok[:, 3, hc], start=True, stop=True)
                    ins.then_inc(*one("g_done"))
                    pe.wait_ge(*at("T_ready", 6 * tt + 6, l))
                    for h in range(HEADS):
                        r = slice(64 * (h % 2), 64 * (h % 2) + 64)
                        ins = M(PS[r, 4, (h // 2) * P:(h // 2 + 1) * P], tok[:, 0, h * 64:h * 64 + 64],
                                TTm[:, h % 2, h // 2, :], start=True, stop=True)
                    ins.then_inc(*one("wt_done"))
                    pe.wait_ge(*at("G_ready", tt + 1, l))
                    for h in range(HEADS):
                        hc = slice(h * 64, h * 64 + 64)
                        ins = M(PS[:, 1, hc], TTm[:, h % 2, h // 2, :], Gm[:, hc], start=True, stop=True)
                    ins.then_inc(*one("u0_done"))
                    pe.wait_ge(*at("wt_ready", tt + 1, l))
                    for q in (2 * tt, 2 * tt + 1):
                        rows = slice(64 * (q % 2), 64 * (q % 2) + 64)
                        pe.wait_ge(*at("S_ready", q + 1, l))
                        for c in range(3):
                            ins = M(PS[:, 5, c * P:(c + 1) * P], wT[:, c, :], S[:, c, :], start=True, stop=True)
                        ins.then_inc(*one("u_done"))
                        for c in range(3):
                            o = c * P + 64 * (q % 2)
                            M(PS[:, 6, o:o + 64], S[:, c, :], rr[:, c, q * 64:q * 64 + 64],
                              start=(q % 2 == 0 and c == 0), stop=False, skip_group_check=True)
                        pe.wait_ge(*at("u_ready", q + 1, l))
                        for c in range(3):
                            cs = slice(c * P, (c + 1) * P)
                            M(PS[:, 3, cs], tok[rows, 1, cs], u_[rows, cs], start=True, stop=False)
                            ins = M(PS[:, 3, cs], tok[rows, 2, cs], tok[rows, 3, cs], start=False, stop=True)
                        ins.then_inc(*one("s_done"))
                    for h in range(HEADS):
                        r = slice(64 * (h % 2), 64 * (h % 2) + 64)
                        cs, hc = slice((h // 2) * P, (h // 2 + 1) * P), slice(h * 64, h * 64 + 64)
                        M(PS[r, 6, cs], u_[:, hc], Arb[:, h % 2, h // 2, :], start=False, stop=False,
                          skip_group_check=True)
                        ins = M(PS[r, 6, cs], tok[:, 3, hc], Ark[:, h % 2, h // 2, :], start=False, stop=True,
                                skip_group_check=True)
                    ins.then_inc(*one("y_done"))
                pe.wait_ge(*at("ya_ready", 2, l))
                for c in range(3):
                    ins = M(PS[:, c // 2, (c % 2) * T:(c % 2 + 1) * T], blk, ya[:, c, :], start=True, stop=True)
                ins.then_inc(*one("gn_mean"))
                pe.wait_ge(*at("gn_sq", 1, l))
                head_stats(ex, "gn_stat")
                pe.wait_ge(*at("gn_rinv", 1, l))
                head_spread("gn_rb")
                for s, o in steps(pe, GATE_IN, 12, tail=4):
                    j = s - GATE_IN
                    pe.wait_ge(*at("gate_ready", j - 3 + o(4), l))
                    for half in range(2):
                        split_ready(s, half, o, l)
                        ins = in_tile(s, half, j % 4, half * T)
                    ins.then_inc(*one("w_used"))
                    if j % 4 == 3:
                        ada_sum(13 + j // 4, l, o, 1)
                pe.wait_ge(*at("mod_done", 1, l))
                pe.wait_ge(*at("ya_lo", 1, l))
                pe.wait_ge(*at("gate_ready", 12, l))
                for kb in range(9):
                    n, k = kb // 3, kb % 3
                    s = BRANCH + kb // 2
                    split_ready(s, kb % 2 if kb < 8 else 1, still, l)
                    if n == 2 and k == 0:
                        pe.wait_ge(*at("br_used", 4, l))
                    w0 = (kb % 2) * D
                    for c in range(KD):
                        b = BR_BANKS[n] + c // 2
                        ins = mm3(PS[:, b, (c % 2) * T:(c % 2 + 1) * T], (s % 2, slice(w0 + c * P, w0 + (c + 1) * P)),
                                  yh[:, kb, :], yl[:, kb, :], k == 0 and c % 2 == 0, k == 2)
                        if c == KD - 1 and (kb % 2 or kb == 8):
                            ins.then_inc(*one("w_used"))
                        elif k == 2 and c % 2:
                            ins.then_inc(*one("br_done"))
                pe.wait_ge(*at("br_used", 8, l))
                for i in range(4):
                    s = MIX_OUT + i
                    pe.wait_ge(*at("mg_lo", i + 1, l))
                    row_slot(s, OUT_BANKS[1], i == 0, i == 3,
                             lambda k: (hh[:, 2 * i + k, :], hl[:, 2 * i + k, :]), l, still)
                norm(l, 2)
                ffn(l, 1)
            norm(DEPTH, 0, inc=once)
            pe.wait_ge(sem("y_ready"), KD)
            for t in range(TT):
                for c in range(KD):
                    o = (c % 4) * P
                    ins = nc.tensor.transpose(PS[:, 2 * t + 4 + c // 4, o:o + P], x[:, c, t * P:(t + 1) * P], ident)
                ins.then_inc(sem("out_tr"), 1)


_INS = ["x", "c", "positions", "ada_w", "ada_b", "norm_g", "ffn1_w_in", "ffn1_w_out", "mix_w_in", "rwkv_mu",
        "rwkv_w0", "rwkv_w2", "rwkv_a0", "rwkv_a2", "rwkv_g2", "rwkv_k_k", "rwkv_k_a", "rwkv_r_k", "rwkv_lnx_g",
        "rwkv_lnx_b", "mla_q_norm_g", "mla_w_uq", "mla_kv_norm_g", "mla_w_ukv", "branch_w", "mix_w_out",
        "ffn2_w_in", "ffn2_w_out", "final_norm_g"]


def build(nc, shapes):
    args = {n: nc.dram_tensor(f"in_{n}", shape, dt, kind="ExternalInput").ap() for n, (shape, dt) in shapes.items()}
    args["out"] = nc.dram_tensor("out_0", (1, T, D), F32, kind="ExternalOutput").ap()
    tally = {}
    hybrid_trunk(nc, args, PER_LAYER, tally)
    return tally


def kernel(**inputs):
    import concourse.bacc as _bacc
    from concourse.bass_utils import run_bass_kernel_spmd as _run

    arrays = {n: np.ascontiguousarray(inputs[n]) for n in _INS}
    arrays["consts"] = shape_constants()
    nc = _bacc.Bacc("TRN2", target_bir_lowering=False, num_devices=1, dynamic_dma_scratch_size=1024)
    build(nc, {n: (v.shape, mybir.dt.from_np(v.dtype)) for n, v in arrays.items()})
    r = _run(nc, [{f"in_{n}": v for n, v in arrays.items()}], core_ids=[0])
    return r.results[0]["out_0"]
```

```python
from contextlib import ExitStack

import numpy as np

import concourse.bass as bass
from concourse import mybir

F32 = mybir.dt.float32
F32R = mybir.dt.float32r
I32 = mybir.dt.int32
ALU = mybir.AluOpType
ACT = mybir.ActivationFunctionType
AX_X = mybir.AxisListType.X

P = 128
DEPTH, D, T, F = 2, 1024, 256, 2816
KD, KF, TT = D // P, F // P, T // P
HEADS, HD, BW, NB = 6, 64, 384, 3
PAIRS = HEADS // 2
LORA_W, LORA_A, LORA_G = 64, 64, 160
Q_LORA, KV_LORA, ROPE, NOPE = 256, 128, 32, 64
RW_COLS = 3 * BW + LORA_W + LORA_A + LORA_G
SBQ, SBV = RW_COLS, RW_COLS + 2 * BW
CQ = RW_COLS + 3 * BW
CKV = CQ + Q_LORA
KR = CKV + KV_LORA
GATE0 = KR + ROPE
D_IN = GATE0 + NB * D
N_ADA = 9
CHUNK = 64
EPS, GN_EPS = 1e-6, 64e-5
SB_SCALE = HD ** -0.5
MLA_SCALE = (NOPE + ROPE) ** -0.5
NEG = -1e30

SLOT = 2048
FFN1_IN, FFN1_OUT = 0, 22
ATT_IN, RW_IN, GATE_IN = 33, 40, 46
BRANCH, MIX_OUT = 58, 63
FFN2_IN, FFN2_OUT = 67, 89
SLOTS = 100
IN_COLS = {
    33: (SBQ, SBQ + 128), 34: (SBQ + 256, SBQ + 384), 35: (SBQ + 512, SBQ + 640),
    37: (SBV + 256, CKV), 38: (CQ, CQ + 128),
    40: (0, 128), 41: (256, 384), 42: (512, 640), 43: (768, 896), 44: (1024, 1152),
    45: (1280, RW_COLS - 128),
}
SLOT_V, SLOT_KR = 36, 39


def slot_size(s):
    if s == SLOT_KR:
        return 2 * KD * 96
    return D if s == MIX_OUT - 1 else SLOT


def slot_dmas(s):
    s %= SLOTS
    if s == SLOT_KR:
        return 3
    if s == SLOT_V or FFN1_OUT <= s < ATT_IN or BRANCH <= s < FFN2_IN or s >= FFN2_OUT:
        return 1
    return 2


def dmas_before(s):
    return sum(slot_dmas(x) for x in range(s % 4, s + 1, 4))


V_ADA, V_NORM, V_MU, V_W0, V_A0, V_KK, V_KA, V_RK, V_LG, V_LB, V_QN, V_KVN = (
    0, 72, 96, 108, 111, 114, 117, 120, 123, 126, 129, 131)
N_VEC = 132

(C_ID, C_ONE, C_BLK, C_TRI, C_SBM, C_MIN, C_CAUS, C_LO1, C_UP, C_UPI, C_UP1, C_UP2, C_UP4, C_UP8,
 C_UP16, C_UP32, C_RST0, C_RST1, C_ROPE) = range(19)
LEVELS = (C_UP2, C_UP4, C_UP8, C_UP16, C_UP32)


def shape_constants():
    r, c = np.arange(P)[:, None], np.arange(P)[None, :]
    same = (r // CHUNK) == (c // CHUNK)
    out = [np.eye(P), np.ones((P, P)), same, r >= c, r < c, np.where(r < c, 0.0, NEG),
           np.where(c <= r, 0.0, NEG), (r // 2 == c // 2) & (r > c), same & (r < c), same & (r <= c)]
    for b in (1, 2, 4, 8, 16, 32):
        out.append((r // (2 * b) == c // (2 * b)) & (r % (2 * b) < b) & (c % (2 * b) >= b))
    reset = np.ones((P, T))
    reset[:, ::CHUNK] = 0.0
    out += [reset[:, :P], reset[:, P:]]
    rope = np.zeros((P, P))
    half = ROPE // 2
    freq = (1.0 / (np.float32(10000.0) ** (np.arange(0, ROPE, 2, dtype=np.float32) / np.float32(ROPE))))
    rope[NOPE:NOPE + half, 0] = freq
    rope[NOPE + half:NOPE + ROPE, 0] = freq
    rope[NOPE:NOPE + half, 1] = -1.0
    rope[NOPE + half:NOPE + ROPE, 1] = 1.0
    out.append(rope)
    return np.concatenate([x.astype(np.float32) for x in out], axis=1)


PER_LAYER = {
    "vec_ready": 1, "w_hi": 200, "hh_ready": 24, "sil_ready": 44, "sq_ready": 24, "rt_ready": 3,
    "att_in": 7, "sb_z": 3, "sb_ln": 3, "sb_w": 3, "sb_yh": 3, "mla_sq": 1, "mla_rt": 1,
    "mla_kv_ready": 2, "mla_qn": 3, "mla_sc": 2, "mla_exp": 2, "mla_p": 6, "mla_yh": 3, "pb_ready":
    6, "lora_in": 1, "wa_ready": 3, "g_ready": 1, "kk_sq": 1, "kk_rt": 1, "e_neg": 1, "e_cum": 1,
    "e_prev": 1, "tok_act": 4, "z_ready": 20, "wt_ready": 2, "ya_ready": 2, "gn_sq": 1, "gn_rt": 1,
    "ya_hi": 1, "gate_ready": 12, "mg_hi": 4, "w_split": 200, "t_ready": 24, "h_ready": 24,
    "hf_ready": 44, "ada_used": 36, "x_ready": 24, "sb_sp": 3, "sb_lw": 3, "sb_yl": 3, "mla_rinv":
    1, "mla_lat": 3, "mla_qr": 3, "mla_sub": 2, "mla_pr": 2, "mla_yl": 3, "shifted": 12,
    "cum_ready": 1, "kk_max": 1, "bon_in": 1, "kk_rinv": 1, "tilde": 1, "S_ready": 5, "tok_dve": 2,
    "at_ready": 2, "T_ready": 22, "ak_ready": 6, "G_ready": 2, "u0_ready": 2, "u_ready": 4,
    "gn_sub": 1, "gn_rinv": 1, "ya_final": 1, "ya_lo": 1, "mod_done": 1, "br_used": 12, "merged": 4,
    "mg_lo": 4, "hid_ready": 44, "sb_min": 3, "pb_zero": 1, "shift_d": 12, "kk0": 1, "X_ready": 10,
    "pcm_ready": 4, "vec_rows": 1, "w_used": 100, "acc_used": 18, "out_done": 9, "sq_used": 24,
    "sb_scored": 3, "sb_summed": 3, "sb_y": 3, "mla_sum": 1, "mla_rb": 1, "mla_k": 3, "mla_v": 1,
    "mla_q": 3, "mla_scored": 2, "mla_tr": 6, "mla_y": 3, "lora_done": 1, "kk_stat": 1, "bon_done":
    1, "kk_rb": 1, "tok_done": 2, "ab_done": 4, "ak_done": 6, "z_done": 20, "tz_done": 20, "g_done":
    2, "wt_done": 2, "u0_done": 2, "u_done": 4, "s_done": 4, "y_done": 2, "gn_mean": 1, "gn_stat":
    1, "gn_rb": 1, "br_done": 10,
}
BEFORE = {"w_split": 7, "w_used": 2, "hf_ready": 4, "hid_ready": 2, "gate_ready": 4, "vec_rows": 1, "lora_done": 1}
OUT_BANKS = ((4, 5, 6, 2), (0, 1, 2, 3), (4, 5, 6, 2))
BR_BANKS = (4, 0, 4)
NORM_BANK = (3, 3, 4, 3)


def hybrid_trunk(nc, a, per_layer, tally):
    out_dram = a["out"]
    ctx = ExitStack()
    with ctx:
        ctx.enter_context(nc.allow_non_contiguous_dma(reason="vectors and column blocks"))

        def sb(name, shape, dt=F32):
            return ctx.enter_context(nc.sbuf_tensor(name, shape, dt))

        raw = sb("raw", [P, 4, SLOT])
        wh = sb("wh", [P, 2, SLOT], F32R)
        wl = sb("wl", [P, 2, SLOT], F32R)
        ada_w = sb("ada_w_ring", [P, 2, SLOT])
        acc = sb("ada_acc", [P, 512])
        x = sb("x", [P, KD, T])
        hh = sb("h_hi", [P, KD, T], F32R)
        hl = sb("h_lo", [P, KD, T], F32R)
        scr = sb("scr", [P, KD, T])
        cst = sb("cst", [P, 19 * P])
        vrows = sb("vrows", [P, 2, P])
        vec = sb("vec", [P, N_VEC])
        mod = sb("mod", [P, N_ADA * KD])
        gsc = sb("gsc", [P, 3, KD])
        hgate = sb("hgate", [P, 3, KD])
        omka = sb("omka", [P, 3])
        cact = sb("cact", [P, 2 * KD])
        warm = sb("warm", [P, 1])
        mla_stat = sb("mla_stat", [P, 2, 12])
        hstat = sb("hstat", [P, 2, 12])
        epsb = sb("eps_col", [P, 1])
        gneps = sb("gn_eps_col", [P, 1])
        one_b = sb("one_col", [P, 1])
        lora = sb("lora", [P, BW])
        lora_g = sb("lora_g", [P, 2, BW])
        w_uq = sb("w_uq", [P, 2, HEADS * 96])
        w_sw = sb("w_sw", [P, 2, HEADS, ROPE])
        w_ukv = sb("w_ukv", [P, HEADS * P])
        cosT = sb("cosT", [P, T])
        sinT = sb("sinT", [P, T])

        def const(n):
            return cst[:, n * P:(n + 1) * P]

        ident, ones, blk = const(C_ID), const(C_ONE), const(C_BLK)
        onecol = cst[:, C_ONE * P:C_ONE * P + 1]
        blk2 = cst[:, C_BLK * P:C_BLK * P + P:CHUNK]
        reset = cst[:, C_RST0 * P:C_RST0 * P + T]

        base = nc.sbuf_base
        base = (base + 63) // 64 * 64
        room = nc.sbuf_usable_end - base
        cur = [0]
        names = {}

        def at_(name, cols, dt=F32, off=None):
            if off is not None:
                cur[0] = off
            o = cur[0]
            cur[0] += cols * 4
            assert cur[0] <= room, (name, cur[0], room)
            names[name] = o
            return nc.alloc_sbuf_tensor_at(name, [P, cols], dt, offset=base + o)

        def v3(t, n):
            return t[:, :].rearrange("p (a b) -> p a b", a=n)

        hidh = v3(at_("hid_hi", KF * T, F32R, 0), KF)
        hidl = v3(at_("hid_lo", KF * T, F32R), KF)
        sil = v3(at_("sil", 2 * T), 2)
        hf = v3(at_("hf", 2 * T), 2)
        yh = v3(at_("y_hi", 9 * T, F32R, 0), 9)
        yl = v3(at_("y_lo", 9 * T, F32R), 9)
        mix0 = cur[0]
        qk = v3(at_("sb_qk", 6 * T, off=mix0), 6)
        vs = v3(at_("sb_v", 2 * BW), 2)
        cqkv = v3(at_("cqkv", 3 * T), 3)
        qT = v3(at_("mla_qT", HEADS * T), HEADS)
        kT = v3(at_("mla_kT", HEADS * T), HEADS)
        vm = v3(at_("mla_v", 2 * BW), 2)
        krA = v3(at_("krope", 2 * T), 2)
        sbz = at_("sb_z", 2 * 768)[:, :].rearrange("p (r h n) -> p r h n", r=2, h=2)
        sbe = at_("sb_e", 2 * 768)[:, :].rearrange("p (r h n) -> p r h n", r=2, h=2)
        sbs = at_("sb_s", 2 * 768)[:, :].rearrange("p (r h n) -> p r h n", r=2, h=2)
        rA = at_("ropeA", 2 * T)
        rB = at_("ropeB", 2 * T)
        mls = at_("mla_s", 6 * 384, off=names["sb_z"])[:, :].rearrange("p (h n) -> p h n", h=6)
        mlp = at_("mla_p", 6 * 384)[:, :].rearrange("p (h n) -> p h n", h=6)
        m = v3(at_("rw_m", 12 * T, off=mix0), 12)
        lw = v3(at_("rw_lw", 3 * T), 3)
        av = v3(at_("rw_a", 3 * T), 3)
        kk = v3(at_("rw_kk", 3 * T), 3)
        cum = v3(at_("rw_cum", 3 * T), 3)
        ex = v3(at_("rw_e", 3 * T), 3)
        g = v3(at_("rw_g", 3 * T), 3)
        bon = v3(at_("rw_bon", 3 * T), 3)
        rr, kp, vv = m[:, 0:3], m[:, 3:6], m[:, 6:9]
        ya = lw
        tokr = at_("rw_tok", 4 * BW)
        tok = v3(tokr, 4)
        scr_all = scr[:, :, :].rearrange("p a b -> p (a b)")
        u_, u0 = scr_all[:, 0:BW], scr_all[:, BW:2 * BW]
        S, wT, pcm = (scr_all[:, i * BW:(i + 1) * BW].rearrange("p (a b) -> p a b", a=3) for i in (2, 3, 4))
        amat = cur[0]

        def six(name, off=None):
            return at_(name, 6 * P, off=off)[:, :].rearrange("p (a c n) -> p a c n", a=2, c=3)

        AT, X, Tm, TTm, Z, Aak = (six(n) for n in ("A_T", "A_X", "A_inv", "A_invT", "A_Z", "A_ak"))
        Arb, Ark = six("A_rb"), six("A_rk")
        pb = at_("rw_pb", 12 * (T + 1), off=amat)[:, :].rearrange("p (a b) -> p a b", a=12)
        Gm = Z[:, :, :, :].rearrange("p a c n -> p (a c n)")[:, 0:BW]
        gates = v3(at_("gates", 24 * T, off=mix0), 24)
        mg = v3(at_("merged", KD * T), KD)
        mt = v3(at_("merge_t", 4 * T), 4)
        xin = v3(at_("x_rows", 2 * D, off=0), 2)
        xo = v3(at_("out_rows", 2 * D), 2)
        posi = at_("pos_i", T, I32)
        ang = at_("ang", 4 * T)[:, :].rearrange("p (a b) -> p a b", a=4)

        PS = ctx.enter_context(nc.psum_tensor("PS", [P, 8, 512], F32))

        def bank(b):
            return PS[:, b, :]

        sems = {}
        tally.clear()
        times = [1]

        def sem(name):
            if name not in sems:
                sems[name] = ctx.enter_context(nc.semaphore(name))
            return sems[name]

        def one(name, n=1):
            tally[name] = tally.get(name, 0) + n * times[0]
            return sem(name), n

        def once(name, n=1):
            return sem(name), n

        def at(name, k, l=0):
            v = k + BEFORE.get(name, 0)
            return sem(name), l * per_layer.get(name, 0) + v

        def still(n):
            return 0

        def steps(eng, first, count, peel=0, tail=0):
            for s in range(first, first + peel):
                yield s, still
            rounds = (count - peel - tail) // 4
            at0 = first + peel
            times[0] = rounds
            with eng.Fori(0, rounds) as i:
                for u in range(4):
                    yield at0 + u, lambda n: i * n
            times[0] = 1
            for s in range(at0 + 4 * rounds, first + count):
                yield s, still

        def ada_place(n, l):
            if n < 32:
                return l, n // 2
            return ((l + 1) % DEPTH, n // 2 - 16) if n < 40 else (l, n // 2 - 4)

        def loaded(s, o, l):
            q = s % 4
            per = sum(slot_dmas(v) for v in range(q, SLOTS, 4))
            per_round = slot_dmas(s)
            return sem(f"raw_loaded{q}"), l * (16 * per) + 16 * dmas_before(s) + o(16 * per_round)

        block = ctx.enter_context(nc.Block())

        @block.sync
        def _(sp):
            win = [a[n].rearrange("l (k p) n -> p (l k) n", p=P) for n in ("ffn1_w_in", "ffn2_w_in")]
            wout = [a[n].rearrange("l (k p) n -> p (l k) n", p=P) for n in ("ffn1_w_out", "ffn2_w_out")]
            wmix = a["mix_w_in"].rearrange("l (k p) n -> p (l k) n", p=P)
            wbr = a["branch_w"].rearrange("l n (k p) d -> p (l n k) d", p=P)
            wmo = a["mix_w_out"].rearrange("l (k p) n -> p (l k) n", p=P)
            wada = a["ada_w"].rearrange("l (k p) n -> p (l k) n", p=P)

            def free(s, o, l):
                sp.wait_ge(*at("w_split", 2 * (s - 4) + 2 + o(8), l))

            def halves(s, n=P):
                return raw[:, s % 4, 0:2 * KD * n].rearrange("p (g k n) -> p g k n", g=2, k=KD)

            def rows(s, k):
                return raw[:, s % 4, 0:k * D].rearrange("p (k n) -> p k n", k=k)

            def ada(n, o, r, l):
                if n >= 2:
                    sp.wait_ge(*at("ada_used", n - 1 + o(r), l))
                layer, group = ada_place(n, l)
                sp.dma_start(ada_w[:, n % 2, :].rearrange("p (k n) -> p k n", k=4),
                             wada[:, bass.ds(layer * KD + (n % 2) * 4, 4), bass.ds(o(256 * r) + group * 512, 512)])\
                    .then_inc(sem(f"ada_loaded{n % 2}"), 16)

            def ffn_loads(l, f):
                s0, s1 = (FFN1_IN, FFN1_OUT) if f == 0 else (FFN2_IN, FFN2_OUT)
                for s, o in steps(sp, s0, KF, *((0, 0), (4, 2))[f]):
                    j = s - s0
                    free(s, o, l)
                    for half in (1, 0):
                        c0 = half * F + j * P
                        cols = bass.ds(o(4 * P) + c0, P)
                        sp.dma_start(halves(s)[:, half], win[f][:, bass.ds(l * KD, KD), cols])\
                            .then_inc(sem(f"raw_loaded{s % 4}"), 16)
                    if f == 0 and j % 2:
                        ada(8 + j // 2, o, 2, l)
                    if f == 1 and j % 2 and 4 <= j < 20:
                        ada(32 + (j - 4) // 2, o, 2, l)
                for s, o in steps(sp, s1, 11, peel=1, tail=2):
                    j = s - s1
                    free(s, o, l)
                    sp.dma_start(rows(s, 2), wout[f][:, bass.ds(l * KF + 2 * j + o(8), 2), :])\
                        .then_inc(sem(f"raw_loaded{s % 4}"), 16)
                    if j and j % 2 == 0 and j <= (10, 8)[f]:
                        ada((19, 40)[f] + j // 2 - 1, o, 2, l)

            sp.dma_start(cst[:, :], a["consts"]).then_inc(sem("cst_loaded"), 16)
            sp.wait_ge(sem("zeroed"), 1)
            sp.dma_start(vrows[0:KD, 0, :], a["c"].rearrange("b (k p) -> (b k) p", p=P))\
                .then_inc(sem("c_loaded"), 16)
            sp.dma_start(vrows[KD:2 * KD, 0, :], a["final_norm_g"].rearrange("(k p) -> k p", p=P))\
                .then_inc(sem("c_loaded"), 16)
            sp.dma_start(posi[NOPE:NOPE + ROPE, :], a["positions"].broadcast_to([ROPE, T]))\
                .then_inc(sem("pos_loaded"), 16)
            ada(0, still, 0, 0)
            ada(1, still, 0, 0)
            sp.dma_start(xin[:, :, :], a["x"][0].rearrange("(t p) d -> p t d", p=P)).then_inc(sem("x_loaded"), 16)
            for n in range(2, 8):
                ada(n, still, 0, 0)
            with sp.Fori(0, DEPTH) as l:
                sp.wait_ge(sem("cT_ready"), 1)
                sp.wait_ge(*at("vec_rows", 0, l))
                ab = a["ada_b"].rearrange("l (k p) -> (l k) p", p=P)
                ng = a["norm_g"].rearrange("l i (k p) -> (l i k) p", p=P)
                todo = [(V_ADA, 0, ab, 72), (V_NORM, 0, ng, 24)]
                for c0, n, w in ((V_W0, "rwkv_w0", 3), (V_A0, "rwkv_a0", 3), (V_KK, "rwkv_k_k", 3),
                                 (V_KA, "rwkv_k_a", 3), (V_LG, "rwkv_lnx_g", 3), (V_LB, "rwkv_lnx_b", 3),
                                 (V_QN, "mla_q_norm_g", 2), (V_KVN, "mla_kv_norm_g", 1)):
                    todo.append((c0 % 126, c0 // 126, a[n].rearrange("l (k p) -> (l k) p", p=P), w))
                rk = a["rwkv_r_k"].rearrange("l (k h) d -> (l k) (h d)", h=2)
                todo.append((V_RK, 0, rk, 3))
                for r0, half, src, w in todo:
                    sp.dma_start(vrows[r0:r0 + w, half, :], src[bass.ds(l * w, w), :])\
                        .then_inc(sem("rows_loaded"), 16)
                mu = a["rwkv_mu"]
                sp.dma_start(vrows[V_MU:V_MU + 11, 0, :],
                             mu[bass.ds(l, 1), 0:11 * P].rearrange("l (k p) -> (l k) p", p=P))\
                    .then_inc(sem("rows_loaded"), 16)
                sp.dma_start(vrows[V_MU + 11:V_MU + 12, 0, :], mu[bass.ds(l, 1), RW_COLS - P:RW_COLS])\
                    .then_inc(sem("rows_loaded"), 16)
                ffn_loads(l, 0)
                sp.wait_ge(*at("lora_done", 0, l))
                sp.dma_start(lora[0:64, :], a["rwkv_w2"].rearrange("l p n -> p l n")[:, bass.ds(l, 1), :])\
                    .then_inc(sem("small_loaded"), 16)
                sp.dma_start(lora[64:128, :], a["rwkv_a2"].rearrange("l p n -> p l n")[:, bass.ds(l, 1), :])\
                    .then_inc(sem("small_loaded"), 16)
                g2 = a["rwkv_g2"].rearrange("l p n -> p l n")
                sp.dma_start(lora_g[:, 0, :], g2[0:P, bass.ds(l, 1), :]).then_inc(sem("small_loaded"), 16)
                sp.dma_start(lora_g[96:128, 1, :], g2[P:LORA_G, bass.ds(l, 1), :])\
                    .then_inc(sem("small_loaded"), 16)
                uq = a["mla_w_uq"].rearrange("l (k p) n -> p (l k) n", p=P)
                sp.dma_start(w_uq[:, :, :], uq[:, bass.ds(l * 2, 2), :]).then_inc(sem("small_loaded"), 16)
                uqh = a["mla_w_uq"].rearrange("l (k p) (h n) -> p (l k) h n", p=P, h=HEADS)
                for k in range(2):
                    for half in range(2):
                        src = NOPE + 16 * (1 - half)
                        sp.dma_start(w_sw[:, k, :, 16 * half:16 * half + 16],
                                     uqh[:, bass.ds(l * 2 + k, 1), :, src:src + 16].rearrange("p k h n -> p (k h) n"))\
                            .then_inc(sem("small_loaded"), 16)
                sp.dma_start(w_ukv[:, :], a["mla_w_ukv"].rearrange("l p n -> p l n")[:, bass.ds(l, 1), :])\
                    .then_inc(sem("small_loaded"), 16)
                for s in range(ATT_IN, GATE_IN):
                    free(s, still, l)
                    kd = bass.ds(l * KD, KD)
                    inc = sem(f"raw_loaded{s % 4}")
                    if s == SLOT_V:
                        sp.dma_start(raw[:, s % 4, :].rearrange("p (k n) -> p k n", k=KD),
                                     wmix[:, kd, SBV:SBV + 256]).then_inc(inc, 16)
                    elif s == SLOT_KR:
                        sp.dma_start(halves(s, 96)[:, 0], wmix[:, kd, KR - 64:KR + 32]).then_inc(inc, 16)
                        sp.dma_start(halves(s, 96)[:, 1, :, 0:80], wmix[:, kd, KR - 48:KR + 32]).then_inc(inc, 16)
                        sp.dma_start(halves(s, 96)[:, 1, :, 80:96], wmix[:, kd, KR:KR + 16]).then_inc(inc, 16)
                    else:
                        for half in (1, 0):
                            c0 = IN_COLS[s][half]
                            sp.dma_start(halves(s)[:, half], wmix[:, kd, c0:c0 + P]).then_inc(inc, 16)
                    if s - ATT_IN in (1, 3, 5):
                        ada(24 + (s - ATT_IN) // 2, still, 0, l)
                for s, o in steps(sp, GATE_IN, 12, tail=4):
                    j = s - GATE_IN
                    free(s, o, l)
                    for half in range(2):
                        c0 = GATE0 + j * 256 + half * P
                        cols = bass.ds(o(4 * 256) + c0, P)
                        sp.dma_start(halves(s)[:, half], wmix[:, bass.ds(l * KD, KD), cols])\
                            .then_inc(sem(f"raw_loaded{s % 4}"), 16)
                    if j % 2 and j < 10:
                        ada(27 + j // 2, o, 2, l)
                for s in range(BRANCH, FFN2_IN):
                    free(s, still, l)
                    w, k0, per = (wbr, 2 * (s - BRANCH), 9) if s < MIX_OUT else (wmo, 2 * (s - MIX_OUT), KD)
                    n = slot_size(s) // D
                    sp.dma_start(rows(s, n), w[:, bass.ds(l * per + k0, n), :])\
                        .then_inc(sem(f"raw_loaded{s % 4}"), 16)
                ffn_loads(l, 1)
            for t in range(TT):
                sp.wait_ge(sem("out_ready"), t + 1)
                sp.dma_start(out_dram[0, t * P:(t + 1) * P, :], xo[:, t, :]).then_inc(sem("stored"), 16)
            sp.wait_ge(sem("stored"), 16 * TT)

        @block.scalar
        def _(act):
            def round_w(s, o, l):
                act.wait_ge(*loaded(s, o, l))
                act.wait_ge(*at("w_used", s - 1 + o(4), l))
                n = slot_size(s) // 2
                for h in range(2):
                    nc.scalar.activation(wh[:, s % 2, h * n:(h + 1) * n], raw[:, s % 4, h * n:(h + 1) * n],
                                         ACT.Copy).then_inc(*one("w_hi"))

            def norm_stats(l, n, inc=one):
                nc.scalar.activation(warm[:, :], one_b[:, :], ACT.Sqrt)
                for c in range(KD):
                    act.wait_ge(*at("x_ready", n * KD + c + 1, l))
                    nc.scalar.activation(scr[:, c, :], x[:, c, :], ACT.Square)\
                        .then_inc(*inc("sq_ready"))
                act.wait_ge(*at("sq_used", (n + 1) * KD, l))
                b = NORM_BANK[n]
                nc.scalar.activation(PS[:, b, T:2 * T], PS[:, b, 0:T], ACT.Sqrt, scale=1.0 / D, bias=epsb[:, 0:1])\
                    .then_inc(*inc("rt_ready"))

            def norm(l, n):
                for c in range(KD):
                    act.wait_ge(*at("t_ready", n * KD + c + 1, l))
                    sh = [0, 3, 6][n] * KD + c
                    nc.scalar.activation(hh[:, c, :], scr[:, c, :], ACT.Identity,
                                         bias=mod[:, sh:sh + 1]).then_inc(*one("hh_ready"))

            def ffn(l, f):
                s0, s1 = (FFN1_IN, FFN1_OUT) if f == 0 else (FFN2_IN, FFN2_OUT)
                for s, o in steps(act, s0, KF):
                    j = s - s0
                    round_w(s + 2, o, l)
                    act.wait_ge(*at("w_used", s + 1 + o(4), l))
                    act.wait_ge(*at("hf_ready", f * KF + j - 1 + o(4), l))
                    nc.scalar.activation(sil[:, j % 2, :], PS[:, j % 4, 0:T], ACT.Silu)\
                        .then_inc(*one("sil_ready"))
                for s, o in steps(act, s1, 11, peel=1, tail=2):
                    if s < s1 + 9 or (s == s1 + 9 and f == 0):
                        round_w(s + 2, o, l)

            act.sem_inc(sem("gate_ready"), BEFORE["gate_ready"])
            act.wait_ge(sem("zeroed"), 1)
            act.wait_ge(sem("cT_ready"), 1)
            nc.scalar.activation(cact[:, 0:KD], bank(6)[:, 0:KD], ACT.Silu)
            nc.scalar.activation(cact[:, KD:2 * KD], bank(6)[:, KD:2 * KD], ACT.Copy)\
                .then_inc(sem("cact_ready"), 1)
            for i in range(4):
                act.wait_ge(sem("x_tr"), i + 1)
                for t in range(2):
                    ins = nc.scalar.activation(x[:, 2 * i:2 * i + 2, t * P:(t + 1) * P],
                                               bank(i).rearrange("p (c t n) -> p c t n", c=2, t=2)[:, :, t], ACT.Copy)
            ins.then_inc(sem("x_ready"), KD)
            norm_stats(0, 0, inc=once)
            act.wait_ge(sem("ang_ready"), 1)
            r6 = slice(NOPE, NOPE + ROPE)
            nc.scalar.activation(ang[r6, 2, :], ang[r6, 0, :], ACT.Sin)
            nc.scalar.activation(ang[r6, 3, :], ang[r6, 0, :], ACT.Sin, scale=0.5).then_inc(sem("sin_ready"), 1)

            with act.Fori(0, DEPTH) as l:
                act.wait_ge(*at("vec_rows", 1, l))
                nc.scalar.activation(vec[:, 0:126], bank(0)[:, 0:126], ACT.Copy)
                nc.scalar.activation(vec[:, 126:N_VEC], bank(0)[:, P:P + 6], ACT.Copy)\
                    .then_inc(*one("vec_ready"))
                round_w(0, still, l)
                round_w(1, still, l)
                norm(l, 0)
                ffn(l, 0)
                norm_stats(l, 1)
                round_w(ATT_IN + 1, still, l)
                norm(l, 1)
                for s in range(ATT_IN, RW_IN):
                    round_w(s + 2, still, l)
                    i = s - ATT_IN
                    act.wait_ge(*at("w_used", s + 1, l))
                    b = bank(i)
                    if i < 3:
                        ins = nc.scalar.activation(qk[:, 2 * i:2 * i + 2, :].rearrange("p a b -> p (a b)"), b,
                                                   ACT.Copy)
                    elif s == SLOT_V:
                        ins = nc.scalar.activation(vs[:, :, 0:256], b.rearrange("p (t n) -> p t n", t=2), ACT.Copy)
                    elif i == 4:
                        nc.scalar.activation(vs[:, :, 256:384], b[:, 0:256].rearrange("p (t n) -> p t n", t=2),
                                             ACT.Copy)
                        ins = nc.scalar.activation(cqkv[:, 2, :], b[:, 256:512], ACT.Copy)
                    elif i == 5:
                        ins = nc.scalar.activation(cqkv[:, 0:2, :].rearrange("p a b -> p (a b)"), b, ACT.Copy)
                    else:
                        ins = nc.scalar.activation(krA[NOPE:96, :, :].rearrange("p a b -> p (a b)"),
                                                   b[NOPE:96, :], ACT.Copy)
                    ins.then_inc(*one("att_in"))

                def sb_scores(c):
                    act.wait_ge(*at("sb_scored", c + 1, l))
                    ps = PS[:, 2 * (c % 2):2 * (c % 2) + 2, 0:384]
                    if c >= 2:
                        act.wait_ge(*at("sb_summed", c - 1, l))
                    nc.scalar.activation(sbz[:, c % 2], ps, ACT.Copy, scale=SB_SCALE).then_inc(*one("sb_z"))
                    act.drain()
                    nc.scalar.activation(sbe[:, c % 2], sbz[:, c % 2], ACT.Abs)
                    act.drain()
                    nc.scalar.activation(sbe[:, c % 2], sbe[:, c % 2], ACT.Exp, scale=-1.0)
                    act.drain()
                    nc.scalar.activation(sbe[:, c % 2], sbe[:, c % 2], ACT.Ln, bias=one_b[:, 0:1])\
                        .then_inc(*one("sb_ln"))

                def sb_weights(c):
                    act.wait_ge(*at("sb_lw", c + 1, l))
                    nc.scalar.activation(sbe[:, c % 2], sbz[:, c % 2], ACT.Exp).then_inc(*one("sb_w"))

                def sb_out(c):
                    act.wait_ge(*at("sb_y", c + 1, l))
                    nc.scalar.activation(yh[:, 3 + c, :], PS[:, 4 + c, 0:T], ACT.Copy)\
                        .then_inc(*one("sb_yh"))

                sb_scores(0)
                sb_scores(1)
                sb_weights(0)
                sb_out(0)
                sb_weights(1)
                sb_scores(2)
                sb_out(1)
                sb_weights(2)
                sb_out(2)
                nc.scalar.activation(scr[:, 0:3, :], cqkv[:, :, :], ACT.Square).then_inc(*one("mla_sq"))
                act.wait_ge(*at("mla_sum", 1, l))
                nc.scalar.activation(hstat[:, 0, 0:2], PS[:, 3, 0:2], ACT.Sqrt, scale=1.0 / Q_LORA, bias=epsb[:, 0:1])
                nc.scalar.activation(hstat[:, 0, 2:4], PS[:, 3, 2:4], ACT.Sqrt, scale=1.0 / KV_LORA,
                                     bias=epsb[:, 0:1]).then_inc(*one("mla_rt"))
                for i in range(PAIRS):
                    act.wait_ge(*at("mla_k", i + 1, l))
                    nc.scalar.activation(kT[0:NOPE, 2 * i:2 * i + 2, :].rearrange("p a b -> p (a b)"),
                                         PS[0:NOPE, i, :], ACT.Copy)
                act.wait_ge(*at("mla_v", 1, l))
                for t in range(TT):
                    nc.scalar.activation(vm[:, t, :], PS[:, 6 + t, 0:BW], ACT.Copy).then_inc(*one("mla_kv_ready"))
                for i in range(PAIRS):
                    act.wait_ge(*at("mla_q", i + 1, l))
                    nc.scalar.activation(qT[0:NOPE, 2 * i:2 * i + 2, :].rearrange("p a b -> p (a b)"),
                                         PS[0:NOPE, 3 + (i % 2), :], ACT.Copy).then_inc(*one("mla_qn"))
                for r in range(2):
                    act.wait_ge(*at("mla_scored", r + 1, l))
                    nc.scalar.activation(mls[:, 3 * r:3 * r + 3, :], PS[:, 3 * r:3 * r + 3, 0:384], ACT.Copy,
                                         scale=MLA_SCALE).then_inc(*one("mla_sc"))
                for r in range(2):
                    act.wait_ge(*at("mla_sub", r + 1, l))
                    nc.scalar.activation(mls[:, 3 * r:3 * r + 3, :], mls[:, 3 * r:3 * r + 3, :], ACT.Exp)\
                        .then_inc(*one("mla_exp"))

                def mla_out(i):
                    act.wait_ge(*at("mla_y", i + 1, l))
                    nc.scalar.activation(yh[:, 6 + i, :], PS[:, 4 + i, 0:T], ACT.Copy).then_inc(*one("mla_yh"))

                for h in range(HEADS):
                    act.wait_ge(*at("mla_tr", h + 1, l))
                    nc.scalar.activation(mlp[:, h, :], PS[:, h % 4, 0:384], ACT.Copy).then_inc(*one("mla_p"))
                    if h in (3, 5):
                        mla_out(h // 2 - 1)
                mla_out(2)
                for i in range(6):
                    round_w(RW_IN + i + 2, still, l)
                    act.wait_ge(*at("w_used", RW_IN + i + 1, l))
                    if i == 0:
                        act.wait_ge(*at("pb_zero", 1, l))
                    nc.scalar.activation(pb[:, 2 * i:2 * i + 2, 1:T + 1],
                                         PS[:, i % 4, :].rearrange("p (a b) -> p a b", a=2), ACT.Copy)\
                        .then_inc(*one("pb_ready"))
                act.wait_ge(*at("shifted", 12, l))
                nc.scalar.activation(ex[0:64, 0, :], m[0:64, 9, :], ACT.Tanh)
                nc.scalar.activation(m[:, 10, :], m[:, 10, :], ACT.Sigmoid)
                nc.scalar.activation(m[96:128, 11, :], m[96:128, 11, :], ACT.Sigmoid).then_inc(*one("lora_in"))
                act.wait_ge(*at("lora_done", 1, l))
                for c in range(3):
                    nc.scalar.activation(lw[:, c, :], PS[:, 2 + c // 2, (c % 2) * T:(c % 2 + 1) * T], ACT.Sigmoid,
                                         bias=vec[:, V_W0 + c:V_W0 + c + 1])
                    nc.scalar.activation(av[:, c, :], PS[:, 4 + c // 2, (c % 2) * T:(c % 2 + 1) * T], ACT.Sigmoid,
                                         bias=vec[:, V_A0 + c:V_A0 + c + 1]).then_inc(*one("wa_ready"))
                nc.scalar.activation(g[:, 0:2, :].rearrange("p a b -> p (a b)"), PS[:, 6, :], ACT.Copy)
                nc.scalar.activation(g[:, 2, :], PS[:, 7, 0:T], ACT.Copy).then_inc(*one("g_ready"))
                act.wait_ge(*at("kk0", 1, l))
                nc.scalar.activation(ex[:, :, :], kk[:, :, :], ACT.Square).then_inc(*one("kk_sq"))
                act.wait_ge(*at("kk_max", 1, l))
                nc.scalar.activation(hstat[:, 0, :], hstat[:, 1, :], ACT.Sqrt).then_inc(*one("kk_rt"))
                act.wait_ge(*at("cum_ready", 1, l))
                act.wait_ge(*at("kk_stat", 1, l))
                nc.scalar.activation(ex[:, :, :], cum[:, :, :], ACT.Exp, scale=-1.0).then_inc(*one("e_neg"))
                act.drain()
                nc.scalar.activation(cum[:, :, :], cum[:, :, :], ACT.Exp).then_inc(*one("e_cum"))
                nc.scalar.activation(lw[:, :, :], lw[:, :, :], ACT.Exp).then_inc(*one("e_prev"))
                for tt in range(TT):
                    act.wait_ge(*at("tok_done", tt + 1, l))
                    for i in (0, 1):
                        nc.scalar.activation(tok[:, i, :], PS[:, i, 0:BW], ACT.Copy).then_inc(*one("tok_act"))
                    for b in range(5):
                        for par in range(2):
                            act.wait_ge(*at("z_done", 2 * (5 * tt + b) + par + 1, l))
                            nc.scalar.activation(Z[:, par, :, :].rearrange("p c n -> p (c n)"), PS[:, par, 0:384],
                                                 ACT.Copy).then_inc(*one("z_ready"))
                    act.wait_ge(*at("wt_done", tt + 1, l))
                    nc.scalar.activation(wT[:, :, :].rearrange("p a b -> p (a b)"), PS[:, 4, 0:BW], ACT.Copy)\
                        .then_inc(*one("wt_ready"))
                    act.wait_ge(*at("y_done", tt + 1, l))
                    nc.scalar.activation(ya[:, :, tt * P:(tt + 1) * P],
                                         PS[:, 6, 0:BW].rearrange("p (a b) -> p a b", a=3), ACT.Copy)\
                        .then_inc(*one("ya_ready"))
                act.wait_ge(*at("gn_sub", 1, l))
                nc.scalar.activation(ex[:, :, :], ya[:, :, :], ACT.Square).then_inc(*one("gn_sq"))
                act.wait_ge(*at("gn_stat", 1, l))
                nc.scalar.activation(hstat[:, 0, :], PS[:, 3, 0:12], ACT.Sqrt, scale=1.0 / HD, bias=gneps[:, 0:1])\
                    .then_inc(*one("gn_rt"))
                act.wait_ge(*at("ya_final", 1, l))
                nc.scalar.activation(yh[:, 0:3, :], ya[:, :, :], ACT.Copy).then_inc(*one("ya_hi"))
                for s, o in steps(act, GATE_IN, 12, tail=4):
                    j = s - GATE_IN
                    round_w(s + 2, o, l)
                    act.wait_ge(*at("w_used", s + 1 + o(4), l))
                    if j < 4:
                        act.wait_ge(*at("ya_lo", 1, l))
                    nc.scalar.activation(gates[:, bass.ds(o(8) + 2 * j, 2), :], PS[:, j % 4, :].rearrange("p (a b) -> p a b", a=2), ACT.Sigmoid)\
                        .then_inc(*one("gate_ready"))
                for s in range(BRANCH, FFN2_IN):
                    if s + 2 < FFN2_IN + 1:
                        round_w(s + 2, still, l)
                    if s == MIX_OUT - 1:
                        for i in range(4):
                            act.wait_ge(*at("merged", i + 1, l))
                            nc.scalar.activation(hh[:, 2 * i:2 * i + 2, :], mg[:, 2 * i:2 * i + 2, :], ACT.Copy)\
                                .then_inc(*one("mg_hi"))
                norm_stats(l, 2)
                round_w(FFN2_IN + 1, still, l)
                norm(l, 2)
                ffn(l, 1)
                norm_stats(l, 3)
            for t in range(TT):
                act.wait_ge(sem("out_tr"), t + 1)
                nc.scalar.activation(xo[:, t, :].rearrange("p (a b) -> p a b", a=2), PS[:, 2 * t + 4:2 * t + 6, :],
                                     ACT.Copy).then_inc(sem("out_ready"), 1)

        @block.vector
        def _(dve):
            V = nc.vector

            def split(s, o, l):
                n = slot_size(s) // 2
                for h in range(2):
                    dve.wait_ge(*at("w_hi", 2 * s + h + 1 + o(8), l))
                    V.tensor_tensor(wl[:, s % 2, h * n:(h + 1) * n], raw[:, s % 4, h * n:(h + 1) * n],
                                    wh[:, s % 2, h * n:(h + 1) * n].bitcast(F32), ALU.subtract)\
                        .then_inc(*one("w_split"))

            def norm_root(l, n):
                rb = PS[:, NORM_BANK[n], T:2 * T]
                dve.wait_ge(*at("rt_ready", n + 1, l))
                V.reciprocal(rb, rb)
                dve.drain()

            def norm(l, n):
                rb = PS[:, NORM_BANK[n], T:2 * T]

                def lo(c):
                    dve.wait_ge(*at("hh_ready", n * KD + c + 1, l))
                    sh = [0, 3, 6][n] * KD + c
                    V.scalar_tensor_tensor(hl[:, c, :], scr[:, c, :], mod[:, sh:sh + 1],
                                           hh[:, c, :].bitcast(F32), ALU.add, ALU.subtract)\
                        .then_inc(*one("h_ready"))

                for c in range(KD + 2):
                    if c < KD:
                        V.scalar_tensor_tensor(scr[:, c, :], x[:, c, :], gsc[:, n, c:c + 1], rb,
                                               ALU.mult, ALU.mult).then_inc(*one("t_ready"))
                    if c >= 2:
                        lo(c - 2)

            def evac_out(l, n, gate):
                for c in range(KD):
                    if c % 2 == 0:
                        dve.wait_ge(*(at("out_done", 3 * n + c // 2 + 1, l) if c < KD - 2 else
                                      at("w_used", (FFN1_OUT + 11, MIX_OUT + 4, FFN2_OUT + 11)[n], l)))
                    b = OUT_BANKS[n][c // 2]
                    V.scalar_tensor_tensor(x[:, c, :], PS[:, b, (c % 2) * T:(c % 2 + 1) * T], gate[:, c:c + 1],
                                           x[:, c, :], ALU.mult, ALU.add).then_inc(*one("x_ready"))

            def ffn(l, f):
                s0, s1 = (FFN1_IN, FFN1_OUT) if f == 0 else (FFN2_IN, FFN2_OUT)
                for s, o in steps(dve, s0, KF, *((0, 0), (4, 2))[f]):
                    j = s - s0
                    split(s + 2, o, l)
                    dve.wait_ge(*at("sil_ready", f * KF + j + 1 + o(4), l))
                    dve.wait_ge(*at("hid_ready", f * KF + j - 1 + o(4), l))
                    V.tensor_tensor(hf[:, j % 2, :], PS[:, j % 4, T:2 * T], sil[:, j % 2, :], ALU.mult)\
                        .then_inc(*one("hf_ready"))
                    if f == 0:
                        ada(8 + j // 2, o, 2, l, half=j % 2)
                    elif 4 <= j < 20:
                        ada(32 + (j - 4) // 2, o, 2, l, half=j % 2)
                for s, o in steps(dve, s1, 11, peel=1, tail=2):
                    j = s - s1
                    if j < 9 or (j == 9 and f == 0):
                        split(s + 2, o, l)
                    if j == 10:
                        continue
                    if 1 <= j <= (10, 8)[f]:
                        ada((19, 40)[f] + (j - 1) // 2, o, 2, l, half=(j - 1) % 2)

            def ada(n, o, r, l, half=None, inc=one):
                q = n % 2
                dve.drain()
                if not half:
                    dve.wait_ge(sem(f"ada_loaded{q}"), l * (18 * 16) + 16 * (n // 2 + 1) + o(8 * r))
                w4 = ada_w[:, q, :].rearrange("p (k n) -> p k n", k=4)
                if q == 0 and n and not half:
                    dve.wait_ge(*at("acc_used", n // 2 + o(r // 2), l))
                for k in range(4) if half is None else (2 * half, 2 * half + 1):
                    cc = cact[:, 4 * q + k:4 * q + k + 1]
                    if q == 0 and k == 0:
                        V.tensor_scalar(acc[:, :], w4[:, 0, :], cc, None, ALU.mult)
                    else:
                        if k % 4 and not (half and k == 2):
                            dve.drain()
                        last = V.scalar_tensor_tensor(acc[:, :], w4[:, k, :], cc, acc[:, :], ALU.mult, ALU.add)
                if half != 0:
                    last.then_inc(*inc("ada_used"))

            def mod_part(l, lo, hi, groups):
                dve.wait_ge(*at("acc_used", groups, l))
                V.tensor_tensor(mod[:, lo:hi], PS[:, 7, lo:hi], vec[:, V_ADA + lo:V_ADA + hi], ALU.add)
                dve.drain()

            def scales(n):
                sc = mod[:, (3 * n + 1) * KD:(3 * n + 2) * KD]
                return V.scalar_tensor_tensor(gsc[:, n, :], sc, 1.0, vec[:, V_NORM + n * KD:V_NORM + (n + 1) * KD],
                                       ALU.add, ALU.mult)

            def half_gate(n, w):
                return V.tensor_scalar(hgate[:, n, :], mod[:, (3 * n + 2) * KD:(3 * n + 3) * KD], w, None, ALU.mult)

            for name in ("w_split", "hf_ready"):
                dve.sem_inc(sem(name), BEFORE[name])
            V.memset(epsb[:, :], EPS)
            V.memset(gneps[:, :], GN_EPS)
            V.memset(one_b[:, :], 1.0)
            V.memset(vrows[:, :, :], 0.0).then_inc(sem("zeroed"), 1)
            dve.wait_ge(sem("cact_ready"), 1)
            ada(0, still, 0, 0, inc=once)
            ada(1, still, 0, 0, inc=once)
            for n in range(2, 8):
                ada(n, still, 0, 0, inc=once)

            with dve.Fori(0, DEPTH) as l:
                dve.wait_ge(*at("vec_ready", 1, l))
                V.tensor_scalar(omka[:, :], vec[:, V_KA:V_KA + 3], -1.0, 1.0, ALU.mult, ALU.add)
                norm_root(l, 0)
                mod_part(l, 0, 16, 4)
                scales(0)
                dve.drain()
                split(0, still, l)
                norm(l, 0)
                split(1, still, l)
                ffn(l, 0)
                mod_part(l, 16, 40, 10)
                scales(1)
                half_gate(0, 0.5)
                dve.drain()
                evac_out(l, 0, hgate[:, 0, :])
                norm_root(l, 1)
                norm(l, 1)
                split(ATT_IN + 1, still, l)
                ada(23, still, 0, l, half=1)
                for s in range(ATT_IN, RW_IN):
                    split(s + 2, still, l)
                    if s - ATT_IN < 6:
                        ada(24 + (s - ATT_IN) // 2, still, 0, l, half=(s - ATT_IN) % 2)
                mod_part(l, 40, 52, 13)
                half_gate(1, 1.0)
                mask2 = const(C_SBM).unsqueeze(1).unsqueeze(1).broadcast_to([P, 2, 2, P])

                def diag(t):
                    return t.rearrange("p h (b n) -> p h b n", b=3)[:, :, 0:3:2, :]

                def sb_soft(c):
                    dve.wait_ge(*at("sb_z", c + 1, l))
                    if c >= 2:
                        dve.wait_ge(*at("sb_summed", c - 1, l))
                    V.tensor_scalar(sbs[:, c % 2], sbz[:, c % 2], 0.0, None, ALU.max)
                    dve.drain()
                    dve.wait_ge(*at("sb_ln", c + 1, l))
                    V.tensor_tensor(sbs[:, c % 2], sbs[:, c % 2], sbe[:, c % 2], ALU.add)
                    dve.drain()
                    V.tensor_tensor(diag(sbs[:, c % 2]), diag(sbs[:, c % 2]), mask2, ALU.mult)\
                        .then_inc(*one("sb_sp"))

                def sb_lw(c):
                    dve.wait_ge(*at("sb_summed", c + 1, l))
                    dve.wait_ge(*at("sb_min", c + 1, l))
                    V.tensor_tensor(sbz[:, c % 2], sbz[:, c % 2], PS[:, 2 * (c % 2):2 * (c % 2) + 2, 0:384],
                                    ALU.subtract).then_inc(*one("sb_lw"))

                def sb_lo(c):
                    dve.wait_ge(*at("sb_yh", c + 1, l))
                    V.tensor_tensor(yl[:, 3 + c, :], PS[:, 4 + c, 0:T], yh[:, 3 + c, :].bitcast(F32), ALU.subtract)\
                        .then_inc(*one("sb_yl"))

                sb_soft(0)
                sb_soft(1)
                sb_lw(0)
                sb_lw(1)
                sb_lo(0)
                sb_soft(2)
                sb_lo(1)
                sb_lw(2)
                sb_lo(2)
                dve.wait_ge(*at("mla_rt", 1, l))
                V.reciprocal(hstat[:, 1, 0:4], hstat[:, 0, 0:4]).then_inc(*one("mla_rinv"))
                dve.wait_ge(*at("mla_rb", 1, l))
                for c in range(3):
                    rb = PS[:, 4 if c < 2 else 5, 0:T]
                    gcol = V_QN + c if c < 2 else V_KVN
                    V.scalar_tensor_tensor(cqkv[:, c, :], cqkv[:, c, :], vec[:, gcol:gcol + 1], rb,
                                           ALU.mult, ALU.mult).then_inc(*one("mla_lat"))
                R = slice(NOPE, 96)
                dve.wait_ge(sem("rope_ready"), 1)
                V.tensor_tensor(rA[R, 0:T], krA[R, 0, :], cosT[R, :], ALU.mult)
                V.tensor_tensor(rB[R, 0:T], krA[R, 1, :], sinT[R, :], ALU.mult)
                dve.drain()
                V.tensor_tensor(kT[R, :, :], rA[R, 0:T].unsqueeze(1).broadcast_to([32, HEADS, T]),
                                rB[R, 0:T].unsqueeze(1).broadcast_to([32, HEADS, T]), ALU.add)
                cos2 = cosT[R, :].unsqueeze(1).broadcast_to([32, 2, T])
                sin2 = sinT[R, :].unsqueeze(1).broadcast_to([32, 2, T])
                for i in range(PAIRS):
                    dve.drain()
                    dve.wait_ge(*at("mla_q", i + 1, l))
                    V.tensor_tensor(rA[R, :].rearrange("p (a b) -> p a b", a=2),
                                    PS[R, 3 + (i % 2), :].rearrange("p (a b) -> p a b", a=2), cos2, ALU.mult)
                    V.tensor_tensor(rB[R, :].rearrange("p (a b) -> p a b", a=2),
                                    PS[R, 5, :].rearrange("p (a b) -> p a b", a=2),
                                    sin2, ALU.mult)
                    dve.drain()
                    V.tensor_tensor(qT[R, 2 * i:2 * i + 2, :].rearrange("p a b -> p (a b)"), rA[R, :], rB[R, :],
                                    ALU.add).then_inc(*one("mla_qr"))
                caus6 = const(C_CAUS).unsqueeze(1).unsqueeze(1).broadcast_to([P, 3, 2, P])

                def by_query(r, op, col):
                    for k, (lo_, n_) in enumerate(((0, P), (P, 256))):
                        v = mls[:, 3 * r:3 * r + 3, lo_:lo_ + n_]
                        c0 = col + 3 * k
                        last = V.tensor_tensor(v, v, mla_stat[:, r, c0:c0 + 3].unsqueeze(2).broadcast_to([P, 3, n_]), op)
                    return last

                for r in range(2):
                    dve.wait_ge(*at("mla_sc", r + 1, l))
                    m3 = mls[:, 3 * r:3 * r + 3, :]
                    V.tensor_tensor(diag(m3), diag(m3), caus6, ALU.add)
                    dve.drain()
                    V.tensor_reduce(mla_stat[:, r, 0:3], m3[:, :, 0:P], AX_X, ALU.max)
                    V.tensor_reduce(mla_stat[:, r, 3:6], m3[:, :, P:384], AX_X, ALU.max)
                    dve.drain()
                    by_query(r, ALU.subtract, 0).then_inc(*one("mla_sub"))
                for r in range(2):
                    dve.wait_ge(*at("mla_exp", r + 1, l))
                    m3 = mls[:, 3 * r:3 * r + 3, :]
                    V.tensor_reduce(mla_stat[:, r, 6:9], m3[:, :, 0:P], AX_X, ALU.add)
                    V.tensor_reduce(mla_stat[:, r, 9:12], m3[:, :, P:384], AX_X, ALU.add)
                    dve.drain()
                    V.reciprocal(mla_stat[:, r, 0:6], mla_stat[:, r, 6:12])
                    dve.drain()
                    by_query(r, ALU.mult, 0).then_inc(*one("mla_pr"))
                for i in range(PAIRS):
                    dve.wait_ge(*at("mla_yh", i + 1, l))
                    V.tensor_tensor(yl[:, 6 + i, :], PS[:, 4 + i, 0:T], yh[:, 6 + i, :].bitcast(F32), ALU.subtract)\
                        .then_inc(*one("mla_yl"))
                for i in range(6):
                    split(RW_IN + i + 2, still, l)
                    for c in (2 * i, 2 * i + 1):
                        dve.wait_ge(*at("shift_d", c + 1, l))
                        V.scalar_tensor_tensor(m[:, c, :], m[:, c, :], vec[:, V_MU + c:V_MU + c + 1],
                                               pb[:, c, 1:T + 1], ALU.mult, ALU.add).then_inc(*one("shifted"))
                dve.wait_ge(*at("wa_ready", 3, l))
                V.tensor_scalar(lw[:, :, :], lw[:, :, :], -float(np.exp(-0.5)), None, ALU.mult)
                dve.drain()
                for c in range(3):
                    V.tensor_tensor_scan(cum[:, c, :], reset, lw[:, c, :], 0.0, ALU.mult, ALU.add)
                dve.drain()
                V.tensor_tensor(lw[:, :, :], cum[:, :, :], lw[:, :, :], ALU.subtract).then_inc(*one("cum_ready"))
                dve.wait_ge(*at("kk_stat", 1, l))
                V.tensor_scalar(hstat[:, 1, :], PS[:, 3, 0:12], 1e-24, None, ALU.max).then_inc(*one("kk_max"))
                for c in range(3):
                    V.tensor_scalar(bon[:, c, :], av[:, c, :], vec[:, V_KA + c:V_KA + c + 1], omka[:, c:c + 1],
                                    ALU.mult, ALU.add)
                dve.drain()
                V.tensor_tensor(kp, kp, bon[:, :, :], ALU.mult)
                dve.drain()
                for c in range(3):
                    last = V.scalar_tensor_tensor(bon[:, c, :], rr[:, c, :], vec[:, V_RK + c:V_RK + c + 1], kp[:, c, :],
                                                  ALU.mult, ALU.mult)
                last.then_inc(*one("bon_in"))
                dve.wait_ge(*at("kk_rt", 1, l))
                V.reciprocal(hstat[:, 1, :], hstat[:, 0, :]).then_inc(*one("kk_rinv"))
                dve.wait_ge(*at("kk_rb", 1, l))
                V.tensor_tensor(kk[:, 0:2, :], kk[:, 0:2, :], PS[:, 4, :].rearrange("p (a b) -> p a b", a=2), ALU.mult)
                V.tensor_tensor(kk[:, 2, :], kk[:, 2, :], PS[:, 5, 0:T], ALU.mult)
                dve.drain()
                V.tensor_tensor(av[:, :, :], kk[:, :, :], av[:, :, :], ALU.mult)
                dve.wait_ge(*at("bon_done", 1, l))
                V.tensor_tensor(bon[:, 0:2, :], PS[:, 6, :].rearrange("p (a b) -> p a b", a=2), vv[:, 0:2, :], ALU.mult)
                V.tensor_tensor(bon[:, 2, :], PS[:, 7, 0:T], vv[:, 2, :], ALU.mult)
                dve.drain()
                dve.wait_ge(*at("e_neg", 1, l))
                V.tensor_tensor(av[:, :, :], av[:, :, :], ex[:, :, :], ALU.mult)
                V.tensor_tensor(kp, kp, ex[:, :, :], ALU.mult)
                dve.wait_ge(*at("e_cum", 1, l))
                V.tensor_tensor(rr, rr, cum[:, :, :], ALU.mult)
                dve.wait_ge(*at("e_prev", 1, l))
                V.scalar_tensor_tensor(kk[:, :, :], kk[:, :, :], -1.0, lw[:, :, :], ALU.mult, ALU.mult)\
                    .then_inc(*one("tilde"))
                V.memset(S[:, :, :], 0.0).then_inc(*one("S_ready"))

                def six_mask(n):
                    return const(n).unsqueeze(1).unsqueeze(1).broadcast_to([P, 2, 3, P])

                def two(b):
                    return PS[:, b:b + 2, 0:384].rearrange("p a (c n) -> p a c n", c=3)

                for tt in range(TT):
                    dve.wait_ge(*at("tok_done", tt + 1, l))
                    for i in (2, 3):
                        last = V.tensor_copy(tok[:, i, :], PS[:, i, 0:BW])
                    last.then_inc(*one("tok_dve"))
                    dve.wait_ge(*at("ab_done", 2 * tt + 1, l))
                    V.tensor_tensor(AT[:, :, :, :], two(4), six_mask(C_UP), ALU.mult).then_inc(*one("at_ready"))
                    dve.wait_ge(*at("ab_done", 2 * tt + 2, l))
                    V.tensor_tensor(Tm[:, :, :, :], two(6), six_mask(C_LO1), ALU.mult)
                    dve.drain()
                    V.tensor_tensor(Tm[:, :, :, :], Tm[:, :, :, :], six_mask(C_ID), ALU.add)
                    V.tensor_tensor(TTm[:, :, :, :], AT[:, :, :, :], six_mask(C_UP1), ALU.mult)
                    dve.drain()
                    V.tensor_tensor(TTm[:, :, :, :], TTm[:, :, :, :], six_mask(C_ID), ALU.add).then_inc(*one("T_ready"))
                    for i, (dst, msk) in enumerate(((Aak, C_UP), (Arb, C_UPI), (Ark, C_UPI))):
                        dve.wait_ge(*at("ak_done", 3 * tt + i + 1, l))
                        V.tensor_tensor(dst[:, :, :, :], two((4, 6, 4)[i]), six_mask(msk), ALU.mult)\
                            .then_inc(*one("ak_ready"))
                    for b in range(5):
                        for par in range(2):
                            dve.wait_ge(*at("tz_done", 2 * (5 * tt + b) + par + 1, l))
                            tm, ttm = (v[:, par, :, :].rearrange("p c n -> p (c n)") for v in (Tm, TTm))
                            if b < 4:
                                V.tensor_tensor(tm, tm, PS[:, 2 + par, 0:384], ALU.add)
                            V.tensor_tensor(ttm, ttm, PS[:, 4 + par, 0:384], ALU.add).then_inc(*one("T_ready"))
                    dve.wait_ge(*at("g_done", tt + 1, l))
                    V.tensor_copy(Gm, PS[:, 0, 0:BW]).then_inc(*one("G_ready"))
                    dve.wait_ge(*at("u0_done", tt + 1, l))
                    V.tensor_copy(u0[:, :], PS[:, 1, 0:BW]).then_inc(*one("u0_ready"))
                    for q in (2 * tt, 2 * tt + 1):
                        rows = slice((q % 2) * 64, (q % 2) * 64 + 64)
                        dve.drain()
                        dve.wait_ge(*at("u_done", q + 1, l))
                        V.tensor_tensor(u_[rows, :], PS[rows, 5, 0:BW], u0[rows, :], ALU.add).then_inc(*one("u_ready"))
                        dve.wait_ge(*at("s_done", q + 1, l))
                        V.tensor_tensor(S[:, :, :].rearrange("p a b -> p (a b)"),
                                        S[:, :, :].rearrange("p a b -> p (a b)"), PS[:, 3, 0:BW], ALU.add)
                        dve.drain()
                        dve.wait_ge(*at("pcm_ready", q + 1, l))
                        V.tensor_tensor(S[:, :, :], S[:, :, :], pcm[:, :, :], ALU.mult).then_inc(*one("S_ready"))
                dve.wait_ge(*at("gn_mean", 1, l))
                V.scalar_tensor_tensor(ya[:, 0:2, :], PS[:, 0, :].rearrange("p (a b) -> p a b", a=2), -1.0 / HD,
                                       ya[:, 0:2, :], ALU.mult, ALU.add)
                V.scalar_tensor_tensor(ya[:, 2, :], PS[:, 1, 0:T], -1.0 / HD, ya[:, 2, :], ALU.mult, ALU.add)\
                    .then_inc(*one("gn_sub"))
                dve.wait_ge(*at("gn_rt", 1, l))
                V.reciprocal(hstat[:, 1, :], hstat[:, 0, :]).then_inc(*one("gn_rinv"))
                dve.wait_ge(*at("gn_rb", 1, l))
                for c in range(3):
                    V.scalar_tensor_tensor(ya[:, c, :], ya[:, c, :], vec[:, V_LG + c:V_LG + c + 1],
                                           PS[:, 4 + c // 2, (c % 2) * T:(c % 2 + 1) * T], ALU.mult, ALU.mult)
                dve.drain()
                for c in range(3):
                    V.scalar_tensor_tensor(ya[:, c, :], ya[:, c, :], vec[:, V_LB + c:V_LB + c + 1], bon[:, c, :],
                                           ALU.add, ALU.add)
                dve.drain()
                V.tensor_tensor(ya[:, :, :], ya[:, :, :], g[:, :, :], ALU.mult).then_inc(*one("ya_final"))
                dve.wait_ge(*at("ya_hi", 1, l))
                V.tensor_tensor(yl[:, 0:3, :], ya[:, :, :], yh[:, 0:3, :].bitcast(F32), ALU.subtract)\
                    .then_inc(*one("ya_lo"))
                for s, o in steps(dve, GATE_IN, 12, tail=4):
                    j = s - GATE_IN
                    split(s + 2, o, l)
                    if j < 10:
                        ada(27 + j // 2, o, 2, l, half=j % 2)
                mod_part(l, 52, 64, 16)
                scales(2).then_inc(*one("mod_done"))
                dve.wait_ge(*at("gate_ready", 12, l))

                def merge(n, i):
                    dve.wait_ge(*(at("br_done", (0, 4, 7)[n] + i + 1, l) if n == 0 or i < 3 else
                                  at("w_used", BRANCH + (3, 5)[n - 1], l)))
                    ps = PS[:, BR_BANKS[n] + i, :].rearrange("p (a b) -> p a b", a=2)
                    gt = gates[:, n * KD + 2 * i:n * KD + 2 * i + 2, :]
                    if n == 0:
                        V.tensor_tensor(mg[:, 2 * i:2 * i + 2, :], ps, gt, ALU.mult).then_inc(*one("br_used"))
                        return
                    t = mt[:, 2 * (i % 2):2 * (i % 2) + 2, :]
                    V.tensor_tensor(t, ps, gt, ALU.mult).then_inc(*one("br_used"))
                    dve.drain()
                    ins = V.tensor_tensor(mg[:, 2 * i:2 * i + 2, :], mg[:, 2 * i:2 * i + 2, :], t, ALU.add)
                    if n == 2:
                        ins.then_inc(*one("merged"))

                def merged_lo(i):
                    dve.wait_ge(*at("mg_hi", i + 1, l))
                    V.tensor_tensor(hl[:, 2 * i:2 * i + 2, :], mg[:, 2 * i:2 * i + 2, :],
                                    hh[:, 2 * i:2 * i + 2, :].bitcast(F32), ALU.subtract).then_inc(*one("mg_lo"))

                split(BRANCH + 2, still, l)
                for i in range(4):
                    merge(0, i)
                split(BRANCH + 3, still, l)
                split(BRANCH + 4, still, l)
                for i in range(4):
                    merge(1, i)
                split(MIX_OUT, still, l)
                for i in range(4):
                    merge(2, i)
                    if i:
                        merged_lo(i - 1)
                    if i == 1:
                        split(MIX_OUT + 1, still, l)
                merged_lo(3)
                for s in range(MIX_OUT + 2, FFN2_IN + 1):
                    split(s, still, l)
                evac_out(l, 1, hgate[:, 1, :])
                norm_root(l, 2)
                norm(l, 2)
                split(FFN2_IN + 1, still, l)
                ffn(l, 1)
                mod_part(l, 64, 72, 22)
                half_gate(2, 0.5)
                dve.drain()
                evac_out(l, 2, hgate[:, 2, :])
            norm_root(DEPTH, 0)
            for c in range(KD):
                V.scalar_tensor_tensor(x[:, c, :], x[:, c, :], cact[:, KD + c:KD + c + 1], PS[:, 3, T:2 * T],
                                       ALU.mult, ALU.mult).then_inc(sem("y_ready"), 1)

        @block.gpsimd
        def _(pool):
            G = nc.gpsimd

            def ffn(l, f):
                s0 = FFN1_IN if f == 0 else FFN2_IN
                for s, o in steps(pool, s0, KF):
                    j = s - s0
                    pool.wait_ge(*at("hf_ready", f * KF + j + 1 + o(4), l))
                    dh = hidh[:, bass.ds(o(4) + j, 1), :].rearrange("p a b -> p (a b)")
                    dl = hidl[:, bass.ds(o(4) + j, 1), :].rearrange("p a b -> p (a b)")
                    pool.sem_inc(sem("pool_on"), 1)
                    G.tensor_copy(dh, hf[:, j % 2, :])
                    pool.drain()
                    G.tensor_tensor(dl, hf[:, j % 2, :], dh.bitcast(F32), ALU.subtract).then_inc(*one("hid_ready"))

            pool.sem_inc(sem("hid_ready"), BEFORE["hid_ready"])
            r6 = slice(NOPE, NOPE + ROPE)
            rc = C_ROPE * P
            pool.wait_ge(sem("pos_loaded"), 16)
            pool.wait_ge(sem("cst_loaded"), 16)
            G.tensor_copy(ang[r6, 1, :], posi[r6, :])
            pool.drain()
            G.tensor_scalar(ang[r6, 0, :], ang[r6, 1, :], cst[r6, rc:rc + 1], None, ALU.mult)
            pool.drain()
            magic = 1.5 * 2.0 ** 23
            G.tensor_scalar(ang[r6, 1, :], ang[r6, 0, :], 1.0 / (2 * np.pi), magic, ALU.mult, ALU.add)
            pool.drain()
            G.tensor_scalar(ang[r6, 1, :], ang[r6, 1, :], magic, None, ALU.subtract)
            c1 = 6.28125
            c2 = 0.0019350051879882812
            c3 = 2 * np.pi - c1 - c2
            for cc in (c1, c2, c3):
                pool.drain()
                G.tensor_scalar(ang[r6, 2, :], ang[r6, 1, :], cc, None, ALU.mult)
                pool.drain()
                G.tensor_tensor(ang[r6, 0, :], ang[r6, 0, :], ang[r6, 2, :], ALU.subtract)
            pool.drain()
            G.tensor_scalar(ang[r6, 0, :], ang[r6, 0, :], 3.1415925, -3.1415925, ALU.min, ALU.max)\
                .then_inc(sem("ang_ready"), 1)
            pool.wait_ge(sem("sin_ready"), 1)
            G.tensor_scalar(sinT[r6, :], ang[r6, 2, :], cst[r6, rc + 1:rc + 2], None, ALU.mult)
            G.tensor_tensor(ang[r6, 1, :], ang[r6, 3, :], ang[r6, 3, :], ALU.mult)
            pool.drain()
            G.tensor_scalar(cosT[r6, :], ang[r6, 1, :], -2.0, 1.0, ALU.mult, ALU.add).then_inc(sem("rope_ready"), 1)
            pool.drain()
            with pool.Fori(0, DEPTH) as l:
                ffn(l, 0)
                pool.wait_ge(*at("att_in", 7, l))
                mn = const(C_MIN).unsqueeze(1).unsqueeze(1).broadcast_to([P, 2, 2, P])
                for c in range(PAIRS):
                    pool.wait_ge(*at("sb_sp", c + 1, l))
                    z = sbz[:, c % 2].rearrange("p h (b n) -> p h b n", b=3)[:, :, 0:3:2, :]
                    G.tensor_tensor(z, z, mn, ALU.add).then_inc(*one("sb_min"))
                pool.wait_ge(*at("mla_yl", 3, l))
                pool.sem_inc(sem("pool_on"), 1)
                G.memset(pb[:, :, 0:1], 0.0).then_inc(*one("pb_zero"))
                for i in range(6):
                    pool.wait_ge(*at("pb_ready", i + 1, l))
                    for c in (2 * i, 2 * i + 1):
                        G.tensor_tensor(m[:, c, :], pb[:, c, 0:T], pb[:, c, 1:T + 1], ALU.subtract)\
                            .then_inc(*one("shift_d"))
                pool.wait_ge(*at("shifted", 12, l))
                pool.sem_inc(sem("pool_on"), 1)
                for c in range(3):
                    ins = G.tensor_scalar(kk[:, c, :], kp[:, c, :], vec[:, V_KK + c:V_KK + c + 1], None, ALU.mult)
                ins.then_inc(*one("kk0"))
                pool.wait_ge(*at("e_cum", 1, l))
                for tt in range(TT):
                    pool.wait_ge(*at("at_ready", tt + 1, l))
                    for b in range(5):
                        if b:
                            pool.wait_ge(*at("z_done", 2 * (5 * tt + b), l))
                        G.tensor_tensor(X[:, :, :, :], AT[:, :, :, :],
                                        const(LEVELS[b]).unsqueeze(1).unsqueeze(1).broadcast_to([P, 2, 3, P]),
                                        ALU.mult).then_inc(*one("X_ready"))
                    for q in (2 * tt, 2 * tt + 1):
                        if q:
                            pool.wait_ge(*at("S_ready", q + 1, l))
                        G.tensor_tensor(pcm[:, :, :],
                                        const(C_BLK).unsqueeze(1).broadcast_to([P, 3, P]),
                                        cum[:, :, 64 * q + 63:64 * q + 64].broadcast_to([P, 3, P]), ALU.mult)\
                            .then_inc(*one("pcm_ready"))
                ffn(l, 1)

        @block.tensor
        def _(pe):
            M = nc.tensor.matmul

            def mm3(out, wsl, rhs_h, rhs_l, start, stop):
                M(out, wh[(slice(None),) + wsl], rhs_h, start=start, stop=False, skip_group_check=True)
                M(out, wh[(slice(None),) + wsl], rhs_l, start=False, stop=False, skip_group_check=True)
                return M(out, wl[(slice(None),) + wsl], rhs_h, start=False, stop=stop, skip_group_check=True)

            def first_slot(s, b, h0, l):
                split_ready(s, 1, still, l)
                for k in range(KD):
                    pe.wait_ge(*at("h_ready", h0 + k + 1, l))
                    for half in range(2):
                        w0 = (half * KD + k) * P
                        ins = mm3(PS[:, b, half * T:(half + 1) * T], (s % 2, slice(w0, w0 + P)), hh[:, k, :],
                                  hl[:, k, :], k == 0 and half == 0, k == KD - 1)
                return ins

            def in_tile(s, half, b, col, n=P):
                for k in range(KD):
                    w0 = (half * KD + k) * n
                    last = mm3(PS[0:n, b, col:col + T], (s % 2, slice(w0, w0 + n)), hh[:, k, :], hl[:, k, :],
                               k == 0, k == KD - 1)
                return last

            def split_ready(s, half, o, l):
                pe.wait_ge(*at("w_split", 2 * s + half + 1 + o(8), l))

            def row_slot(s, banks, first, last_, moving, l, o):
                for k in range(2):
                    split_ready(s, k, o, l)
                    for c in range(KD):
                        w0 = k * D + c * P
                        rh, rl = moving(k)
                        ins = mm3(PS[:, banks[c // 2], (c % 2) * T:(c % 2 + 1) * T], (s % 2, slice(w0, w0 + P)),
                                  rh, rl, first and k == 0 and c % 2 == 0, last_ and k == 1)
                        if last_ and k == 1 and c % 2 and c < KD - 1:
                            ins.then_inc(*one("out_done"))
                ins.then_inc(*one("w_used"))

            def tok_mm(out, k, t, wsl):
                ts = slice(t * P, (t + 1) * P)
                w = (slice(None),) + wsl
                M(out, hh[:, k, ts], wh[w], start=(k == 0), stop=False)
                M(out, hl[:, k, ts], wh[w], start=False, stop=False)
                return M(out, hh[:, k, ts], wl[w], start=False, stop=(k == KD - 1))

            def norm(l, n, inc=one):
                for c in range(KD):
                    pe.wait_ge(*at("sq_ready", n * KD + c + 1, l))
                    M(PS[:, NORM_BANK[n], 0:T], ones, scr[:, c, :], start=(c == 0), stop=(c == KD - 1))\
                        .then_inc(*inc("sq_used"))

            def ada_sum(gr, l, o=still, r=0, inc=one):
                col = 4 * ada_place(2 * gr, 0)[1]
                pe.wait_ge(*at("ada_used", 2 * gr + 2 + o(2 * r), l))
                for i in range(4):
                    ins = M(PS[:, 7, bass.ds(o(4 * r) + col + i, 1)], acc[:, i * P:(i + 1) * P], onecol,
                            start=True, stop=True)
                ins.then_inc(*inc("acc_used"))

            def ffn(l, f):
                s0, s1 = (FFN1_IN, FFN1_OUT) if f == 0 else (FFN2_IN, FFN2_OUT)
                for s, o in steps(pe, s0, KF, peel=(2, 6)[f]):
                    j = s - s0
                    pe.wait_ge(*at("hf_ready", f * KF + j - 3 + o(4), l))
                    if j == 0:
                        ins = first_slot(s, 0, f * 2 * KD, l)
                    for half in range(2) if j else ():
                        split_ready(s, half, o, l)
                        ins = in_tile(s, half, j % 4, half * T)
                    ins.then_inc(*one("w_used"))
                    if f == 0 and j % 4 == 0 and j >= 4:
                        ada_sum(3 + j // 4, l, o, 1)
                    if f == 1 and j % 4 == 0 and j >= 8:
                        ada_sum(14 + j // 4, l, o, 1)
                for s, o in steps(pe, s1, 11, *((1, 2), (2, 1))[f]):
                    j = s - s1
                    pe.wait_ge(*at("hid_ready", f * KF + 2 * j + 2 + o(8), l))
                    if s == s1:
                        pe.wait_ge(*at("hid_ready", f * KF + 19, l))

                    def moving(k):
                        r = bass.ds(o(8) + 2 * j + k, 1)
                        return (hidh[:, r, :].rearrange("p a b -> p (a b)"),
                                hidl[:, r, :].rearrange("p a b -> p (a b)"))

                    row_slot(s, OUT_BANKS[2 * f], s == s1, s == s1 + 10, moving, l, o)
                    if j == (3, 5)[f]:
                        ada_sum((9, 20)[f], l, o, 1)

            for name in ("w_used", "vec_rows", "lora_done"):
                pe.sem_inc(sem(name), BEFORE[name])
            pe.wait_ge(sem("cst_loaded"), 16)
            pe.wait_ge(sem("c_loaded"), 32)
            pe.wait_ge(sem("zeroed"), 1)
            nc.tensor.transpose(PS[:, 6, 0:P], vrows[:, 0, :], ident).then_inc(sem("cT_ready"), 1)
            pe.wait_ge(sem("x_loaded"), 16)
            for i in range(4):
                for c in (2 * i, 2 * i + 1):
                    for t in range(TT):
                        col = ((c % 2) * 2 + t) * P
                        ins = nc.tensor.transpose(PS[:, i, col:col + P], xin[:, t, c * P:(c + 1) * P], ident)
                ins.then_inc(sem("x_tr"), 1)
            norm(0, 0, inc=once)
            pe.wait_ge(sem("cact_ready"), 1)
            for gr in range(4):
                ada_sum(gr, 0, inc=once)

            with pe.Fori(0, DEPTH) as l:
                pe.wait_ge(sem("rows_loaded"), (l + 1) * (16 * 13))
                pe.wait_ge(*at("x_ready", KD, l))
                nc.tensor.transpose(PS[:, 0, 0:P], vrows[:, 0, :], ident)
                nc.tensor.transpose(PS[:, 0, P:2 * P], vrows[:, 1, :], ident).then_inc(*one("vec_rows"))
                ffn(l, 0)
                norm(l, 1)
                for s in range(ATT_IN, RW_IN):
                    i = s - ATT_IN
                    split_ready(s, 1, still, l)
                    if s == SLOT_V:
                        for t in range(TT):
                            for k in range(KD):
                                ins = tok_mm(PS[:, i, t * 256:(t + 1) * 256], k, t, (s % 2, slice(k * 256, (k + 1) * 256)))
                    elif i == 4:
                        for t in range(TT):
                            for k in range(KD):
                                tok_mm(PS[:, i, t * P:(t + 1) * P], k, t, (s % 2, slice(k * P, (k + 1) * P)))
                        ins = in_tile(s, 1, i, T)
                    elif i == 0:
                        ins = first_slot(s, i, KD, l)
                    else:
                        n = 96 if s == SLOT_KR else P
                        in_tile(s, 0, i, 0, n)
                        ins = in_tile(s, 1, i, T, n)
                    ins.then_inc(*one("w_used"))
                    if i in (1, 5):
                        ada_sum(11 + i // 4, l)
                pe.wait_ge(*at("att_in", 7, l))

                def sb_scores(c):
                    if c == 2:
                        pe.wait_ge(*at("sb_lw", 1, l))
                    for h in range(2):
                        r = slice(64 * h, 64 * h + 64)
                        b = 2 * (c % 2) + h
                        q, k = qk[:, c, :], qk[:, 3 + c, :]
                        M(PS[:, b, 0:T], k[r, 0:P], q[r, :], start=True, stop=True)
                        ins = M(PS[:, b, T:384], k[r, P:T], q[r, P:T], start=True, stop=True)
                    ins.then_inc(*one("sb_scored"))

                def sb_sum(c):
                    pe.wait_ge(*at("sb_sp", c + 1, l))
                    pe.wait_ge(*at("sb_ln", c + 1, l))
                    for h in range(2):
                        b = 2 * (c % 2) + h
                        s0, s1 = sbs[:, c % 2, h, 0:T], sbs[:, c % 2, h, T:384]
                        M(PS[:, b, 0:T], const(C_TRI), s0, start=True, stop=False, skip_group_check=True)
                        M(PS[:, b, P:T], ones, s1, start=False, stop=True, skip_group_check=True)
                        ins = M(PS[:, b, T:384], const(C_TRI), s1, start=False, stop=True, skip_group_check=True)
                    ins.then_inc(*one("sb_summed"))

                def sb_y(c):
                    pe.wait_ge(*at("sb_w", c + 1, l))
                    for h in range(2):
                        r = slice(64 * h, 64 * h + 64)
                        hc = slice((2 * c + h) * 64, (2 * c + h) * 64 + 64)
                        M(PS[r, 4 + c, 0:T], vs[:, 0, hc], sbe[:, c % 2, h, 0:T], start=True, stop=False,
                          skip_group_check=True)
                        ins = M(PS[r, 4 + c, P:T], vs[:, 1, hc], sbe[:, c % 2, h, T:384], start=False, stop=True,
                                skip_group_check=True)
                    ins.then_inc(*one("sb_y"))

                sb_scores(0)
                sb_scores(1)
                sb_sum(0)
                sb_sum(1)
                sb_y(0)
                sb_scores(2)
                sb_y(1)
                sb_sum(2)
                sb_y(2)
                pe.wait_ge(*at("mla_sq", 1, l))
                pe.wait_ge(*at("sb_lw", 3, l))
                for i, (c, st, sp_) in enumerate(((0, True, False), (1, False, True), (2, True, True))):
                    for t in range(TT):
                        col = t if c < 2 else 2 + t
                        ins = M(PS[:, 3, col:col + 1], scr[:, c, t * P:(t + 1) * P], onecol, start=(i == 0 and t == 0),
                                stop=sp_, skip_group_check=True)
                ins.then_inc(*one("mla_sum"))
                pe.wait_ge(*at("mla_rinv", 1, l))
                pe.wait_ge(*at("sb_yl", 2, l))
                for i in range(2):
                    for t in range(TT):
                        ins = M(PS[:, 4 + i, t * P:(t + 1) * P],
                                hstat[:, 1, 2 * i + t:2 * i + t + 1].broadcast_to([P, P]), ident, start=True, stop=True)
                ins.then_inc(*one("mla_rb"))
                pe.wait_ge(*at("mla_lat", 3, l))
                pe.wait_ge(sem("small_loaded"), (l + 1) * (16 * 10))
                for i in range(PAIRS):
                    for h in range(2):
                        c0 = (2 * i + h) * P
                        ins = M(PS[0:NOPE, i, h * T:(h + 1) * T], w_ukv[:, c0:c0 + NOPE], cqkv[:, 2, :],
                                start=True, stop=True)
                    ins.then_inc(*one("mla_k"))
                pe.wait_ge(*at("sb_yl", 3, l))
                vcols = w_ukv[:, :].rearrange("p (h n) -> p h n", h=HEADS)[:, :, NOPE:P]
                for t in range(TT):
                    ins = M(PS[:, 6 + t, 0:BW], cqkv[:, 2, t * P:(t + 1) * P], vcols, start=True, stop=True)
                ins.then_inc(*one("mla_v"))
                for i in range(PAIRS):
                    if i:
                        pe.wait_ge(*at("mla_qr", i, l))
                    if i == 2:
                        pe.wait_ge(*at("mla_qn", 1, l))
                    for h in range(2):
                        hd = 2 * i + h
                        for k in range(2):
                            M(PS[0:96, 3 + (i % 2), h * T:(h + 1) * T], w_uq[:, k, hd * 96:(hd + 1) * 96], cqkv[:, k, :],
                              start=(k == 0), stop=(k == 1))
                        for k in range(2):
                            ins = M(PS[NOPE:96, 5, h * T:(h + 1) * T], w_sw[:, k, hd, :], cqkv[:, k, :],
                                    start=(k == 0), stop=(k == 1))
                    ins.then_inc(*one("mla_q"))
                pe.wait_ge(*at("mla_kv_ready", 2, l))
                pe.wait_ge(*at("mla_qr", 3, l))
                pe.wait_ge(*at("mla_qn", 3, l))
                for r in range(2):
                    for i in range(3):
                        h = 3 * r + i
                        M(PS[:, h, 0:P], qT[0:96, h, 0:P], kT[0:96, h, 0:P], start=True, stop=True)
                        ins = M(PS[:, h, P:384], qT[0:96, h, P:T], kT[0:96, h, :], start=True, stop=True)
                    ins.then_inc(*one("mla_scored"))
                def mla_y(h):
                    pe.wait_ge(*at("mla_p", h + 1, l))
                    r = slice(64 * (h % 2), 64 * (h % 2) + 64)
                    M(PS[r, 4 + h // 2, 0:T], vm[:, 0, h * 64:(h + 1) * 64], mlp[:, h, 0:T], start=True, stop=False,
                      skip_group_check=True)
                    ins = M(PS[r, 4 + h // 2, P:T], vm[:, 1, h * 64:(h + 1) * 64], mlp[:, h, T:384], start=False,
                            stop=True, skip_group_check=True)
                    if h % 2:
                        ins.then_inc(*one("mla_y"))

                pe.wait_ge(*at("mla_sc", 2, l))
                for h in range(HEADS):
                    if h % 3 == 0:
                        pe.wait_ge(*at("mla_pr", h // 3 + 1, l))
                    if h >= 4:
                        pe.wait_ge(*at("mla_p", h - 3, l))
                    for j in range(3):
                        ins = nc.tensor.transpose(PS[:, h % 4, j * P:(j + 1) * P], mls[:, h, j * P:(j + 1) * P], ident)
                    ins.then_inc(*one("mla_tr"))
                    if h:
                        mla_y(h - 1)
                mla_y(HEADS - 1)
                for i in range(6):
                    s = RW_IN + i
                    if i >= 4:
                        pe.wait_ge(*at("pb_ready", i - 3, l))
                    split_ready(s, 1, still, l)
                    in_tile(s, 0, i % 4, 0)
                    in_tile(s, 1, i % 4, T).then_inc(*one("w_used"))
                pe.wait_ge(*at("lora_in", 1, l))
                for c in range(3):
                    cs, col = slice(c * P, (c + 1) * P), slice((c % 2) * T, (c % 2 + 1) * T)
                    M(PS[:, 2 + c // 2, col], lora[0:64, cs], ex[0:64, 0, :], start=True, stop=True)
                    M(PS[:, 4 + c // 2, col], lora[64:128, cs], m[64:128, 9, :], start=True, stop=True)
                for c in range(3):
                    cs, col = slice(c * P, (c + 1) * P), slice((c % 2) * T, (c % 2 + 1) * T)
                    M(PS[:, 6 + c // 2, col], lora_g[:, 0, cs], m[:, 10, :], start=True, stop=False)
                    ins = M(PS[:, 6 + c // 2, col], lora_g[96:128, 1, cs], m[96:128, 11, :], start=False, stop=True)
                ins.then_inc(*one("lora_done"))

                def head_stats(src, name):
                    for c in range(3):
                        for t in range(TT):
                            col = (t * 3 + c) * 2
                            ins = M(PS[:, 3, col:col + 2], src[:, c, t * P:(t + 1) * P], blk2, start=True, stop=True)
                    ins.then_inc(*one(name))

                def head_spread(name):
                    for c in range(3):
                        for t in range(TT):
                            col = (t * 3 + c) * 2
                            o = (c % 2) * T + t * P
                            for h in range(2):
                                w = hstat[:, 1, col + h:col + h + 1].broadcast_to([P, 64])
                                ins = M(PS[64 * h:64 * h + 64, 4 + c // 2, o:o + P], w, ident, start=True, stop=True)
                    ins.then_inc(*one(name))

                pe.wait_ge(*at("kk_sq", 1, l))
                pe.wait_ge(*at("wa_ready", 3, l))
                head_stats(ex, "kk_stat")
                pe.wait_ge(*at("bon_in", 1, l))
                pe.wait_ge(*at("g_ready", 1, l))
                for c in range(3):
                    ins = M(PS[:, 6 + c // 2, (c % 2) * T:(c % 2 + 1) * T], blk, bon[:, c, :], start=True, stop=True)
                ins.then_inc(*one("bon_done"))
                pe.wait_ge(*at("kk_rinv", 1, l))
                head_spread("kk_rb")
                pe.wait_ge(*at("tilde", 1, l))

                def A(dst, lhs, rhs, tt, name):
                    ts = slice(tt * P, (tt + 1) * P)
                    for par in range(2):
                        r = slice(64 * par, 64 * par + 64)
                        for c in range(3):
                            ins = M(PS[:, dst + par, c * P:(c + 1) * P], lhs[:, c, ts][r], rhs[:, c, ts][r],
                                    start=True, stop=True)
                    ins.then_inc(*one(name))

                for tt in range(TT):
                    ts = slice(tt * P, (tt + 1) * P)
                    pe.wait_ge(*at("S_ready", 2 * tt + 1, l))
                    for i, src in enumerate((kk, av, kp, vv)):
                        for c in range(3):
                            ins = nc.tensor.transpose(PS[:, i, c * P:(c + 1) * P], src[:, c, ts], ident)
                    ins.then_inc(*one("tok_done"))
                    A(4, av, kk, tt, "ab_done")
                    if tt:
                        pe.wait_ge(*at("ya_ready", tt, l))
                    A(6, kk, av, tt, "ab_done")
                    pe.wait_ge(*at("at_ready", tt + 1, l))
                    A(4, kp, kk, tt, "ak_done")
                    pe.wait_ge(*at("T_ready", 11 * tt + 1, l))
                    A(6, av, rr, tt, "ak_done")
                    pe.wait_ge(*at("ak_ready", 3 * tt + 1, l))
                    A(4, kp, rr, tt, "ak_done")
                    pe.wait_ge(*at("tok_act", 2 * tt + 2, l))
                    pe.wait_ge(*at("tok_dve", tt + 1, l))
                    for b in range(5):
                        pe.wait_ge(*at("X_ready", 5 * tt + b + 1, l))
                        for par in range(2):
                            pe.wait_ge(*at("T_ready", 11 * tt + (2 * b + par if b else 1), l))
                            for c in range(3):
                                ins = M(PS[:, par, c * P:(c + 1) * P], X[:, par, c, :], Tm[:, par, c, :], start=True,
                                        stop=True)
                            ins.then_inc(*one("z_done"))
                        for par in range(2):
                            pe.wait_ge(*at("z_ready", 2 * (5 * tt + b) + par + 1, l))
                            if b == 0:
                                pe.wait_ge(*at("ak_ready", 3 * tt + 3, l))
                            for c in range(3):
                                if b < 4:
                                    M(PS[:, 2 + par, c * P:(c + 1) * P], TTm[:, par, c, :], Z[:, par, c, :],
                                      start=True, stop=True)
                                ins = M(PS[:, 4 + par, c * P:(c + 1) * P], Z[:, par, c, :], TTm[:, par, c, :],
                                        start=True, stop=True)
                            ins.then_inc(*one("tz_done"))
                    for h in range(HEADS):
                        hc = slice(h * 64, h * 64 + 64)
                        ins = M(PS[:, 0, hc], Aak[:, h % 2, h // 2, :], tok[:, 3, hc], start=True, stop=True)
                    ins.then_inc(*one("g_done"))
                    pe.wait_ge(*at("T_ready", 11 * tt + 11, l))
                    for h in range(HEADS):
                        r = slice(64 * (h % 2), 64 * (h % 2) + 64)
                        ins = M(PS[r, 4, (h // 2) * P:(h // 2 + 1) * P], tok[:, 0, h * 64:h * 64 + 64],
                                TTm[:, h % 2, h // 2, :], start=True, stop=True)
                    ins.then_inc(*one("wt_done"))
                    pe.wait_ge(*at("G_ready", tt + 1, l))
                    for h in range(HEADS):
                        hc = slice(h * 64, h * 64 + 64)
                        ins = M(PS[:, 1, hc], TTm[:, h % 2, h // 2, :], Gm[:, hc], start=True, stop=True)
                    ins.then_inc(*one("u0_done"))
                    pe.wait_ge(*at("wt_ready", tt + 1, l))
                    for q in (2 * tt, 2 * tt + 1):
                        rows = slice(64 * (q % 2), 64 * (q % 2) + 64)
                        pe.wait_ge(*at("S_ready", q + 1, l))
                        for c in range(3):
                            ins = M(PS[:, 5, c * P:(c + 1) * P], wT[:, c, :], S[:, c, :], start=True, stop=True)
                        ins.then_inc(*one("u_done"))
                        for c in range(3):
                            o = c * P + 64 * (q % 2)
                            M(PS[:, 6, o:o + 64], S[:, c, :], rr[:, c, q * 64:q * 64 + 64],
                              start=(q % 2 == 0 and c == 0), stop=False, skip_group_check=True)
                        pe.wait_ge(*at("u_ready", q + 1, l))
                        for c in range(3):
                            cs = slice(c * P, (c + 1) * P)
                            M(PS[:, 3, cs], tok[rows, 1, cs], u_[rows, cs], start=True, stop=False)
                            ins = M(PS[:, 3, cs], tok[rows, 2, cs], tok[rows, 3, cs], start=False, stop=True)
                        ins.then_inc(*one("s_done"))
                    for h in range(HEADS):
                        r = slice(64 * (h % 2), 64 * (h % 2) + 64)
                        cs, hc = slice((h // 2) * P, (h // 2 + 1) * P), slice(h * 64, h * 64 + 64)
                        M(PS[r, 6, cs], u_[:, hc], Arb[:, h % 2, h // 2, :], start=False, stop=False,
                          skip_group_check=True)
                        ins = M(PS[r, 6, cs], tok[:, 3, hc], Ark[:, h % 2, h // 2, :], start=False, stop=True,
                                skip_group_check=True)
                    ins.then_inc(*one("y_done"))
                pe.wait_ge(*at("ya_ready", 2, l))
                for c in range(3):
                    ins = M(PS[:, c // 2, (c % 2) * T:(c % 2 + 1) * T], blk, ya[:, c, :], start=True, stop=True)
                ins.then_inc(*one("gn_mean"))
                pe.wait_ge(*at("gn_sq", 1, l))
                head_stats(ex, "gn_stat")
                pe.wait_ge(*at("gn_rinv", 1, l))
                head_spread("gn_rb")
                for s, o in steps(pe, GATE_IN, 12, tail=4):
                    j = s - GATE_IN
                    pe.wait_ge(*at("gate_ready", j - 3 + o(4), l))
                    for half in range(2):
                        split_ready(s, half, o, l)
                        ins = in_tile(s, half, j % 4, half * T)
                    ins.then_inc(*one("w_used"))
                    if j % 4 == 2:
                        ada_sum(13 + j // 4, l, o, 1)
                pe.wait_ge(*at("mod_done", 1, l))
                pe.wait_ge(*at("ya_lo", 1, l))
                pe.wait_ge(*at("gate_ready", 12, l))
                for kb in range(9):
                    n, k = kb // 3, kb % 3
                    s = BRANCH + kb // 2
                    split_ready(s, kb % 2 if kb < 8 else 1, still, l)
                    if n == 2 and k == 0:
                        pe.wait_ge(*at("br_used", 4, l))
                    w0 = (kb % 2) * D
                    for c in range(KD):
                        b = BR_BANKS[n] + c // 2
                        ins = mm3(PS[:, b, (c % 2) * T:(c % 2 + 1) * T], (s % 2, slice(w0 + c * P, w0 + (c + 1) * P)),
                                  yh[:, kb, :], yl[:, kb, :], k == 0 and c % 2 == 0, k == 2)
                        if c == KD - 1 and (kb % 2 or kb == 8):
                            ins.then_inc(*one("w_used"))
                        elif k == 2 and c % 2:
                            ins.then_inc(*one("br_done"))
                pe.wait_ge(*at("br_used", 8, l))
                for i in range(4):
                    s = MIX_OUT + i
                    pe.wait_ge(*at("mg_lo", i + 1, l))
                    row_slot(s, OUT_BANKS[1], i == 0, i == 3,
                             lambda k: (hh[:, 2 * i + k, :], hl[:, 2 * i + k, :]), l, still)
                norm(l, 2)
                ffn(l, 1)
                norm(l, 3)
            pe.wait_ge(sem("y_ready"), KD)
            for t in range(TT):
                for c in range(KD):
                    o = (c % 4) * P
                    ins = nc.tensor.transpose(PS[:, 2 * t + 4 + c // 4, o:o + P], x[:, c, t * P:(t + 1) * P], ident)
                ins.then_inc(sem("out_tr"), 1)


_INS = ["x", "c", "positions", "ada_w", "ada_b", "norm_g", "ffn1_w_in", "ffn1_w_out", "mix_w_in", "rwkv_mu",
        "rwkv_w0", "rwkv_w2", "rwkv_a0", "rwkv_a2", "rwkv_g2", "rwkv_k_k", "rwkv_k_a", "rwkv_r_k", "rwkv_lnx_g",
        "rwkv_lnx_b", "mla_q_norm_g", "mla_w_uq", "mla_kv_norm_g", "mla_w_ukv", "branch_w", "mix_w_out",
        "ffn2_w_in", "ffn2_w_out", "final_norm_g"]


def build(nc, shapes):
    args = {n: nc.dram_tensor(f"in_{n}", shape, dt, kind="ExternalInput").ap() for n, (shape, dt) in shapes.items()}
    args["out"] = nc.dram_tensor("out_0", (1, T, D), F32, kind="ExternalOutput").ap()
    tally = {}
    hybrid_trunk(nc, args, PER_LAYER, tally)
    return tally


def kernel(**inputs):
    import concourse.bacc as _bacc
    from concourse.bass_utils import run_bass_kernel_spmd as _run

    arrays = {n: np.ascontiguousarray(inputs[n]) for n in _INS}
    arrays["consts"] = shape_constants()
    nc = _bacc.Bacc("TRN2", target_bir_lowering=False, num_devices=1, dynamic_dma_scratch_size=1024)
    build(nc, {n: (v.shape, mybir.dt.from_np(v.dtype)) for n, v in arrays.items()})
    r = _run(nc, [{f"in_{n}": v for n, v in arrays.items()}], core_ids=[0])
    return r.results[0]["out_0"]
```

```python
from contextlib import ExitStack

import numpy as np

import concourse.bass as bass
from concourse import mybir

F32 = mybir.dt.float32
F32R = mybir.dt.float32r
I32 = mybir.dt.int32
ALU = mybir.AluOpType
ACT = mybir.ActivationFunctionType
AX_X = mybir.AxisListType.X

P = 128
DEPTH, D, T, F = 2, 1024, 256, 2816
KD, KF, TT = D // P, F // P, T // P
HEADS, HD, BW, NB = 6, 64, 384, 3
PAIRS = HEADS // 2
LORA_W, LORA_A, LORA_G = 64, 64, 160
Q_LORA, KV_LORA, ROPE, NOPE = 256, 128, 32, 64
RW_COLS = 3 * BW + LORA_W + LORA_A + LORA_G
SBQ, SBV = RW_COLS, RW_COLS + 2 * BW
CQ = RW_COLS + 3 * BW
CKV = CQ + Q_LORA
KR = CKV + KV_LORA
GATE0 = KR + ROPE
D_IN = GATE0 + NB * D
N_ADA = 9
CHUNK = 64
EPS, GN_EPS = 1e-6, 64e-5
SB_SCALE = HD ** -0.5
MLA_SCALE = (NOPE + ROPE) ** -0.5
NEG = -1e30

SLOT = 2048
FFN1_IN, FFN1_OUT = 0, 22
ATT_IN, RW_IN, GATE_IN = 33, 40, 46
BRANCH, MIX_OUT = 58, 63
FFN2_IN, FFN2_OUT = 67, 89
SLOTS = 100
IN_COLS = {
    33: (SBQ, SBQ + 128), 34: (SBQ + 256, SBQ + 384), 35: (SBQ + 512, SBQ + 640),
    37: (SBV + 256, CKV), 38: (CQ, CQ + 128),
    40: (0, 128), 41: (256, 384), 42: (512, 640), 43: (768, 896), 44: (1024, 1152),
    45: (1280, RW_COLS - 128),
}
SLOT_V, SLOT_KR = 36, 39


def slot_size(s):
    if s == SLOT_KR:
        return 2 * KD * 96
    return D if s == MIX_OUT - 1 else SLOT


def slot_dmas(s):
    s %= SLOTS
    if s == SLOT_KR:
        return 3
    if s == SLOT_V or FFN1_OUT <= s < ATT_IN or BRANCH <= s < FFN2_IN or s >= FFN2_OUT:
        return 1
    return 2


def dmas_before(s):
    return sum(slot_dmas(x) for x in range(s % 4, s + 1, 4))


V_ADA, V_NORM, V_MU, V_W0, V_A0, V_KK, V_KA, V_RK, V_LG, V_LB, V_QN, V_KVN = (
    0, 72, 96, 108, 111, 114, 117, 120, 123, 126, 129, 131)
N_VEC = 132

(C_ID, C_ONE, C_BLK, C_TRI, C_SBM, C_MIN, C_CAUS, C_LO1, C_UP, C_UPI, C_UP1, C_UP2, C_UP4, C_UP8,
 C_UP16, C_UP32, C_RST0, C_RST1, C_ROPE) = range(19)
LEVELS = (C_UP2, C_UP4, C_UP8, C_UP16, C_UP32)


def shape_constants():
    r, c = np.arange(P)[:, None], np.arange(P)[None, :]
    same = (r // CHUNK) == (c // CHUNK)
    out = [np.eye(P), np.ones((P, P)), same, r >= c, r < c, np.where(r < c, 0.0, NEG),
           np.where(c <= r, 0.0, NEG), (r // 2 == c // 2) & (r > c), same & (r < c), same & (r <= c)]
    for b in (1, 2, 4, 8, 16, 32):
        out.append((r // (2 * b) == c // (2 * b)) & (r % (2 * b) < b) & (c % (2 * b) >= b))
    reset = np.ones((P, T))
    reset[:, ::CHUNK] = 0.0
    out += [reset[:, :P], reset[:, P:]]
    rope = np.zeros((P, P))
    half = ROPE // 2
    freq = (1.0 / (np.float32(10000.0) ** (np.arange(0, ROPE, 2, dtype=np.float32) / np.float32(ROPE))))
    rope[NOPE:NOPE + half, 0] = freq
    rope[NOPE + half:NOPE + ROPE, 0] = freq
    rope[NOPE:NOPE + half, 1] = -1.0
    rope[NOPE + half:NOPE + ROPE, 1] = 1.0
    out.append(rope)
    return np.concatenate([x.astype(np.float32) for x in out], axis=1)


PER_LAYER = {
    "vec_ready": 1, "w_hi": 200, "hh_ready": 24, "sil_ready": 44, "sq_ready": 24, "rt_ready": 3,
    "att_in": 7, "sb_z": 3, "sb_ln": 3, "pb_ready": 6, "sb_w": 3, "sb_yh": 3, "mla_sq": 1, "mla_rt":
    1, "mla_kv_ready": 2, "mla_qn": 3, "mla_sc": 2, "mla_exp": 2, "mla_p": 6, "mla_yh": 3,
    "lora_in": 1, "kk_sq": 1, "w_gate": 3, "wa_ready": 3, "kk_rt": 1, "e_neg": 1, "e_cum": 1,
    "e_prev": 1, "g_ready": 1, "tok_act": 4, "z_ready": 20, "wt_ready": 2, "ya_ready": 2, "gn_sq":
    1, "gn_rt": 1, "ya_hi": 1, "gate_ready": 12, "mg_hi": 4, "w_split": 200, "t_ready": 24,
    "h_ready": 24, "hf_ready": 44, "ada_used": 72, "x_ready": 24, "mod_mid": 1, "sb_sp": 3, "sb_lw":
    3, "sb_yl": 3, "shifted": 12, "mla_rinv": 1, "mla_lat": 3, "mla_qr": 3, "mla_sub": 2, "mla_pr":
    2, "mla_yl": 3, "kk_max": 1, "cum_ready": 1, "kk_rinv": 1, "bon_in": 1, "tilde": 1, "S_ready":
    5, "bon_ready": 1, "tok_dve": 2, "at_ready": 2, "T_ready": 22, "ak_ready": 6, "G_ready": 2,
    "u0_ready": 2, "u_ready": 4, "gn_sub": 1, "gn_rinv": 1, "ya_final": 1, "ya_lo": 1, "mod_done":
    1, "br_used": 12, "merged": 4, "mg_lo": 4, "hid_ready": 44, "pb_zero": 1, "sb_min": 3,
    "shift_d": 12, "kk0": 1, "X_ready": 10, "pcm_ready": 4, "vec_rows": 1, "w_used": 100,
    "acc_used": 18, "out_done": 9, "sq_used": 24, "sb_scored": 3, "sb_summed": 3, "sb_y": 3,
    "mla_sum": 1, "mla_rb": 1, "mla_k": 3, "mla_v": 1, "mla_q": 3, "mla_scored": 2, "mla_tr": 6,
    "mla_y": 3, "wa_done": 1, "kk_stat": 1, "kk_rb": 1, "bon_done": 1, "lora_done": 1, "tok_done":
    2, "ab_done": 4, "ak_done": 6, "z_done": 20, "tz_done": 20, "g_done": 2, "wt_done": 2,
    "u0_done": 2, "u_done": 4, "s_done": 4, "y_done": 2, "gn_mean": 1, "gn_stat": 1, "gn_rb": 1,
    "br_done": 10,
}
BEFORE = {"w_split": 7, "w_used": 2, "hf_ready": 4, "hid_ready": 2, "gate_ready": 4, "lora_done": 1}
OUT_BANKS = ((4, 5, 6, 2), (0, 1, 2, 3), (4, 5, 6, 2))
BR_BANKS = (4, 0, 4)
NORM_BANK = (3, 3, 4, 3)


def hybrid_trunk(nc, a, per_layer, tally):
    out_dram = a["out"]
    ctx = ExitStack()
    with ctx:
        ctx.enter_context(nc.allow_non_contiguous_dma(reason="vectors and column blocks"))

        def sb(name, shape, dt=F32):
            return ctx.enter_context(nc.sbuf_tensor(name, shape, dt))

        raw = sb("raw", [P, 4, SLOT])
        wh = sb("wh", [P, 2, SLOT], F32R)
        wl = sb("wl", [P, 2, SLOT], F32R)
        ada_w = sb("ada_w_ring", [P, 4, SLOT // 2])
        acc = sb("ada_acc", [P, 512])
        x = sb("x", [P, KD, T])
        hh = sb("h_hi", [P, KD, T], F32R)
        hl = sb("h_lo", [P, KD, T], F32R)
        scr = sb("scr", [P, KD, T])
        cst = sb("cst", [P, 19 * P])
        vrows = sb("vrows", [P, 2, P])
        vec = sb("vec", [P, N_VEC])
        mod = sb("mod", [P, N_ADA * KD])
        gsc = sb("gsc", [P, 3, KD])
        hgate = sb("hgate", [P, 3, KD])
        omka = sb("omka", [P, 3])
        cact = sb("cact", [P, 2 * KD])
        warm = sb("warm", [P, 1])
        mla_stat = sb("mla_stat", [P, 2, 12])
        hstat = sb("hstat", [P, 2, 12])
        epsb = sb("eps_col", [P, 1])
        gneps = sb("gn_eps_col", [P, 1])
        one_b = sb("one_col", [P, 1])
        lora = sb("lora", [P, BW])
        lora_g = sb("lora_g", [P, 2, BW])
        w_uq = sb("w_uq", [P, 2, HEADS * 96])
        w_sw = sb("w_sw", [P, 2, HEADS, ROPE])
        w_ukv = sb("w_ukv", [P, HEADS * P])
        cosT = sb("cosT", [P, T])
        sinT = sb("sinT", [P, T])

        def const(n):
            return cst[:, n * P:(n + 1) * P]

        ident, ones, blk = const(C_ID), const(C_ONE), const(C_BLK)
        onecol = cst[:, C_ONE * P:C_ONE * P + 1]
        blk2 = cst[:, C_BLK * P:C_BLK * P + P:CHUNK]
        reset = cst[:, C_RST0 * P:C_RST0 * P + T]

        base = nc.sbuf_base
        base = (base + 63) // 64 * 64
        room = nc.sbuf_usable_end - base
        cur = [0]
        names = {}

        def at_(name, cols, dt=F32, off=None):
            if off is not None:
                cur[0] = off
            o = cur[0]
            cur[0] += cols * 4
            assert cur[0] <= room, (name, cur[0], room)
            names[name] = o
            return nc.alloc_sbuf_tensor_at(name, [P, cols], dt, offset=base + o)

        def v3(t, n):
            return t[:, :].rearrange("p (a b) -> p a b", a=n)

        hidh = v3(at_("hid_hi", KF * T, F32R, 0), KF)
        hidl = v3(at_("hid_lo", KF * T, F32R), KF)
        sil = v3(at_("sil", 2 * T), 2)
        hf = v3(at_("hf", 2 * T), 2)
        yh = v3(at_("y_hi", 9 * T, F32R, 0), 9)
        yl = v3(at_("y_lo", 9 * T, F32R), 9)
        mix0 = cur[0]
        qk = v3(at_("sb_qk", 6 * T, off=mix0), 6)
        vs = v3(at_("sb_v", 2 * BW), 2)
        cqkv = v3(at_("cqkv", 3 * T), 3)
        qT = v3(at_("mla_qT", HEADS * T), HEADS)
        kT = v3(at_("mla_kT", HEADS * T), HEADS)
        vm = v3(at_("mla_v", 2 * BW), 2)
        krA = v3(at_("krope", 2 * T), 2)
        sbz = at_("sb_z", 2 * 768)[:, :].rearrange("p (r h n) -> p r h n", r=2, h=2)
        sbe = at_("sb_e", 2 * 768)[:, :].rearrange("p (r h n) -> p r h n", r=2, h=2)
        sbs = at_("sb_s", 2 * 768)[:, :].rearrange("p (r h n) -> p r h n", r=2, h=2)
        rA = at_("ropeA", 2 * T)
        rB = at_("ropeB", 2 * T)
        rope_end = cur[0]
        mls = at_("mla_s", 6 * 384, off=names["sb_z"])[:, :].rearrange("p (h n) -> p h n", h=6)
        mlp = at_("mla_p", 6 * 384)[:, :].rearrange("p (h n) -> p h n", h=6)
        cur[0] = rope_end
        m = v3(at_("rw_m", 12 * T), 12)
        rw_end = names["rw_m"]
        lw = v3(at_("rw_lw", 3 * T, off=mix0), 3)
        av = v3(at_("rw_a", 3 * T), 3)
        kk = v3(at_("rw_kk", 3 * T), 3)
        cum = v3(at_("rw_cum", 3 * T), 3)
        ex = v3(at_("rw_e", 3 * T), 3)
        g = v3(at_("rw_g", 3 * T), 3)
        bon = v3(at_("rw_bon", 3 * T), 3)
        rr, kp, vv = m[:, 0:3], m[:, 3:6], m[:, 6:9]
        ya = lw
        tokr = at_("rw_tok", 4 * BW)
        tok = v3(tokr, 4)
        scr_all = scr[:, :, :].rearrange("p a b -> p (a b)")
        u_, u0 = scr_all[:, 0:BW], scr_all[:, BW:2 * BW]
        S, wT, pcm = (scr_all[:, i * BW:(i + 1) * BW].rearrange("p (a b) -> p a b", a=3) for i in (2, 3, 4))
        def six(name, off=None):
            return at_(name, 6 * P, off=off)[:, :].rearrange("p (a c n) -> p a c n", a=2, c=3)

        AT, X, Tm, TTm, Z, Aak = (six(n) for n in ("A_T", "A_X", "A_inv", "A_invT", "A_Z", "A_ak"))
        Arb, Ark = six("A_rb"), six("A_rk")
        assert cur[0] <= rw_end
        pb = scr_all[:, 0:4 * (T + 1)].rearrange("p (r a b) -> p r a b", r=2, a=2)
        lat_sq = scr_all[:, KD * T - 3 * T:KD * T].rearrange("p (a b) -> p a b", a=3)
        Gm = Z[:, :, :, :].rearrange("p a c n -> p (a c n)")[:, 0:BW]
        gates = v3(at_("gates", 24 * T, off=names["rw_tok"]), 24)
        mg = v3(at_("merged", KD * T), KD)
        mt = v3(at_("merge_t", 4 * T), 4)
        xin = v3(at_("x_rows", 2 * D, off=0), 2)
        xo = v3(at_("out_rows", 2 * D), 2)
        posi = at_("pos_i", T, I32)
        ang = at_("ang", 4 * T)[:, :].rearrange("p (a b) -> p a b", a=4)

        PS = ctx.enter_context(nc.psum_tensor("PS", [P, 8, 512], F32))

        def bank(b):
            return PS[:, b, :]

        sems = {}
        tally.clear()
        times = [1]

        def sem(name):
            if name not in sems:
                sems[name] = ctx.enter_context(nc.semaphore(name))
            return sems[name]

        def one(name, n=1):
            tally[name] = tally.get(name, 0) + n * times[0]
            return sem(name), n

        def once(name, n=1):
            return sem(name), n

        def at(name, k, l=0):
            v = k + BEFORE.get(name, 0)
            return sem(name), l * per_layer.get(name, 0) + v

        def still(n):
            return 0

        def steps(eng, first, count, peel=0, tail=0):
            for s in range(first, first + peel):
                yield s, still
            rounds = (count - peel - tail) // 4
            at0 = first + peel
            times[0] = rounds
            with eng.Fori(0, rounds) as i:
                for u in range(4):
                    yield at0 + u, lambda n: i * n
            times[0] = 1
            for s in range(at0 + 4 * rounds, first + count):
                yield s, still

        def ada_place(n, l):
            if n < 64:
                return l, n // 4
            return ((l + 1) % DEPTH, n // 4 - 16) if n < 80 else (l, n // 4 - 4)

        def loaded(s, o, l):
            q = s % 4
            per = sum(slot_dmas(v) for v in range(q, SLOTS, 4))
            per_round = slot_dmas(s)
            return sem(f"raw_loaded{q}"), l * (16 * per) + 16 * dmas_before(s) + o(16 * per_round)

        block = ctx.enter_context(nc.Block())

        @block.sync
        def _(sp):
            win = [a[n].rearrange("l (k p) n -> p (l k) n", p=P) for n in ("ffn1_w_in", "ffn2_w_in")]
            wout = [a[n].rearrange("l (k p) n -> p (l k) n", p=P) for n in ("ffn1_w_out", "ffn2_w_out")]
            wmix = a["mix_w_in"].rearrange("l (k p) n -> p (l k) n", p=P)
            wbr = a["branch_w"].rearrange("l n (k p) d -> p (l n k) d", p=P)
            wmo = a["mix_w_out"].rearrange("l (k p) n -> p (l k) n", p=P)
            wada = a["ada_w"].rearrange("l (k p) n -> p (l k) n", p=P)

            def free(s, o, l):
                sp.wait_ge(*at("w_split", 2 * (s - 4) + 2 + o(8), l))

            def halves(s, n=P):
                return raw[:, s % 4, 0:2 * KD * n].rearrange("p (g k n) -> p g k n", g=2, k=KD)

            def rows(s, k):
                return raw[:, s % 4, 0:k * D].rearrange("p (k n) -> p k n", k=k)

            def ada(n, o, l):
                if n >= 4:
                    sp.wait_ge(*at("ada_used", n - 3 + o(4), l))
                layer, group = ada_place(n, l)
                sp.dma_start(ada_w[:, n % 4, :].rearrange("p (k n) -> p k n", k=2),
                             wada[:, bass.ds(layer * KD + (n % 4) * 2, 2), bass.ds(o(512) + group * 512, 512)])\
                    .then_inc(sem(f"ada_loaded{n % 4}"), 16)

            def ffn_loads(l, f):
                s0, s1 = (FFN1_IN, FFN1_OUT) if f == 0 else (FFN2_IN, FFN2_OUT)
                for s, o in steps(sp, s0, KF, *((2, 0), (5, 1))[f]):
                    j = s - s0
                    free(s, o, l)
                    for half in (1, 0):
                        c0 = half * F + j * P
                        cols = bass.ds(o(4 * P) + c0, P)
                        sp.dma_start(halves(s)[:, half], win[f][:, bass.ds(l * KD, KD), cols])\
                            .then_inc(sem(f"raw_loaded{s % 4}"), 16)
                    if 2 <= j and (f == 0 or 5 <= j < 21):
                        ada((14, 59)[f] + j, o, l)
                for s, o in steps(sp, s1, 11, peel=1, tail=2):
                    j = s - s1
                    free(s, o, l)
                    sp.dma_start(rows(s, 2), wout[f][:, bass.ds(l * KF + 2 * j + o(8), 2), :])\
                        .then_inc(sem(f"raw_loaded{s % 4}"), 16)
                    if f == 0 or 1 <= j <= 8:
                        ada((36, 79)[f] + j, o, l)

            def row_loads(layer):
                ab = a["ada_b"].rearrange("l (k p) -> (l k) p", p=P)
                ng = a["norm_g"].rearrange("l i (k p) -> (l i k) p", p=P)
                todo = [(V_ADA, 0, ab, 72), (V_NORM, 0, ng, 24)]
                for c0, n, w in ((V_W0, "rwkv_w0", 3), (V_A0, "rwkv_a0", 3), (V_KK, "rwkv_k_k", 3),
                                 (V_KA, "rwkv_k_a", 3), (V_LG, "rwkv_lnx_g", 3), (V_LB, "rwkv_lnx_b", 3),
                                 (V_QN, "mla_q_norm_g", 2), (V_KVN, "mla_kv_norm_g", 1)):
                    todo.append((c0 % 126, c0 // 126, a[n].rearrange("l (k p) -> (l k) p", p=P), w))
                rk = a["rwkv_r_k"].rearrange("l (k h) d -> (l k) (h d)", h=2)
                todo.append((V_RK, 0, rk, 3))
                for r0, half, src, w in todo:
                    sp.dma_start(vrows[r0:r0 + w, half, :], src[bass.ds(layer * w, w), :])\
                        .then_inc(sem("rows_loaded"), 16)
                mu = a["rwkv_mu"]
                sp.dma_start(vrows[V_MU:V_MU + 11, 0, :],
                             mu[bass.ds(layer, 1), 0:11 * P].rearrange("l (k p) -> (l k) p", p=P))\
                    .then_inc(sem("rows_loaded"), 16)
                sp.dma_start(vrows[V_MU + 11:V_MU + 12, 0, :], mu[bass.ds(layer, 1), RW_COLS - P:RW_COLS])\
                    .then_inc(sem("rows_loaded"), 16)

            sp.dma_start(cst[:, :], a["consts"]).then_inc(sem("cst_loaded"), 16)
            sp.wait_ge(sem("zeroed"), 1)
            sp.dma_start(vrows[0:KD, 0, :], a["c"].rearrange("b (k p) -> (b k) p", p=P))\
                .then_inc(sem("c_loaded"), 16)
            sp.dma_start(vrows[KD:2 * KD, 0, :], a["final_norm_g"].rearrange("(k p) -> k p", p=P))\
                .then_inc(sem("c_loaded"), 16)
            sp.dma_start(posi[NOPE:NOPE + ROPE, :], a["positions"].broadcast_to([ROPE, T]))\
                .then_inc(sem("pos_loaded"), 16)
            for n in range(4):
                ada(n, still, 0)
            sp.dma_start(xin[:, :, :], a["x"][0].rearrange("(t p) d -> p t d", p=P)).then_inc(sem("x_loaded"), 16)
            for n in range(4, 16):
                if n == 8:
                    sp.wait_ge(sem("cT_ready"), 1)
                    row_loads(0)
                ada(n, still, 0)
            with sp.Fori(0, DEPTH) as l:
                ffn_loads(l, 0)
                sp.wait_ge(*at("vec_rows", 1, l))
                row_loads((l + 1) % DEPTH)
                sp.wait_ge(*at("lora_done", 0, l))
                sp.dma_start(lora[0:64, :], a["rwkv_w2"].rearrange("l p n -> p l n")[:, bass.ds(l, 1), :])\
                    .then_inc(sem("small_loaded"), 16)
                sp.dma_start(lora[64:128, :], a["rwkv_a2"].rearrange("l p n -> p l n")[:, bass.ds(l, 1), :])\
                    .then_inc(sem("small_loaded"), 16)
                g2 = a["rwkv_g2"].rearrange("l p n -> p l n")
                sp.dma_start(lora_g[:, 0, :], g2[0:P, bass.ds(l, 1), :]).then_inc(sem("small_loaded"), 16)
                sp.dma_start(lora_g[96:128, 1, :], g2[P:LORA_G, bass.ds(l, 1), :])\
                    .then_inc(sem("small_loaded"), 16)
                uq = a["mla_w_uq"].rearrange("l (k p) n -> p (l k) n", p=P)
                sp.dma_start(w_uq[:, :, :], uq[:, bass.ds(l * 2, 2), :]).then_inc(sem("small_loaded"), 16)
                uqh = a["mla_w_uq"].rearrange("l (k p) (h n) -> p (l k) h n", p=P, h=HEADS)
                for k in range(2):
                    for half in range(2):
                        src = NOPE + 16 * (1 - half)
                        sp.dma_start(w_sw[:, k, :, 16 * half:16 * half + 16],
                                     uqh[:, bass.ds(l * 2 + k, 1), :, src:src + 16].rearrange("p k h n -> p (k h) n"))\
                            .then_inc(sem("small_loaded"), 16)
                sp.dma_start(w_ukv[:, :], a["mla_w_ukv"].rearrange("l p n -> p l n")[:, bass.ds(l, 1), :])\
                    .then_inc(sem("small_loaded"), 16)
                for s in range(ATT_IN, GATE_IN):
                    free(s, still, l)
                    kd = bass.ds(l * KD, KD)
                    inc = sem(f"raw_loaded{s % 4}")
                    if s == SLOT_V:
                        sp.dma_start(raw[:, s % 4, :].rearrange("p (k n) -> p k n", k=KD),
                                     wmix[:, kd, SBV:SBV + 256]).then_inc(inc, 16)
                    elif s == SLOT_KR:
                        sp.dma_start(halves(s, 96)[:, 0], wmix[:, kd, KR - 64:KR + 32]).then_inc(inc, 16)
                        sp.dma_start(halves(s, 96)[:, 1, :, 0:80], wmix[:, kd, KR - 48:KR + 32]).then_inc(inc, 16)
                        sp.dma_start(halves(s, 96)[:, 1, :, 80:96], wmix[:, kd, KR:KR + 16]).then_inc(inc, 16)
                    else:
                        for half in (1, 0):
                            c0 = IN_COLS[s][half]
                            sp.dma_start(halves(s)[:, half], wmix[:, kd, c0:c0 + P]).then_inc(inc, 16)
                    if s < RW_IN:
                        ada(47 + s - ATT_IN, still, l)
                for s, o in steps(sp, GATE_IN, 12, tail=4):
                    j = s - GATE_IN
                    free(s, o, l)
                    for half in range(2):
                        c0 = GATE0 + j * 256 + half * P
                        cols = bass.ds(o(4 * 256) + c0, P)
                        sp.dma_start(halves(s)[:, half], wmix[:, bass.ds(l * KD, KD), cols])\
                            .then_inc(sem(f"raw_loaded{s % 4}"), 16)
                    if j < 10:
                        ada(54 + j, o, l)
                for s in range(BRANCH, FFN2_IN):
                    free(s, still, l)
                    w, k0, per = (wbr, 2 * (s - BRANCH), 9) if s < MIX_OUT else (wmo, 2 * (s - MIX_OUT), KD)
                    n = slot_size(s) // D
                    sp.dma_start(rows(s, n), w[:, bass.ds(l * per + k0, n), :])\
                        .then_inc(sem(f"raw_loaded{s % 4}"), 16)
                ffn_loads(l, 1)
            for t in range(TT):
                sp.wait_ge(sem("out_ready"), t + 1)
                sp.dma_start(out_dram[0, t * P:(t + 1) * P, :], xo[:, t, :]).then_inc(sem("stored"), 16)
            sp.wait_ge(sem("stored"), 16 * TT)
            sp.wait_ge(sem("rows_loaded"), (DEPTH + 1) * (16 * 13))

        @block.scalar
        def _(act):
            def round_w(s, o, l):
                act.wait_ge(*loaded(s, o, l))
                act.wait_ge(*at("w_used", s - 1 + o(4), l))
                n = slot_size(s) // 2
                for h in range(2):
                    nc.scalar.activation(wh[:, s % 2, h * n:(h + 1) * n], raw[:, s % 4, h * n:(h + 1) * n],
                                         ACT.Copy).then_inc(*one("w_hi"))

            def norm_stats(l, n, inc=one):
                nc.scalar.activation(warm[:, :], one_b[:, :], ACT.Sqrt)
                for c in range(KD):
                    act.wait_ge(*at("x_ready", n * KD + c + 1, l))
                    nc.scalar.activation(scr[:, c, :], x[:, c, :], ACT.Square)\
                        .then_inc(*inc("sq_ready"))
                act.wait_ge(*at("sq_used", (n + 1) * KD, l))
                b = NORM_BANK[n]
                nc.scalar.activation(PS[:, b, T:2 * T], PS[:, b, 0:T], ACT.Sqrt, scale=1.0 / D, bias=epsb[:, 0:1])\
                    .then_inc(*inc("rt_ready"))

            def norm(l, n):
                for c in range(KD):
                    act.wait_ge(*at("t_ready", n * KD + c + 1, l))
                    sh = [0, 3, 6][n] * KD + c
                    nc.scalar.activation(hh[:, c, :], scr[:, c, :], ACT.Identity,
                                         bias=mod[:, sh:sh + 1]).then_inc(*one("hh_ready"))

            def ffn(l, f):
                s0, s1 = (FFN1_IN, FFN1_OUT) if f == 0 else (FFN2_IN, FFN2_OUT)
                for s, o in steps(act, s0, KF):
                    j = s - s0
                    round_w(s + 2, o, l)
                    act.wait_ge(*at("w_used", s + 1 + o(4), l))
                    act.wait_ge(*at("hf_ready", f * KF + j - 1 + o(4), l))
                    nc.scalar.activation(sil[:, j % 2, :], PS[:, j % 4, 0:T], ACT.Silu)\
                        .then_inc(*one("sil_ready"))
                for s, o in steps(act, s1, 11, peel=1, tail=2):
                    if s < s1 + 9 or (s == s1 + 9 and f == 0):
                        round_w(s + 2, o, l)

            act.sem_inc(sem("gate_ready"), BEFORE["gate_ready"])
            act.wait_ge(sem("zeroed"), 1)
            act.wait_ge(sem("cT_ready"), 1)
            nc.scalar.activation(cact[:, 0:KD], bank(6)[:, 0:KD], ACT.Silu)
            nc.scalar.activation(cact[:, KD:2 * KD], bank(6)[:, KD:2 * KD], ACT.Copy)\
                .then_inc(sem("cact_ready"), 1)
            for i in range(4):
                act.wait_ge(sem("x_tr"), i + 1)
                for t in range(2):
                    ins = nc.scalar.activation(x[:, 2 * i:2 * i + 2, t * P:(t + 1) * P],
                                               bank(i).rearrange("p (c t n) -> p c t n", c=2, t=2)[:, :, t], ACT.Copy)
            ins.then_inc(sem("x_ready"), KD)
            norm_stats(0, 0, inc=once)
            act.wait_ge(sem("ang_ready"), 1)
            r6 = slice(NOPE, NOPE + ROPE)
            nc.scalar.activation(ang[r6, 2, :], ang[r6, 0, :], ACT.Sin)
            nc.scalar.activation(ang[r6, 3, :], ang[r6, 0, :], ACT.Sin, scale=0.5).then_inc(sem("sin_ready"), 1)

            with act.Fori(0, DEPTH) as l:
                act.wait_ge(*at("vec_rows", 1, l))
                nc.scalar.activation(vec[:, 0:126], bank(0)[:, 0:126], ACT.Copy)
                nc.scalar.activation(vec[:, 126:N_VEC], bank(0)[:, P:P + 6], ACT.Copy)\
                    .then_inc(*one("vec_ready"))
                round_w(0, still, l)
                round_w(1, still, l)
                norm(l, 0)
                ffn(l, 0)
                norm_stats(l, 1)
                round_w(ATT_IN + 1, still, l)
                norm(l, 1)
                for s in range(ATT_IN, RW_IN):
                    round_w(s + 2, still, l)
                    i = s - ATT_IN
                    act.wait_ge(*at("w_used", s + 1, l))
                    b = bank(i)
                    if i < 3:
                        ins = nc.scalar.activation(qk[:, 2 * i:2 * i + 2, :].rearrange("p a b -> p (a b)"), b,
                                                   ACT.Copy)
                    elif s == SLOT_V:
                        ins = nc.scalar.activation(vs[:, :, 0:256], b.rearrange("p (t n) -> p t n", t=2), ACT.Copy)
                    elif i == 4:
                        nc.scalar.activation(vs[:, :, 256:384], b[:, 0:256].rearrange("p (t n) -> p t n", t=2),
                                             ACT.Copy)
                        ins = nc.scalar.activation(cqkv[:, 2, :], b[:, 256:512], ACT.Copy)
                    elif i == 5:
                        ins = nc.scalar.activation(cqkv[:, 0:2, :].rearrange("p a b -> p (a b)"), b, ACT.Copy)
                    else:
                        ins = nc.scalar.activation(krA[NOPE:96, :, :].rearrange("p a b -> p (a b)"),
                                                   b[NOPE:96, :], ACT.Copy)
                    ins.then_inc(*one("att_in"))

                def sb_scores(c):
                    act.wait_ge(*at("sb_scored", c + 1, l))
                    ps = PS[:, 2 * (c % 2):2 * (c % 2) + 2, 0:384]
                    if c >= 2:
                        act.wait_ge(*at("sb_summed", c - 1, l))
                    nc.scalar.activation(sbz[:, c % 2], ps, ACT.Copy, scale=SB_SCALE).then_inc(*one("sb_z"))
                    act.drain()
                    nc.scalar.activation(sbe[:, c % 2], sbz[:, c % 2], ACT.Abs)
                    act.drain()
                    nc.scalar.activation(sbe[:, c % 2], sbe[:, c % 2], ACT.Exp, scale=-1.0)

                def sb_log(c):
                    act.drain()
                    nc.scalar.activation(sbe[:, c % 2], sbe[:, c % 2], ACT.Ln, bias=one_b[:, 0:1])\
                        .then_inc(*one("sb_ln"))

                def sb_weights(c):
                    act.wait_ge(*at("sb_lw", c + 1, l))
                    nc.scalar.activation(sbe[:, c % 2], sbz[:, c % 2], ACT.Exp).then_inc(*one("sb_w"))

                def sb_out(c):
                    act.wait_ge(*at("sb_y", c + 1, l))
                    nc.scalar.activation(yh[:, 3 + c, :], PS[:, 4 + c, 0:T], ACT.Copy)\
                        .then_inc(*one("sb_yh"))

                def rw_in(i):
                    act.wait_ge(*at("w_used", RW_IN + i + 1, l))
                    if i == 0:
                        act.wait_ge(*at("pb_zero", 1, l))
                    if i >= 2:
                        act.wait_ge(*at("shifted", 2 * i - 2, l))
                    nc.scalar.activation(pb[:, i % 2, :, 1:T + 1], PS[:, 7, :].rearrange("p (a b) -> p a b", a=2),
                                         ACT.Copy).then_inc(*one("pb_ready"))
                    round_w(RW_IN + i + 2, still, l)

                act.drain()
                nc.scalar.activation(lat_sq, cqkv[:, :, :], ACT.Square).then_inc(*one("mla_sq"))
                sb_scores(0)
                sb_scores(1)
                sb_log(0)
                sb_log(1)
                rw_in(0)
                sb_weights(0)
                sb_out(0)
                sb_weights(1)
                sb_scores(2)
                sb_log(2)
                rw_in(1)
                sb_out(1)
                act.wait_ge(*at("mla_sum", 1, l))
                nc.scalar.activation(hstat[:, 0, 0:2], PS[:, 6, 0:2], ACT.Sqrt, scale=1.0 / Q_LORA, bias=epsb[:, 0:1])
                nc.scalar.activation(hstat[:, 0, 2:4], PS[:, 6, 2:4], ACT.Sqrt, scale=1.0 / KV_LORA,
                                     bias=epsb[:, 0:1]).then_inc(*one("mla_rt"))
                sb_weights(2)
                rw_in(2)
                sb_out(2)
                rw_in(3)
                for i in range(PAIRS):
                    act.wait_ge(*at("mla_k", i + 1, l))
                    nc.scalar.activation(kT[0:NOPE, 2 * i:2 * i + 2, :].rearrange("p a b -> p (a b)"),
                                         PS[0:NOPE, i, :], ACT.Copy)
                act.wait_ge(*at("mla_v", 1, l))
                for t in range(TT):
                    nc.scalar.activation(vm[:, t, :], PS[:, 6 + t, 0:BW], ACT.Copy).then_inc(*one("mla_kv_ready"))
                for i in range(PAIRS):
                    act.wait_ge(*at("mla_q", i + 1, l))
                    nc.scalar.activation(qT[0:NOPE, 2 * i:2 * i + 2, :].rearrange("p a b -> p (a b)"),
                                         PS[0:NOPE, 3 + (i % 2), :], ACT.Copy).then_inc(*one("mla_qn"))
                for r in range(2):
                    act.wait_ge(*at("mla_scored", r + 1, l))
                    nc.scalar.activation(mls[:, 3 * r:3 * r + 3, :], PS[:, 3 * r:3 * r + 3, 0:384], ACT.Copy,
                                         scale=MLA_SCALE).then_inc(*one("mla_sc"))
                for r in range(2):
                    if r:
                        rw_in(4)
                    act.wait_ge(*at("mla_sub", r + 1, l))
                    for k, ks in enumerate((slice(0, P), slice(P, 384))):
                        for i in range(3):
                            v = mls[:, 3 * r + i, ks]
                            c0 = 3 * k + i
                            ins = nc.scalar.activation(v, v, ACT.Exp, bias=mla_stat[:, r, c0:c0 + 1],
                                                       accum_out=mla_stat[:, r, 6 + c0:7 + c0])
                    ins.then_inc(*one("mla_exp"))


                def mla_out(i):
                    act.wait_ge(*at("mla_y", i + 1, l))
                    nc.scalar.activation(yh[:, 6 + i, :], PS[:, 4 + i, 0:T], ACT.Copy).then_inc(*one("mla_yh"))

                for h in range(HEADS):
                    if h == 3:
                        rw_in(5)
                    act.wait_ge(*at("mla_tr", h + 1, l))
                    nc.scalar.activation(mlp[:, h, :], PS[:, h % 4, 0:384], ACT.Copy).then_inc(*one("mla_p"))
                    if h in (3, 5):
                        mla_out(h // 2 - 1)
                mla_out(2)
                act.wait_ge(*at("shifted", 12, l))
                nc.scalar.activation(ex[0:64, 0, :], m[0:64, 9, :], ACT.Tanh)
                nc.scalar.activation(m[:, 10, :], m[:, 10, :], ACT.Sigmoid)
                nc.scalar.activation(m[96:128, 11, :], m[96:128, 11, :], ACT.Sigmoid).then_inc(*one("lora_in"))
                act.wait_ge(*at("kk0", 1, l))
                nc.scalar.activation(cum[:, :, :], kk[:, :, :], ACT.Square).then_inc(*one("kk_sq"))
                act.wait_ge(*at("wa_done", 1, l))
                for c in range(3):
                    nc.scalar.activation(lw[:, c, :], PS[:, 2 + c // 2, (c % 2) * T:(c % 2 + 1) * T], ACT.Sigmoid,
                                         bias=vec[:, V_W0 + c:V_W0 + c + 1]).then_inc(*one("w_gate"))
                for c in range(3):
                    nc.scalar.activation(av[:, c, :], PS[:, 4 + c // 2, (c % 2) * T:(c % 2 + 1) * T], ACT.Sigmoid,
                                         bias=vec[:, V_A0 + c:V_A0 + c + 1]).then_inc(*one("wa_ready"))
                act.wait_ge(*at("kk_max", 1, l))
                nc.scalar.activation(hstat[:, 0, :], hstat[:, 1, :], ACT.Sqrt).then_inc(*one("kk_rt"))
                act.wait_ge(*at("cum_ready", 1, l))
                nc.scalar.activation(ex[:, :, :], cum[:, :, :], ACT.Exp, scale=-1.0).then_inc(*one("e_neg"))
                act.drain()
                nc.scalar.activation(cum[:, :, :], cum[:, :, :], ACT.Exp).then_inc(*one("e_cum"))
                nc.scalar.activation(lw[:, :, :], lw[:, :, :], ACT.Exp).then_inc(*one("e_prev"))
                act.wait_ge(*at("lora_done", 1, l))
                nc.scalar.activation(g[:, 0:2, :].rearrange("p a b -> p (a b)"), PS[:, 2, :], ACT.Copy)
                nc.scalar.activation(g[:, 2, :], PS[:, 3, 0:T], ACT.Copy).then_inc(*one("g_ready"))
                for tt in range(TT):
                    act.wait_ge(*at("tok_done", tt + 1, l))
                    for i in (0, 1):
                        nc.scalar.activation(tok[:, i, :], PS[:, i, 0:BW], ACT.Copy).then_inc(*one("tok_act"))
                    for b in range(5):
                        for par in range(2):
                            act.wait_ge(*at("z_done", 2 * (5 * tt + b) + par + 1, l))
                            nc.scalar.activation(Z[:, par, :, :].rearrange("p c n -> p (c n)"), PS[:, par, 0:384],
                                                 ACT.Copy).then_inc(*one("z_ready"))
                    act.wait_ge(*at("wt_done", tt + 1, l))
                    nc.scalar.activation(wT[:, :, :].rearrange("p a b -> p (a b)"), PS[:, 4, 0:BW], ACT.Copy)\
                        .then_inc(*one("wt_ready"))
                    act.wait_ge(*at("y_done", tt + 1, l))
                    nc.scalar.activation(ya[:, :, tt * P:(tt + 1) * P],
                                         PS[:, 6, 0:BW].rearrange("p (a b) -> p a b", a=3), ACT.Copy)\
                        .then_inc(*one("ya_ready"))
                act.wait_ge(*at("gn_sub", 1, l))
                nc.scalar.activation(ex[:, :, :], ya[:, :, :], ACT.Square).then_inc(*one("gn_sq"))
                round_w(GATE_IN + 2, still, l)
                act.wait_ge(*at("gn_stat", 1, l))
                nc.scalar.activation(hstat[:, 0, :], PS[:, 7, T:T + 12], ACT.Sqrt, scale=1.0 / HD, bias=gneps[:, 0:1])\
                    .then_inc(*one("gn_rt"))
                round_w(GATE_IN + 3, still, l)

                def gate_out(s, o):
                    j = s - GATE_IN
                    act.wait_ge(*at("w_used", s + 1 + o(4), l))
                    nc.scalar.activation(gates[:, bass.ds(o(8) + 2 * j, 2), :],
                                         PS[:, j % 4, :].rearrange("p (a b) -> p a b", a=2), ACT.Sigmoid)\
                        .then_inc(*one("gate_ready"))

                gate_out(GATE_IN, still)
                gate_out(GATE_IN + 1, still)
                act.wait_ge(*at("ya_final", 1, l))
                nc.scalar.activation(yh[:, 0:3, :], ya[:, :, :], ACT.Copy).then_inc(*one("ya_hi"))
                for s, o in steps(act, GATE_IN, 12, peel=2, tail=2):
                    j = s - GATE_IN
                    if j >= 2:
                        round_w(s + 2, o, l)
                        gate_out(s, o)
                for s in range(BRANCH, FFN2_IN - 1):
                    if s != MIX_OUT - 1:
                        round_w(s + 2, still, l)
                        continue
                    for i in range(4):
                        if i == 2:
                            round_w(s + 2, still, l)
                        act.wait_ge(*at("merged", i + 1, l))
                        nc.scalar.activation(hh[:, 2 * i:2 * i + 2, :], mg[:, 2 * i:2 * i + 2, :], ACT.Copy)\
                            .then_inc(*one("mg_hi"))
                norm_stats(l, 2)
                round_w(FFN2_IN + 1, still, l)
                norm(l, 2)
                ffn(l, 1)
                norm_stats(l, 3)
            for t in range(TT):
                act.wait_ge(sem("out_tr"), t + 1)
                nc.scalar.activation(xo[:, t, :].rearrange("p (a b) -> p a b", a=2), PS[:, 2 * t + 4:2 * t + 6, :],
                                     ACT.Copy).then_inc(sem("out_ready"), 1)

        @block.vector
        def _(dve):
            V = nc.vector

            def split(s, o, l):
                n = slot_size(s) // 2
                for h in range(2):
                    dve.wait_ge(*at("w_hi", 2 * s + h + 1 + o(8), l))
                    V.tensor_tensor(wl[:, s % 2, h * n:(h + 1) * n], raw[:, s % 4, h * n:(h + 1) * n],
                                    wh[:, s % 2, h * n:(h + 1) * n].bitcast(F32), ALU.subtract)\
                        .then_inc(*one("w_split"))

            def norm_root(l, n):
                rb = PS[:, NORM_BANK[n], T:2 * T]
                dve.wait_ge(*at("rt_ready", n + 1, l))
                V.reciprocal(rb, rb)
                dve.drain()

            def norm(l, n):
                rb = PS[:, NORM_BANK[n], T:2 * T]

                def lo(c):
                    dve.wait_ge(*at("hh_ready", n * KD + c + 1, l))
                    sh = [0, 3, 6][n] * KD + c
                    V.scalar_tensor_tensor(hl[:, c, :], scr[:, c, :], mod[:, sh:sh + 1],
                                           hh[:, c, :].bitcast(F32), ALU.add, ALU.subtract)\
                        .then_inc(*one("h_ready"))

                for c in range(KD + 2):
                    if c < KD:
                        V.scalar_tensor_tensor(scr[:, c, :], x[:, c, :], gsc[:, n, c:c + 1], rb,
                                               ALU.mult, ALU.mult).then_inc(*one("t_ready"))
                    if c >= 2:
                        lo(c - 2)

            def evac_out(l, n, gate):
                for c in range(KD):
                    if c % 2 == 0:
                        dve.wait_ge(*(at("out_done", 3 * n + c // 2 + 1, l) if c < KD - 2 else
                                      at("w_used", (FFN1_OUT + 11, MIX_OUT + 4, FFN2_OUT + 11)[n], l)))
                    b = OUT_BANKS[n][c // 2]
                    V.scalar_tensor_tensor(x[:, c, :], PS[:, b, (c % 2) * T:(c % 2 + 1) * T], gate[:, c:c + 1],
                                           x[:, c, :], ALU.mult, ALU.add).then_inc(*one("x_ready"))

            def ffn(l, f):
                s0, s1 = (FFN1_IN, FFN1_OUT) if f == 0 else (FFN2_IN, FFN2_OUT)
                for s, o in steps(dve, s0, KF, *((0, 0), (4, 2))[f]):
                    j = s - s0
                    split(s + 2, o, l)
                    dve.wait_ge(*at("sil_ready", f * KF + j + 1 + o(4), l))
                    dve.wait_ge(*at("hid_ready", f * KF + j - 1 + o(4), l))
                    V.tensor_tensor(hf[:, j % 2, :], PS[:, j % 4, T:2 * T], sil[:, j % 2, :], ALU.mult)\
                        .then_inc(*one("hf_ready"))
                    if f == 0 or 4 <= j < 20:
                        ada((16, 60)[f] + j, o, l)
                for s, o in steps(dve, s1, 11, peel=1, tail=2):
                    j = s - s1
                    if j < 9 or (j == 9 and f == 0):
                        split(s + 2, o, l)
                    if j == 10:
                        continue
                    if 1 <= j <= (10, 8)[f]:
                        ada((37, 79)[f] + j, o, l)

            def ada(n, o, l, inc=one):
                q = n % 4
                dve.drain()
                dve.wait_ge(sem(f"ada_loaded{q}"), l * (18 * 16) + 16 * (n // 4 + 1) + o(16))
                if q == 0 and n:
                    dve.wait_ge(*at("acc_used", n // 4 + o(1), l))
                for k in range(2):
                    w = ada_w[:, q, k * 512:(k + 1) * 512]
                    cc = cact[:, 2 * q + k:2 * q + k + 1]
                    if q == 0 and k == 0:
                        V.tensor_scalar(acc[:, :], w, cc, None, ALU.mult)
                    else:
                        if k:
                            dve.drain()
                        last = V.scalar_tensor_tensor(acc[:, :], w, cc, acc[:, :], ALU.mult, ALU.add)
                last.then_inc(*inc("ada_used"))

            def mod_part(l, lo, hi, groups):
                dve.wait_ge(*at("acc_used", groups, l))
                V.tensor_tensor(mod[:, lo:hi], PS[:, 7, lo:hi], vec[:, V_ADA + lo:V_ADA + hi], ALU.add)
                dve.drain()

            def scales(n):
                sc = mod[:, (3 * n + 1) * KD:(3 * n + 2) * KD]
                return V.scalar_tensor_tensor(gsc[:, n, :], sc, 1.0, vec[:, V_NORM + n * KD:V_NORM + (n + 1) * KD],
                                       ALU.add, ALU.mult)

            def half_gate(n, w):
                return V.tensor_scalar(hgate[:, n, :], mod[:, (3 * n + 2) * KD:(3 * n + 3) * KD], w, None, ALU.mult)

            for name in ("w_split", "hf_ready"):
                dve.sem_inc(sem(name), BEFORE[name])
            V.memset(epsb[:, :], EPS)
            V.memset(gneps[:, :], GN_EPS)
            V.memset(one_b[:, :], 1.0)
            V.memset(vrows[:, :, :], 0.0).then_inc(sem("zeroed"), 1)
            dve.wait_ge(sem("cact_ready"), 1)
            for n in range(16):
                ada(n, still, 0, inc=once)

            with dve.Fori(0, DEPTH) as l:
                norm_root(l, 0)
                dve.wait_ge(*at("vec_ready", 1, l))
                V.tensor_scalar(omka[:, :], vec[:, V_KA:V_KA + 3], -1.0, 1.0, ALU.mult, ALU.add)
                mod_part(l, 0, 16, 4)
                scales(0)
                dve.drain()
                split(0, still, l)
                norm(l, 0)
                split(1, still, l)
                ffn(l, 0)
                mod_part(l, 16, 40, 10)
                scales(1)
                half_gate(0, 0.5)
                dve.drain()
                evac_out(l, 0, hgate[:, 0, :])
                norm_root(l, 1)
                norm(l, 1)
                split(ATT_IN + 1, still, l)
                ada(47, still, l)
                for s in range(ATT_IN, RW_IN):
                    split(s + 2, still, l)
                    if s - ATT_IN < 6:
                        ada(48 + s - ATT_IN, still, l)
                mod_part(l, 40, 52, 13)
                half_gate(1, 1.0).then_inc(*one("mod_mid"))
                mask2 = const(C_SBM).unsqueeze(1).unsqueeze(1).broadcast_to([P, 2, 2, P])

                def diag(t):
                    return t.rearrange("p h (b n) -> p h b n", b=3)[:, :, 0:3:2, :]

                def sb_soft(c):
                    dve.wait_ge(*at("sb_z", c + 1, l))
                    if c >= 2:
                        dve.wait_ge(*at("sb_summed", c - 1, l))
                    V.tensor_scalar(sbs[:, c % 2], sbz[:, c % 2], 0.0, None, ALU.max)
                    dve.drain()
                    dve.wait_ge(*at("sb_ln", c + 1, l))
                    V.tensor_tensor(sbs[:, c % 2], sbs[:, c % 2], sbe[:, c % 2], ALU.add)
                    dve.drain()
                    V.tensor_tensor(diag(sbs[:, c % 2]), diag(sbs[:, c % 2]), mask2, ALU.mult)\
                        .then_inc(*one("sb_sp"))

                def sb_lw(c):
                    dve.wait_ge(*at("sb_summed", c + 1, l))
                    dve.wait_ge(*at("sb_min", c + 1, l))
                    V.tensor_tensor(sbz[:, c % 2], sbz[:, c % 2], PS[:, 2 * (c % 2):2 * (c % 2) + 2, 0:384],
                                    ALU.subtract).then_inc(*one("sb_lw"))

                def sb_lo(c):
                    dve.wait_ge(*at("sb_yh", c + 1, l))
                    V.tensor_tensor(yl[:, 3 + c, :], PS[:, 4 + c, 0:T], yh[:, 3 + c, :].bitcast(F32), ALU.subtract)\
                        .then_inc(*one("sb_yl"))

                def rw_mix(i):
                    for c in (2 * i, 2 * i + 1):
                        dve.wait_ge(*at("shift_d", c + 1, l))
                        V.scalar_tensor_tensor(m[:, c, :], m[:, c, :], vec[:, V_MU + c:V_MU + c + 1],
                                               pb[:, i % 2, c % 2, 1:T + 1], ALU.mult, ALU.add).then_inc(*one("shifted"))

                def rw_in(i):
                    split(RW_IN + i + 2, still, l)
                    if i:
                        rw_mix(i - 1)

                sb_soft(0)
                sb_soft(1)
                rw_in(0)
                sb_lw(0)
                sb_lw(1)
                sb_lo(0)
                sb_soft(2)
                rw_in(1)
                sb_lo(1)
                dve.wait_ge(*at("mla_rt", 1, l))
                V.reciprocal(hstat[:, 1, 0:4], hstat[:, 0, 0:4]).then_inc(*one("mla_rinv"))
                sb_lw(2)
                rw_in(2)
                sb_lo(2)
                dve.wait_ge(*at("mla_rb", 1, l))
                for c in range(3):
                    rb = PS[:, 4 if c < 2 else 5, 0:T]
                    gcol = V_QN + c if c < 2 else V_KVN
                    V.scalar_tensor_tensor(cqkv[:, c, :], cqkv[:, c, :], vec[:, gcol:gcol + 1], rb,
                                           ALU.mult, ALU.mult).then_inc(*one("mla_lat"))
                R = slice(NOPE, 96)
                dve.wait_ge(sem("rope_ready"), 1)
                V.tensor_tensor(rA[R, 0:T], krA[R, 0, :], cosT[R, :], ALU.mult)
                V.tensor_tensor(rB[R, 0:T], krA[R, 1, :], sinT[R, :], ALU.mult)
                dve.drain()
                V.tensor_tensor(kT[R, :, :], rA[R, 0:T].unsqueeze(1).broadcast_to([32, HEADS, T]),
                                rB[R, 0:T].unsqueeze(1).broadcast_to([32, HEADS, T]), ALU.add)
                rw_in(3)
                cos2 = cosT[R, :].unsqueeze(1).broadcast_to([32, 2, T])
                sin2 = sinT[R, :].unsqueeze(1).broadcast_to([32, 2, T])
                for i in range(PAIRS):
                    dve.drain()
                    dve.wait_ge(*at("mla_q", i + 1, l))
                    V.tensor_tensor(rA[R, :].rearrange("p (a b) -> p a b", a=2),
                                    PS[R, 3 + (i % 2), :].rearrange("p (a b) -> p a b", a=2), cos2, ALU.mult)
                    V.tensor_tensor(rB[R, :].rearrange("p (a b) -> p a b", a=2),
                                    PS[R, (5, 2, 5)[i], :].rearrange("p (a b) -> p a b", a=2),
                                    sin2, ALU.mult)
                    dve.drain()
                    V.tensor_tensor(qT[R, 2 * i:2 * i + 2, :].rearrange("p a b -> p (a b)"), rA[R, :], rB[R, :],
                                    ALU.add).then_inc(*one("mla_qr"))
                caus6 = const(C_CAUS).unsqueeze(1).unsqueeze(1).broadcast_to([P, 3, 2, P])

                for r in range(2):
                    dve.wait_ge(*at("mla_sc", r + 1, l))
                    m3 = mls[:, 3 * r:3 * r + 3, :]
                    V.tensor_tensor(diag(m3), diag(m3), caus6, ALU.add)
                    dve.drain()
                    V.tensor_reduce(mla_stat[:, r, 0:3], m3[:, :, 0:P], AX_X, ALU.max)
                    V.tensor_reduce(mla_stat[:, r, 3:6], m3[:, :, P:384], AX_X, ALU.max)
                    dve.drain()
                    V.tensor_scalar(mla_stat[:, r, 0:6], mla_stat[:, r, 0:6], -1.0, None, ALU.mult)\
                        .then_inc(*one("mla_sub"))
                for r in range(2):
                    dve.wait_ge(*at("mla_exp", r + 1, l))
                    V.reciprocal(mla_stat[:, r, 0:6], mla_stat[:, r, 6:12])
                    dve.drain()
                    for k, (lo_, n_) in enumerate(((0, P), (P, 256))):
                        v = mls[:, 3 * r:3 * r + 3, lo_:lo_ + n_]
                        last = V.tensor_tensor(v, v, mla_stat[:, r, 3 * k:3 * k + 3].unsqueeze(2)
                                               .broadcast_to([P, 3, n_]), ALU.mult)
                    last.then_inc(*one("mla_pr"))
                    if r == 0:
                        rw_in(4)
                rw_in(5)
                rw_mix(5)
                dve.drain()
                for c in range(3):
                    last = V.tensor_scalar(kk[:, c, :], kp[:, c, :], vec[:, V_KK + c:V_KK + c + 1], None, ALU.mult)
                last.then_inc(*one("kk0"))
                for i in range(PAIRS):
                    dve.wait_ge(*at("mla_yh", i + 1, l))
                    V.tensor_tensor(yl[:, 6 + i, :], PS[:, 4 + i, 0:T], yh[:, 6 + i, :].bitcast(F32), ALU.subtract)\
                        .then_inc(*one("mla_yl"))
                dve.wait_ge(*at("kk_stat", 1, l))
                V.tensor_scalar(hstat[:, 1, :], PS[:, 0, 0:12], 1e-24, None, ALU.max).then_inc(*one("kk_max"))
                dve.wait_ge(*at("w_gate", 3, l))
                V.tensor_scalar(lw[:, :, :], lw[:, :, :], -float(np.exp(-0.5)), None, ALU.mult)
                dve.drain()
                for c in range(3):
                    V.tensor_tensor_scan(cum[:, c, :], reset, lw[:, c, :], 0.0, ALU.mult, ALU.add)
                dve.drain()
                V.tensor_tensor(lw[:, :, :], cum[:, :, :], lw[:, :, :], ALU.subtract).then_inc(*one("cum_ready"))
                dve.wait_ge(*at("wa_ready", 3, l))
                dve.wait_ge(*at("kk_rt", 1, l))
                V.reciprocal(hstat[:, 1, :], hstat[:, 0, :]).then_inc(*one("kk_rinv"))
                for c in range(3):
                    V.tensor_scalar(bon[:, c, :], av[:, c, :], vec[:, V_KA + c:V_KA + c + 1], omka[:, c:c + 1],
                                    ALU.mult, ALU.add)
                dve.drain()
                V.tensor_tensor(kp, kp, bon[:, :, :], ALU.mult)
                dve.drain()
                for c in range(3):
                    last = V.scalar_tensor_tensor(bon[:, c, :], rr[:, c, :], vec[:, V_RK + c:V_RK + c + 1], kp[:, c, :],
                                                  ALU.mult, ALU.mult)
                last.then_inc(*one("bon_in"))
                dve.wait_ge(*at("kk_rb", 1, l))
                V.tensor_tensor(kk[:, 0:2, :], kk[:, 0:2, :], PS[:, 4, :].rearrange("p (a b) -> p a b", a=2), ALU.mult)
                V.tensor_tensor(kk[:, 2, :], kk[:, 2, :], PS[:, 5, 0:T], ALU.mult)
                dve.drain()
                V.tensor_tensor(av[:, :, :], kk[:, :, :], av[:, :, :], ALU.mult)
                dve.drain()
                dve.wait_ge(*at("e_neg", 1, l))
                V.tensor_tensor(av[:, :, :], av[:, :, :], ex[:, :, :], ALU.mult)
                V.tensor_tensor(kp, kp, ex[:, :, :], ALU.mult)
                dve.wait_ge(*at("e_cum", 1, l))
                V.tensor_tensor(rr, rr, cum[:, :, :], ALU.mult)
                dve.wait_ge(*at("e_prev", 1, l))
                V.scalar_tensor_tensor(kk[:, :, :], kk[:, :, :], -1.0, lw[:, :, :], ALU.mult, ALU.mult)\
                    .then_inc(*one("tilde"))
                V.memset(S[:, :, :], 0.0).then_inc(*one("S_ready"))
                dve.wait_ge(*at("bon_done", 1, l))
                V.tensor_tensor(bon[:, 0:2, :], PS[:, 6, :].rearrange("p (a b) -> p a b", a=2), vv[:, 0:2, :], ALU.mult)
                V.tensor_tensor(bon[:, 2, :], PS[:, 7, 0:T], vv[:, 2, :], ALU.mult).then_inc(*one("bon_ready"))

                def six_mask(n):
                    return const(n).unsqueeze(1).unsqueeze(1).broadcast_to([P, 2, 3, P])

                def two(b):
                    return PS[:, b:b + 2, 0:384].rearrange("p a (c n) -> p a c n", c=3)

                for tt in range(TT):
                    dve.wait_ge(*at("tok_done", tt + 1, l))
                    for i in (2, 3):
                        last = V.tensor_copy(tok[:, i, :], PS[:, i, 0:BW])
                    last.then_inc(*one("tok_dve"))
                    dve.wait_ge(*at("ab_done", 2 * tt + 1, l))
                    V.tensor_tensor(AT[:, :, :, :], two(4), six_mask(C_UP), ALU.mult).then_inc(*one("at_ready"))
                    dve.wait_ge(*at("ab_done", 2 * tt + 2, l))
                    V.tensor_tensor(Tm[:, :, :, :], two(6), six_mask(C_LO1), ALU.mult)
                    dve.drain()
                    V.tensor_tensor(Tm[:, :, :, :], Tm[:, :, :, :], six_mask(C_ID), ALU.add)
                    V.tensor_tensor(TTm[:, :, :, :], AT[:, :, :, :], six_mask(C_UP1), ALU.mult)
                    dve.drain()
                    V.tensor_tensor(TTm[:, :, :, :], TTm[:, :, :, :], six_mask(C_ID), ALU.add).then_inc(*one("T_ready"))
                    for i, (dst, msk) in enumerate(((Aak, C_UP), (Arb, C_UPI), (Ark, C_UPI))):
                        dve.wait_ge(*at("ak_done", 3 * tt + i + 1, l))
                        V.tensor_tensor(dst[:, :, :, :], two((4, 6, 4)[i]), six_mask(msk), ALU.mult)\
                            .then_inc(*one("ak_ready"))
                    for b in range(5):
                        for par in range(2):
                            dve.wait_ge(*at("tz_done", 2 * (5 * tt + b) + par + 1, l))
                            tm, ttm = (v[:, par, :, :].rearrange("p c n -> p (c n)") for v in (Tm, TTm))
                            if b < 4:
                                V.tensor_tensor(tm, tm, PS[:, 2 + par, 0:384], ALU.add)
                            V.tensor_tensor(ttm, ttm, PS[:, 4 + par, 0:384], ALU.add).then_inc(*one("T_ready"))
                    dve.wait_ge(*at("g_done", tt + 1, l))
                    V.tensor_copy(Gm, PS[:, 0, 0:BW]).then_inc(*one("G_ready"))
                    dve.wait_ge(*at("u0_done", tt + 1, l))
                    V.tensor_copy(u0[:, :], PS[:, 1, 0:BW]).then_inc(*one("u0_ready"))
                    for q in (2 * tt, 2 * tt + 1):
                        rows = slice((q % 2) * 64, (q % 2) * 64 + 64)
                        dve.drain()
                        dve.wait_ge(*at("u_done", q + 1, l))
                        V.tensor_tensor(u_[rows, :], PS[rows, 5, 0:BW], u0[rows, :], ALU.add).then_inc(*one("u_ready"))
                        dve.wait_ge(*at("s_done", q + 1, l))
                        V.tensor_tensor(S[:, :, :].rearrange("p a b -> p (a b)"),
                                        S[:, :, :].rearrange("p a b -> p (a b)"), PS[:, 3, 0:BW], ALU.add)
                        dve.drain()
                        dve.wait_ge(*at("pcm_ready", q + 1, l))
                        V.tensor_tensor(S[:, :, :], S[:, :, :], pcm[:, :, :], ALU.mult).then_inc(*one("S_ready"))
                dve.wait_ge(*at("gn_mean", 1, l))
                V.scalar_tensor_tensor(ya[:, 0:2, :], PS[:, 6, :].rearrange("p (a b) -> p a b", a=2), -1.0 / HD,
                                       ya[:, 0:2, :], ALU.mult, ALU.add)
                V.scalar_tensor_tensor(ya[:, 2, :], PS[:, 7, 0:T], -1.0 / HD, ya[:, 2, :], ALU.mult, ALU.add)\
                    .then_inc(*one("gn_sub"))
                split(GATE_IN + 2, still, l)
                dve.wait_ge(*at("gn_rt", 1, l))
                V.reciprocal(hstat[:, 1, :], hstat[:, 0, :]).then_inc(*one("gn_rinv"))
                ada(54, still, l)
                ada(55, still, l)
                split(GATE_IN + 3, still, l)
                dve.wait_ge(*at("gn_rb", 1, l))
                for c in range(3):
                    V.scalar_tensor_tensor(ya[:, c, :], ya[:, c, :], vec[:, V_LG + c:V_LG + c + 1],
                                           PS[:, 4 + c // 2, (c % 2) * T:(c % 2 + 1) * T], ALU.mult, ALU.mult)
                dve.drain()
                for c in range(3):
                    V.scalar_tensor_tensor(ya[:, c, :], ya[:, c, :], vec[:, V_LB + c:V_LB + c + 1], bon[:, c, :],
                                           ALU.add, ALU.add)
                dve.drain()
                V.tensor_tensor(ya[:, :, :], ya[:, :, :], g[:, :, :], ALU.mult).then_inc(*one("ya_final"))
                dve.wait_ge(*at("ya_hi", 1, l))
                V.tensor_tensor(yl[:, 0:3, :], ya[:, :, :], yh[:, 0:3, :].bitcast(F32), ALU.subtract)\
                    .then_inc(*one("ya_lo"))
                for s, o in steps(dve, GATE_IN, 12, peel=2, tail=2):
                    j = s - GATE_IN
                    if j == 11:
                        mod_part(l, 52, 64, 16)
                        scales(2).then_inc(*one("mod_done"))
                    if j >= 2:
                        split(s + 2, o, l)
                    if 2 <= j < 10:
                        ada(54 + j, o, l)
                dve.wait_ge(*at("gate_ready", 12, l))

                def merge(n, i):
                    dve.wait_ge(*(at("br_done", (0, 4, 7)[n] + i + 1, l) if n == 0 or i < 3 else
                                  at("w_used", BRANCH + (3, 5)[n - 1], l)))
                    ps = PS[:, BR_BANKS[n] + i, :].rearrange("p (a b) -> p a b", a=2)
                    gt = gates[:, n * KD + 2 * i:n * KD + 2 * i + 2, :]
                    if n == 0:
                        V.tensor_tensor(mg[:, 2 * i:2 * i + 2, :], ps, gt, ALU.mult).then_inc(*one("br_used"))
                        return
                    t = mt[:, 2 * (i % 2):2 * (i % 2) + 2, :]
                    V.tensor_tensor(t, ps, gt, ALU.mult).then_inc(*one("br_used"))
                    dve.drain()
                    ins = V.tensor_tensor(mg[:, 2 * i:2 * i + 2, :], mg[:, 2 * i:2 * i + 2, :], t, ALU.add)
                    if n == 2:
                        ins.then_inc(*one("merged"))

                def merged_lo(i):
                    dve.wait_ge(*at("mg_hi", i + 1, l))
                    V.tensor_tensor(hl[:, 2 * i:2 * i + 2, :], mg[:, 2 * i:2 * i + 2, :],
                                    hh[:, 2 * i:2 * i + 2, :].bitcast(F32), ALU.subtract).then_inc(*one("mg_lo"))

                split(BRANCH + 2, still, l)
                for i in range(4):
                    merge(0, i)
                split(BRANCH + 3, still, l)
                merge(1, 0)
                merge(1, 1)
                split(BRANCH + 4, still, l)
                merge(1, 2)
                merge(1, 3)
                merge(2, 0)
                split(MIX_OUT, still, l)
                merged_lo(0)
                merge(2, 1)
                merged_lo(1)
                split(MIX_OUT + 1, still, l)
                merge(2, 2)
                merge(2, 3)
                merged_lo(2)
                merged_lo(3)
                for s in range(MIX_OUT + 2, FFN2_IN + 1):
                    split(s, still, l)
                evac_out(l, 1, hgate[:, 1, :])
                norm_root(l, 2)
                norm(l, 2)
                split(FFN2_IN + 1, still, l)
                ffn(l, 1)
                mod_part(l, 64, 72, 22)
                half_gate(2, 0.5)
                dve.drain()
                evac_out(l, 2, hgate[:, 2, :])
            norm_root(DEPTH, 0)
            for c in range(KD):
                V.scalar_tensor_tensor(x[:, c, :], x[:, c, :], cact[:, KD + c:KD + c + 1], PS[:, 3, T:2 * T],
                                       ALU.mult, ALU.mult).then_inc(sem("y_ready"), 1)

        @block.gpsimd
        def _(pool):
            G = nc.gpsimd

            def ffn(l, f):
                s0 = FFN1_IN if f == 0 else FFN2_IN
                for s, o in steps(pool, s0, KF):
                    j = s - s0
                    pool.wait_ge(*at("hf_ready", f * KF + j + 1 + o(4), l))
                    dh = hidh[:, bass.ds(o(4) + j, 1), :].rearrange("p a b -> p (a b)")
                    dl = hidl[:, bass.ds(o(4) + j, 1), :].rearrange("p a b -> p (a b)")
                    pool.sem_inc(sem("pool_on"), 1)
                    G.tensor_copy(dh, hf[:, j % 2, :])
                    pool.drain()
                    G.tensor_tensor(dl, hf[:, j % 2, :], dh.bitcast(F32), ALU.subtract).then_inc(*one("hid_ready"))

            pool.sem_inc(sem("hid_ready"), BEFORE["hid_ready"])
            r6 = slice(NOPE, NOPE + ROPE)
            rc = C_ROPE * P
            pool.wait_ge(sem("pos_loaded"), 16)
            pool.wait_ge(sem("cst_loaded"), 16)
            G.tensor_copy(ang[r6, 1, :], posi[r6, :])
            pool.drain()
            G.tensor_scalar(ang[r6, 0, :], ang[r6, 1, :], cst[r6, rc:rc + 1], None, ALU.mult)
            pool.drain()
            magic = 1.5 * 2.0 ** 23
            G.tensor_scalar(ang[r6, 1, :], ang[r6, 0, :], 1.0 / (2 * np.pi), magic, ALU.mult, ALU.add)
            pool.drain()
            G.tensor_scalar(ang[r6, 1, :], ang[r6, 1, :], magic, None, ALU.subtract)
            c1 = 6.28125
            c2 = 0.0019350051879882812
            c3 = 2 * np.pi - c1 - c2
            for cc in (c1, c2, c3):
                pool.drain()
                G.tensor_scalar(ang[r6, 2, :], ang[r6, 1, :], cc, None, ALU.mult)
                pool.drain()
                G.tensor_tensor(ang[r6, 0, :], ang[r6, 0, :], ang[r6, 2, :], ALU.subtract)
            pool.drain()
            G.tensor_scalar(ang[r6, 0, :], ang[r6, 0, :], 3.1415925, -3.1415925, ALU.min, ALU.max)\
                .then_inc(sem("ang_ready"), 1)
            pool.wait_ge(sem("sin_ready"), 1)
            G.tensor_scalar(sinT[r6, :], ang[r6, 2, :], cst[r6, rc + 1:rc + 2], None, ALU.mult)
            G.tensor_tensor(ang[r6, 1, :], ang[r6, 3, :], ang[r6, 3, :], ALU.mult)
            pool.drain()
            G.tensor_scalar(cosT[r6, :], ang[r6, 1, :], -2.0, 1.0, ALU.mult, ALU.add).then_inc(sem("rope_ready"), 1)
            pool.drain()
            with pool.Fori(0, DEPTH) as l:
                ffn(l, 0)
                pool.wait_ge(*at("att_in", 7, l))
                pool.sem_inc(sem("pool_on"), 1)
                mn = const(C_MIN).unsqueeze(1).unsqueeze(1).broadcast_to([P, 2, 2, P])
                G.memset(pb[:, :, :, 0:1], 0.0).then_inc(*one("pb_zero"))

                def sb_mask(c):
                    pool.wait_ge(*at("sb_sp", c + 1, l))
                    z = sbz[:, c % 2].rearrange("p h (b n) -> p h b n", b=3)[:, :, 0:3:2, :]
                    G.tensor_tensor(z, z, mn, ALU.add).then_inc(*one("sb_min"))

                def rw_diff(i):
                    pool.wait_ge(*at("pb_ready", i + 1, l))
                    for c in (2 * i, 2 * i + 1):
                        G.tensor_tensor(m[:, c, :], pb[:, i % 2, c % 2, 0:T], pb[:, i % 2, c % 2, 1:T + 1],
                                        ALU.subtract).then_inc(*one("shift_d"))

                sb_mask(0)
                sb_mask(1)
                rw_diff(0)
                sb_mask(2)
                for i in range(1, 6):
                    rw_diff(i)
                pool.wait_ge(*at("e_cum", 1, l))
                for tt in range(TT):
                    pool.wait_ge(*at("at_ready", tt + 1, l))
                    for b in range(5):
                        if b:
                            pool.wait_ge(*at("z_done", 2 * (5 * tt + b), l))
                        G.tensor_tensor(X[:, :, :, :], AT[:, :, :, :],
                                        const(LEVELS[b]).unsqueeze(1).unsqueeze(1).broadcast_to([P, 2, 3, P]),
                                        ALU.mult).then_inc(*one("X_ready"))
                    for q in (2 * tt, 2 * tt + 1):
                        if q:
                            pool.wait_ge(*at("S_ready", q + 1, l))
                        G.tensor_tensor(pcm[:, :, :],
                                        const(C_BLK).unsqueeze(1).broadcast_to([P, 3, P]),
                                        cum[:, :, 64 * q + 63:64 * q + 64].broadcast_to([P, 3, P]), ALU.mult)\
                            .then_inc(*one("pcm_ready"))
                ffn(l, 1)

        @block.tensor
        def _(pe):
            M = nc.tensor.matmul

            def mm3(out, wsl, rhs_h, rhs_l, start, stop):
                M(out, wh[(slice(None),) + wsl], rhs_h, start=start, stop=False, skip_group_check=True)
                M(out, wh[(slice(None),) + wsl], rhs_l, start=False, stop=False, skip_group_check=True)
                return M(out, wl[(slice(None),) + wsl], rhs_h, start=False, stop=stop, skip_group_check=True)

            def first_slot(s, b, h0, l):
                split_ready(s, 1, still, l)
                for k in range(KD):
                    pe.wait_ge(*at("h_ready", h0 + k + 1, l))
                    for half in range(2):
                        w0 = (half * KD + k) * P
                        ins = mm3(PS[:, b, half * T:(half + 1) * T], (s % 2, slice(w0, w0 + P)), hh[:, k, :],
                                  hl[:, k, :], k == 0 and half == 0, k == KD - 1)
                return ins

            def in_tile(s, half, b, col, n=P):
                for k in range(KD):
                    w0 = (half * KD + k) * n
                    last = mm3(PS[0:n, b, col:col + T], (s % 2, slice(w0, w0 + n)), hh[:, k, :], hl[:, k, :],
                               k == 0, k == KD - 1)
                return last

            def split_ready(s, half, o, l):
                pe.wait_ge(*at("w_split", 2 * s + half + 1 + o(8), l))

            def row_slot(s, banks, first, last_, moving, l, o):
                for k in range(2):
                    split_ready(s, k, o, l)
                    for c in range(KD):
                        w0 = k * D + c * P
                        rh, rl = moving(k)
                        ins = mm3(PS[:, banks[c // 2], (c % 2) * T:(c % 2 + 1) * T], (s % 2, slice(w0, w0 + P)),
                                  rh, rl, first and k == 0 and c % 2 == 0, last_ and k == 1)
                        if last_ and k == 1 and c % 2 and c < KD - 1:
                            ins.then_inc(*one("out_done"))
                ins.then_inc(*one("w_used"))

            def tok_mm(out, k, t, wsl):
                ts = slice(t * P, (t + 1) * P)
                w = (slice(None),) + wsl
                M(out, hh[:, k, ts], wh[w], start=(k == 0), stop=False)
                M(out, hl[:, k, ts], wh[w], start=False, stop=False)
                return M(out, hh[:, k, ts], wl[w], start=False, stop=(k == KD - 1))

            def norm(l, n, inc=one):
                for c in range(KD):
                    pe.wait_ge(*at("sq_ready", n * KD + c + 1, l))
                    M(PS[:, NORM_BANK[n], 0:T], ones, scr[:, c, :], start=(c == 0), stop=(c == KD - 1))\
                        .then_inc(*inc("sq_used"))

            def ada_sum(gr, l, o=still, inc=one):
                col = 4 * ada_place(4 * gr, 0)[1]
                pe.wait_ge(*at("ada_used", 4 * gr + 4 + o(4), l))
                for i in range(4):
                    ins = M(PS[:, 7, bass.ds(o(4) + col + i, 1)], acc[:, i * P:(i + 1) * P], onecol,
                            start=True, stop=True)
                ins.then_inc(*inc("acc_used"))

            def ffn(l, f):
                s0, s1 = (FFN1_IN, FFN1_OUT) if f == 0 else (FFN2_IN, FFN2_OUT)
                for s, o in steps(pe, s0, KF, peel=(2, 6)[f]):
                    j = s - s0
                    pe.wait_ge(*at("hf_ready", f * KF + j - 3 + o(4), l))
                    if j == 0:
                        ins = first_slot(s, 0, f * 2 * KD, l)
                    for half in range(2) if j else ():
                        split_ready(s, half, o, l)
                        ins = in_tile(s, half, j % 4, half * T)
                    ins.then_inc(*one("w_used"))
                    if f == 0 and j % 4 == 0 and j >= 4:
                        ada_sum(3 + j // 4, l, o)
                    if f == 1 and j % 4 == 0 and j >= 8:
                        ada_sum(14 + j // 4, l, o)
                for s, o in steps(pe, s1, 11, *((1, 2), (2, 1))[f]):
                    j = s - s1
                    pe.wait_ge(*at("hid_ready", f * KF + 2 * j + 2 + o(8), l))
                    if s == s1:
                        pe.wait_ge(*at("hid_ready", f * KF + 19, l))

                    def moving(k):
                        r = bass.ds(o(8) + 2 * j + k, 1)
                        return (hidh[:, r, :].rearrange("p a b -> p (a b)"),
                                hidl[:, r, :].rearrange("p a b -> p (a b)"))

                    row_slot(s, OUT_BANKS[2 * f], s == s1, s == s1 + 10, moving, l, o)
                    if j == (3, 5)[f]:
                        ada_sum((9, 20)[f], l, o)

            for name in ("w_used", "lora_done"):
                pe.sem_inc(sem(name), BEFORE[name])
            pe.wait_ge(sem("cst_loaded"), 16)
            pe.wait_ge(sem("c_loaded"), 32)
            pe.wait_ge(sem("zeroed"), 1)
            nc.tensor.transpose(PS[:, 6, 0:P], vrows[:, 0, :], ident).then_inc(sem("cT_ready"), 1)
            pe.wait_ge(sem("x_loaded"), 16)
            for i in range(4):
                for c in (2 * i, 2 * i + 1):
                    for t in range(TT):
                        col = ((c % 2) * 2 + t) * P
                        ins = nc.tensor.transpose(PS[:, i, col:col + P], xin[:, t, c * P:(c + 1) * P], ident)
                ins.then_inc(sem("x_tr"), 1)
            pe.wait_ge(sem("cact_ready"), 1)
            for gr in range(4):
                ada_sum(gr, 0, inc=once)
                if gr == 1:
                    norm(0, 0, inc=once)

            with pe.Fori(0, DEPTH) as l:
                pe.wait_ge(sem("rows_loaded"), (l + 1) * (16 * 13))
                pe.wait_ge(*at("x_ready", KD, l))
                nc.tensor.transpose(PS[:, 0, 0:P], vrows[:, 0, :], ident)
                nc.tensor.transpose(PS[:, 0, P:2 * P], vrows[:, 1, :], ident).then_inc(*one("vec_rows"))
                ffn(l, 0)
                norm(l, 1)
                for s in range(ATT_IN, RW_IN):
                    i = s - ATT_IN
                    split_ready(s, 1, still, l)
                    if s == SLOT_V:
                        for t in range(TT):
                            for k in range(KD):
                                ins = tok_mm(PS[:, i, t * 256:(t + 1) * 256], k, t,
                                             (s % 2, slice(k * 256, (k + 1) * 256)))
                    elif i == 4:
                        for t in range(TT):
                            for k in range(KD):
                                tok_mm(PS[:, i, t * P:(t + 1) * P], k, t, (s % 2, slice(k * P, (k + 1) * P)))
                        ins = in_tile(s, 1, i, T)
                    elif i == 0:
                        ins = first_slot(s, i, KD, l)
                    else:
                        n = 96 if s == SLOT_KR else P
                        in_tile(s, 0, i, 0, n)
                        ins = in_tile(s, 1, i, T, n)
                    ins.then_inc(*one("w_used"))
                    if i in (1, 5):
                        ada_sum(11 + i // 4, l)
                pe.wait_ge(*at("att_in", 7, l))

                def sb_scores(c):
                    if c == 2:
                        pe.wait_ge(*at("sb_lw", 1, l))
                    for h in range(2):
                        r = slice(64 * h, 64 * h + 64)
                        b = 2 * (c % 2) + h
                        q, k = qk[:, c, :], qk[:, 3 + c, :]
                        M(PS[:, b, 0:T], k[r, 0:P], q[r, :], start=True, stop=True)
                        ins = M(PS[:, b, T:384], k[r, P:T], q[r, P:T], start=True, stop=True)
                    ins.then_inc(*one("sb_scored"))

                def sb_sum(c):
                    pe.wait_ge(*at("sb_sp", c + 1, l))
                    pe.wait_ge(*at("sb_ln", c + 1, l))
                    for h in range(2):
                        b = 2 * (c % 2) + h
                        s0, s1 = sbs[:, c % 2, h, 0:T], sbs[:, c % 2, h, T:384]
                        M(PS[:, b, 0:T], const(C_TRI), s0, start=True, stop=False, skip_group_check=True)
                        M(PS[:, b, P:T], ones, s1, start=False, stop=True, skip_group_check=True)
                        ins = M(PS[:, b, T:384], const(C_TRI), s1, start=False, stop=True, skip_group_check=True)
                    ins.then_inc(*one("sb_summed"))

                def sb_y(c):
                    pe.wait_ge(*at("sb_w", c + 1, l))
                    for h in range(2):
                        r = slice(64 * h, 64 * h + 64)
                        hc = slice((2 * c + h) * 64, (2 * c + h) * 64 + 64)
                        M(PS[r, 4 + c, 0:T], vs[:, 0, hc], sbe[:, c % 2, h, 0:T], start=True, stop=False,
                          skip_group_check=True)
                        ins = M(PS[r, 4 + c, P:T], vs[:, 1, hc], sbe[:, c % 2, h, T:384], start=False, stop=True,
                                skip_group_check=True)
                    ins.then_inc(*one("sb_y"))

                def rw_in(i):
                    s = RW_IN + i
                    if i == 0:
                        pe.wait_ge(*at("mod_mid", 1, l))
                    else:
                        pe.wait_ge(*at("pb_ready", i, l))
                    split_ready(s, 1, still, l)
                    in_tile(s, 0, 7, 0)
                    in_tile(s, 1, 7, T).then_inc(*one("w_used"))

                sb_scores(0)
                sb_scores(1)
                rw_in(0)
                sb_sum(0)
                sb_sum(1)
                rw_in(1)
                sb_y(0)
                sb_scores(2)
                sb_y(1)
                pe.wait_ge(*at("mla_sq", 1, l))
                for i, (c, st, sp_) in enumerate(((0, True, False), (1, False, True), (2, True, True))):
                    for t in range(TT):
                        col = t if c < 2 else 2 + t
                        ins = M(PS[:, 6, col:col + 1], lat_sq[:, c, t * P:(t + 1) * P], onecol, start=(i == 0 and t == 0),
                                stop=sp_, skip_group_check=True)
                ins.then_inc(*one("mla_sum"))
                rw_in(2)
                sb_sum(2)
                pe.wait_ge(*at("mla_rt", 1, l))
                sb_y(2)
                pe.wait_ge(*at("mla_rinv", 1, l))
                pe.wait_ge(*at("sb_yl", 2, l))
                for i in range(2):
                    for t in range(TT):
                        ins = M(PS[:, 4 + i, t * P:(t + 1) * P],
                                hstat[:, 1, 2 * i + t:2 * i + t + 1].broadcast_to([P, P]), ident, start=True, stop=True)
                ins.then_inc(*one("mla_rb"))
                rw_in(3)
                pe.wait_ge(*at("mla_lat", 3, l))
                pe.wait_ge(sem("small_loaded"), (l + 1) * (16 * 10))
                for i in range(PAIRS):
                    for h in range(2):
                        c0 = (2 * i + h) * P
                        ins = M(PS[0:NOPE, i, h * T:(h + 1) * T], w_ukv[:, c0:c0 + NOPE], cqkv[:, 2, :],
                                start=True, stop=True)
                    ins.then_inc(*one("mla_k"))
                pe.wait_ge(*at("sb_yl", 3, l))
                pe.wait_ge(*at("pb_ready", 4, l))
                vcols = w_ukv[:, :].rearrange("p (h n) -> p h n", h=HEADS)[:, :, NOPE:P]
                for t in range(TT):
                    ins = M(PS[:, 6 + t, 0:BW], cqkv[:, 2, t * P:(t + 1) * P], vcols, start=True, stop=True)
                ins.then_inc(*one("mla_v"))
                for i in range(PAIRS):
                    if i == 1:
                        pe.wait_ge(*at("mla_kv_ready", 2, l))
                    if i == 2:
                        pe.wait_ge(*at("mla_qr", 1, l))
                        pe.wait_ge(*at("mla_qn", 1, l))
                    for h in range(2):
                        hd = 2 * i + h
                        for k in range(2):
                            M(PS[0:96, 3 + (i % 2), h * T:(h + 1) * T], w_uq[:, k, hd * 96:(hd + 1) * 96], cqkv[:, k, :],
                              start=(k == 0), stop=(k == 1))
                        for k in range(2):
                            ins = M(PS[NOPE:96, (5, 2, 5)[i], h * T:(h + 1) * T], w_sw[:, k, hd, :], cqkv[:, k, :],
                                    start=(k == 0), stop=(k == 1))
                    ins.then_inc(*one("mla_q"))
                pe.wait_ge(*at("mla_kv_ready", 2, l))
                pe.wait_ge(*at("mla_qr", 3, l))
                pe.wait_ge(*at("mla_qn", 3, l))
                for r in range(2):
                    for i in range(3):
                        h = 3 * r + i
                        M(PS[:, h, 0:P], qT[0:96, h, 0:P], kT[0:96, h, 0:P], start=True, stop=True)
                        ins = M(PS[:, h, P:384], qT[0:96, h, P:T], kT[0:96, h, :], start=True, stop=True)
                    ins.then_inc(*one("mla_scored"))
                rw_in(4)
                def mla_y(h):
                    pe.wait_ge(*at("mla_p", h + 1, l))
                    r = slice(64 * (h % 2), 64 * (h % 2) + 64)
                    M(PS[r, 4 + h // 2, 0:T], vm[:, 0, h * 64:(h + 1) * 64], mlp[:, h, 0:T], start=True, stop=False,
                      skip_group_check=True)
                    ins = M(PS[r, 4 + h // 2, P:T], vm[:, 1, h * 64:(h + 1) * 64], mlp[:, h, T:384], start=False,
                            stop=True, skip_group_check=True)
                    if h % 2:
                        ins.then_inc(*one("mla_y"))

                pe.wait_ge(*at("mla_sc", 2, l))
                for h in range(HEADS):
                    if h == 3:
                        rw_in(5)
                    if h % 3 == 0:
                        pe.wait_ge(*at("mla_pr", h // 3 + 1, l))
                    if h >= 4:
                        pe.wait_ge(*at("mla_p", h - 3, l))
                    for j in range(3):
                        ins = nc.tensor.transpose(PS[:, h % 4, j * P:(j + 1) * P], mls[:, h, j * P:(j + 1) * P], ident)
                    ins.then_inc(*one("mla_tr"))
                    if h:
                        mla_y(h - 1)
                mla_y(HEADS - 1)
                def head_stats(src, name, b, col0=0):
                    for c in range(3):
                        for t in range(TT):
                            col = col0 + (t * 3 + c) * 2
                            ins = M(PS[:, b, col:col + 2], src[:, c, t * P:(t + 1) * P], blk2, start=True, stop=True)
                    ins.then_inc(*one(name))

                pe.wait_ge(*at("lora_in", 1, l))
                pe.wait_ge(*at("mla_yl", 3, l))
                for c in range(3):
                    cs, col = slice(c * P, (c + 1) * P), slice((c % 2) * T, (c % 2 + 1) * T)
                    M(PS[:, 2 + c // 2, col], lora[0:64, cs], ex[0:64, 0, :], start=True, stop=True)
                    ins = M(PS[:, 4 + c // 2, col], lora[64:128, cs], m[64:128, 9, :], start=True, stop=True)
                ins.then_inc(*one("wa_done"))
                pe.wait_ge(*at("kk_sq", 1, l))
                head_stats(cum, "kk_stat", 0)
                def head_spread(name):
                    for c in range(3):
                        for t in range(TT):
                            col = (t * 3 + c) * 2
                            o = (c % 2) * T + t * P
                            for h in range(2):
                                w = hstat[:, 1, col + h:col + h + 1].broadcast_to([P, 64])
                                ins = M(PS[64 * h:64 * h + 64, 4 + c // 2, o:o + P], w, ident, start=True, stop=True)
                    ins.then_inc(*one(name))

                pe.wait_ge(*at("wa_ready", 3, l))
                pe.wait_ge(*at("kk_rinv", 1, l))
                head_spread("kk_rb")
                pe.wait_ge(*at("bon_in", 1, l))
                for c in range(3):
                    ins = M(PS[:, 6 + c // 2, (c % 2) * T:(c % 2 + 1) * T], blk, bon[:, c, :], start=True, stop=True)
                ins.then_inc(*one("bon_done"))
                for c in range(3):
                    cs, col = slice(c * P, (c + 1) * P), slice((c % 2) * T, (c % 2 + 1) * T)
                    M(PS[:, 2 + c // 2, col], lora_g[:, 0, cs], m[:, 10, :], start=True, stop=False)
                    ins = M(PS[:, 2 + c // 2, col], lora_g[96:128, 1, cs], m[96:128, 11, :], start=False, stop=True)
                ins.then_inc(*one("lora_done"))
                pe.wait_ge(*at("g_ready", 1, l))
                pe.wait_ge(*at("tilde", 1, l))

                def A(dst, lhs, rhs, tt, name):
                    ts = slice(tt * P, (tt + 1) * P)
                    for par in range(2):
                        r = slice(64 * par, 64 * par + 64)
                        for c in range(3):
                            ins = M(PS[:, dst + par, c * P:(c + 1) * P], lhs[:, c, ts][r], rhs[:, c, ts][r],
                                    start=True, stop=True)
                    ins.then_inc(*one(name))

                for tt in range(TT):
                    ts = slice(tt * P, (tt + 1) * P)
                    pe.wait_ge(*at("S_ready", 2 * tt + 1, l))
                    for i, src in enumerate((kk, av, kp, vv)):
                        for c in range(3):
                            ins = nc.tensor.transpose(PS[:, i, c * P:(c + 1) * P], src[:, c, ts], ident)
                    ins.then_inc(*one("tok_done"))
                    A(4, av, kk, tt, "ab_done")
                    if tt:
                        pe.wait_ge(*at("ya_ready", tt, l))
                    if tt == 0:
                        pe.wait_ge(*at("bon_ready", 1, l))
                    A(6, kk, av, tt, "ab_done")
                    pe.wait_ge(*at("at_ready", tt + 1, l))
                    A(4, kp, kk, tt, "ak_done")
                    pe.wait_ge(*at("T_ready", 11 * tt + 1, l))
                    A(6, av, rr, tt, "ak_done")
                    pe.wait_ge(*at("ak_ready", 3 * tt + 1, l))
                    A(4, kp, rr, tt, "ak_done")
                    pe.wait_ge(*at("tok_act", 2 * tt + 2, l))
                    pe.wait_ge(*at("tok_dve", tt + 1, l))
                    for b in range(5):
                        pe.wait_ge(*at("X_ready", 5 * tt + b + 1, l))
                        for par in range(2):
                            pe.wait_ge(*at("T_ready", 11 * tt + (2 * b + par if b else 1), l))
                            for c in range(3):
                                ins = M(PS[:, par, c * P:(c + 1) * P], X[:, par, c, :], Tm[:, par, c, :], start=True,
                                        stop=True)
                            ins.then_inc(*one("z_done"))
                        for par in range(2):
                            pe.wait_ge(*at("z_ready", 2 * (5 * tt + b) + par + 1, l))
                            if b == 0:
                                pe.wait_ge(*at("ak_ready", 3 * tt + 3, l))
                            for c in range(3):
                                if b < 4:
                                    M(PS[:, 2 + par, c * P:(c + 1) * P], TTm[:, par, c, :], Z[:, par, c, :],
                                      start=True, stop=True)
                                ins = M(PS[:, 4 + par, c * P:(c + 1) * P], Z[:, par, c, :], TTm[:, par, c, :],
                                        start=True, stop=True)
                            ins.then_inc(*one("tz_done"))
                    for h in range(HEADS):
                        hc = slice(h * 64, h * 64 + 64)
                        ins = M(PS[:, 0, hc], Aak[:, h % 2, h // 2, :], tok[:, 3, hc], start=True, stop=True)
                    ins.then_inc(*one("g_done"))
                    pe.wait_ge(*at("T_ready", 11 * tt + 11, l))
                    for h in range(HEADS):
                        r = slice(64 * (h % 2), 64 * (h % 2) + 64)
                        ins = M(PS[r, 4, (h // 2) * P:(h // 2 + 1) * P], tok[:, 0, h * 64:h * 64 + 64],
                                TTm[:, h % 2, h // 2, :], start=True, stop=True)
                    ins.then_inc(*one("wt_done"))
                    pe.wait_ge(*at("G_ready", tt + 1, l))
                    for h in range(HEADS):
                        hc = slice(h * 64, h * 64 + 64)
                        ins = M(PS[:, 1, hc], TTm[:, h % 2, h // 2, :], Gm[:, hc], start=True, stop=True)
                    ins.then_inc(*one("u0_done"))
                    pe.wait_ge(*at("wt_ready", tt + 1, l))
                    for q in (2 * tt, 2 * tt + 1):
                        rows = slice(64 * (q % 2), 64 * (q % 2) + 64)
                        pe.wait_ge(*at("S_ready", q + 1, l))
                        for c in range(3):
                            ins = M(PS[:, 5, c * P:(c + 1) * P], wT[:, c, :], S[:, c, :], start=True, stop=True)
                        ins.then_inc(*one("u_done"))
                        for c in range(3):
                            o = c * P + 64 * (q % 2)
                            M(PS[:, 6, o:o + 64], S[:, c, :], rr[:, c, q * 64:q * 64 + 64],
                              start=(q % 2 == 0 and c == 0), stop=False, skip_group_check=True)
                        pe.wait_ge(*at("u_ready", q + 1, l))
                        for c in range(3):
                            cs = slice(c * P, (c + 1) * P)
                            M(PS[:, 3, cs], tok[rows, 1, cs], u_[rows, cs], start=True, stop=False)
                            ins = M(PS[:, 3, cs], tok[rows, 2, cs], tok[rows, 3, cs], start=False, stop=True)
                        ins.then_inc(*one("s_done"))
                    for h in range(HEADS):
                        r = slice(64 * (h % 2), 64 * (h % 2) + 64)
                        cs, hc = slice((h // 2) * P, (h // 2 + 1) * P), slice(h * 64, h * 64 + 64)
                        M(PS[r, 6, cs], u_[:, hc], Arb[:, h % 2, h // 2, :], start=False, stop=False,
                          skip_group_check=True)
                        ins = M(PS[r, 6, cs], tok[:, 3, hc], Ark[:, h % 2, h // 2, :], start=False, stop=True,
                                skip_group_check=True)
                    ins.then_inc(*one("y_done"))
                pe.wait_ge(*at("ya_ready", 2, l))
                for c in range(3):
                    ins = M(PS[:, 6 + c // 2, (c % 2) * T:(c % 2 + 1) * T], blk, ya[:, c, :], start=True, stop=True)
                ins.then_inc(*one("gn_mean"))

                def gate_slot(s, o):
                    j = s - GATE_IN
                    pe.wait_ge(*at("gate_ready", j - 3 + o(4), l))
                    for half in range(2):
                        split_ready(s, half, o, l)
                        ins = in_tile(s, half, j % 4, half * T)
                    ins.then_inc(*one("w_used"))

                gate_slot(GATE_IN, still)
                pe.wait_ge(*at("gn_sq", 1, l))
                head_stats(ex, "gn_stat", 7, T)
                gate_slot(GATE_IN + 1, still)
                pe.wait_ge(*at("gn_rinv", 1, l))
                head_spread("gn_rb")
                for s, o in steps(pe, GATE_IN, 12, peel=2, tail=2):
                    j = s - GATE_IN
                    if j < 2:
                        continue
                    gate_slot(s, o)
                    if j % 4 == 2:
                        ada_sum(13 + j // 4, l, o)
                pe.wait_ge(*at("mod_done", 1, l))
                pe.wait_ge(*at("ya_lo", 1, l))
                for kb in range(9):
                    n, k = kb // 3, kb % 3
                    s = BRANCH + kb // 2
                    split_ready(s, kb % 2 if kb < 8 else 1, still, l)
                    if n == 1 and k == 0:
                        pe.wait_ge(*at("gate_ready", 12, l))
                    if n == 2 and k == 0:
                        pe.wait_ge(*at("br_used", 4, l))
                    w0 = (kb % 2) * D
                    for c in range(KD):
                        b = BR_BANKS[n] + c // 2
                        ins = mm3(PS[:, b, (c % 2) * T:(c % 2 + 1) * T], (s % 2, slice(w0 + c * P, w0 + (c + 1) * P)),
                                  yh[:, kb, :], yl[:, kb, :], k == 0 and c % 2 == 0, k == 2)
                        if c == KD - 1 and (kb % 2 or kb == 8):
                            ins.then_inc(*one("w_used"))
                        elif k == 2 and c % 2:
                            ins.then_inc(*one("br_done"))
                pe.wait_ge(*at("br_used", 8, l))
                for i in range(4):
                    s = MIX_OUT + i
                    pe.wait_ge(*at("mg_lo", i + 1, l))
                    row_slot(s, OUT_BANKS[1], i == 0, i == 3,
                             lambda k: (hh[:, 2 * i + k, :], hl[:, 2 * i + k, :]), l, still)
                norm(l, 2)
                ffn(l, 1)
                norm(l, 3)
            pe.wait_ge(sem("y_ready"), KD)
            for t in range(TT):
                for c in range(KD):
                    o = (c % 4) * P
                    ins = nc.tensor.transpose(PS[:, 2 * t + 4 + c // 4, o:o + P], x[:, c, t * P:(t + 1) * P], ident)
                ins.then_inc(sem("out_tr"), 1)


_INS = ["x", "c", "positions", "ada_w", "ada_b", "norm_g", "ffn1_w_in", "ffn1_w_out", "mix_w_in", "rwkv_mu",
        "rwkv_w0", "rwkv_w2", "rwkv_a0", "rwkv_a2", "rwkv_g2", "rwkv_k_k", "rwkv_k_a", "rwkv_r_k", "rwkv_lnx_g",
        "rwkv_lnx_b", "mla_q_norm_g", "mla_w_uq", "mla_kv_norm_g", "mla_w_ukv", "branch_w", "mix_w_out",
        "ffn2_w_in", "ffn2_w_out", "final_norm_g"]


def build(nc, shapes):
    args = {n: nc.dram_tensor(f"in_{n}", shape, dt, kind="ExternalInput").ap() for n, (shape, dt) in shapes.items()}
    args["out"] = nc.dram_tensor("out_0", (1, T, D), F32, kind="ExternalOutput").ap()
    tally = {}
    hybrid_trunk(nc, args, PER_LAYER, tally)
    return tally


def kernel(**inputs):
    import concourse.bacc as _bacc
    from concourse.bass_utils import run_bass_kernel_spmd as _run

    arrays = {n: np.ascontiguousarray(inputs[n]) for n in _INS}
    arrays["consts"] = shape_constants()
    nc = _bacc.Bacc("TRN2", target_bir_lowering=False, num_devices=1, dynamic_dma_scratch_size=1024)
    build(nc, {n: (v.shape, mybir.dt.from_np(v.dtype)) for n, v in arrays.items()})
    r = _run(nc, [{f"in_{n}": v for n, v in arrays.items()}], core_ids=[0])
    return r.results[0]["out_0"]
```
